# Optimizing a Trainium2 kernel written in Bass

```python
import math
import jax, jax.numpy as jnp
from jax import lax
import numpy as np

D_MODEL = 1024
BATCH = 1
SEQ = 512
DEPTH = 1

CHUNK = 64
Q_BLOCK = 128
HEAD_DIM = 64
ROT_DIM = HEAD_DIM // 4
ROPE_THETA = 500000.0
RMS_EPS = 1e-6
A_HEADS = 4
A_QK_DIM = HEAD_DIM
A_V_DIM = 2 * HEAD_DIM
A_WIDTH = A_HEADS * A_V_DIM
B_HEADS = 8
B_QK_DIM = HEAD_DIM
B_LATENT = 128
B_OUT_DIM = HEAD_DIM
B_WIDTH = B_HEADS * B_OUT_DIM
IDX_HEADS = 8
IDX_DIM = 64
IDX_TOPK_MAX = 256
MIX_WIDTH = A_WIDTH + B_WIDTH
IN_SIZES = (A_HEADS * A_QK_DIM, A_HEADS * A_QK_DIM, A_HEADS * A_QK_DIM, A_HEADS * A_QK_DIM,
            A_HEADS * A_V_DIM,
            B_HEADS * B_QK_DIM, B_QK_DIM, B_LATENT, IDX_HEADS * IDX_DIM, IDX_DIM, IDX_HEADS)
N_IN = sum(IN_SIZES)
N_EXPERTS = 32
TOP_K = 4
D_FF = D_MODEL
SWIGLU_LIMIT = 7.0
SWIGLU_ALPHA = 1.702
EXPERT_BLOCK = 256

kernel_name = "hybrid_diffattn_dsa_moe_block"

def rms_norm(x, g):
    xf = x.astype(jnp.float32)
    y = xf * lax.rsqrt(jnp.mean(xf * xf, axis=-1, keepdims=True) + RMS_EPS)
    return (y * g.astype(jnp.float32)).astype(x.dtype)

def rope_tables(S):
    pos = jnp.arange(S, dtype=jnp.float32)
    inv = ROPE_THETA ** (-jnp.arange(0, ROT_DIM, 2, dtype=jnp.float32) / ROT_DIM)
    ang = pos[:, None] * inv[None, :]
    return jnp.cos(ang), jnp.sin(ang)

def apply_partial_rope(x, cos, sin):
    half = ROT_DIM // 2
    shape = (1, x.shape[1]) + (1,) * (x.ndim - 3) + (half,)
    cs, sn = cos.reshape(shape), sin.reshape(shape)
    xr = x[..., :ROT_DIM].astype(jnp.float32)
    x1, x2 = xr[..., :half], xr[..., half:]
    rot = jnp.concatenate([x1 * cs - x2 * sn, x2 * cs + x1 * sn], axis=-1)
    return jnp.concatenate([rot.astype(x.dtype), x[..., ROT_DIM:]], axis=-1)

def to_blocks(t):
    B, S = t.shape[:2]
    return jnp.moveaxis(t.reshape((B, S // Q_BLOCK, Q_BLOCK) + t.shape[2:]), 1, 0)

def from_blocks(t):
    nb, B, qb = t.shape[:3]
    return jnp.moveaxis(t, 0, 1).reshape((B, nb * qb) + t.shape[3:])

def diff_attention(q1, q2, k1, k2, v, lam_vecs, sub_g, lambda_init):
    B, S = q1.shape[:2]
    lv = lam_vecs.astype(jnp.float32)
    lam = jnp.exp(jnp.sum(lv[0] * lv[1])) - jnp.exp(jnp.sum(lv[2] * lv[3])) + lambda_init
    key_chunk = jnp.arange(S) // CHUNK
    scale = A_QK_DIM ** -0.5

    def block(args):
        q1b, q2b, i = args
        q_chunk = (i * Q_BLOCK + jnp.arange(Q_BLOCK)) // CHUNK
        allowed = key_chunk[None, :] <= q_chunk[:, None]

        def probs(qb, k):
            s = jnp.einsum('bqhd,bshd->bhqs', qb, k).astype(jnp.float32) * scale
            return jax.nn.softmax(jnp.where(allowed, s, -jnp.inf), axis=-1)

        a = probs(q1b, k1) - lam * probs(q2b, k2)
        return jnp.einsum('bhqs,bshe->bqhe', a.astype(v.dtype), v)

    nqb = S // Q_BLOCK
    o = from_blocks(lax.map(block, (to_blocks(q1), to_blocks(q2), jnp.arange(nqb))))
    o = rms_norm(o, sub_g) * (1.0 - lambda_init)
    return o.reshape(B, S, A_WIDTH)

def dsa_attention(q, k, lat, iq, ik, iw, w_uv):
    B, S = q.shape[:2]
    topk = min(IDX_TOPK_MAX, S // 4)
    key_chunk = jnp.arange(S) // CHUNK
    scale = B_QK_DIM ** -0.5
    iw = iw.astype(jnp.float32) * (IDX_HEADS ** -0.5) * (IDX_DIM ** -0.5)
    gather = jax.vmap(lambda arr, idx: arr[idx])

    def block(args):
        qb, iqb, iwb, i = args
        q_chunk = (i * Q_BLOCK + jnp.arange(Q_BLOCK)) // CHUNK
        allowed = key_chunk[None, :] <= q_chunk[:, None]
        rel = jax.nn.relu(jnp.einsum('bqhd,bsd->bqhs', iqb, ik).astype(jnp.float32))
        score = jnp.einsum('bqhs,bqh->bqs', rel, iwb)
        score = jnp.where(allowed[None], score, -jnp.inf)
        _, idx = lax.top_k(score, topk)
        valid = (idx // CHUNK) <= q_chunk[None, :, None]
        flat = idx.reshape(B, Q_BLOCK * topk)
        k_sel = gather(k, flat).reshape(B, Q_BLOCK, topk, B_QK_DIM)
        v_sel = gather(lat, flat).reshape(B, Q_BLOCK, topk, B_LATENT)
        s = jnp.einsum('bqhd,bqkd->bqhk', qb, k_sel).astype(jnp.float32) * scale
        p = jax.nn.softmax(jnp.where(valid[:, :, None, :], s, -jnp.inf), axis=-1)
        return jnp.einsum('bqhk,bqkc->bqhc', p.astype(v_sel.dtype), v_sel)

    nqb = S // Q_BLOCK
    o = from_blocks(lax.map(block, (to_blocks(q), to_blocks(iq), to_blocks(iw), jnp.arange(nqb))))
    o = jnp.einsum('bshc,hcd->bshd', o, w_uv)
    return o.reshape(B, S, B_WIDTH)

def moe(h, router_w, router_b, w_gate, b_gate, w_up, b_up, w_down, b_down):
    B, S, D = h.shape
    T = B * S
    P = T * TOP_K
    G = EXPERT_BLOCK
    hf = h.reshape(T, D)
    logits = (hf @ router_w + router_b).astype(jnp.float32)
    top_vals, top_idx = lax.top_k(logits, TOP_K)
    gates = jax.nn.softmax(top_vals, axis=-1)
    e_flat = top_idx.reshape(P)
    g_flat = gates.reshape(P)
    tok = jnp.arange(P) // TOP_K
    order = jnp.argsort(e_flat, stable=True)
    e_s, tok_s, g_s = e_flat[order], tok[order], g_flat[order]
    counts = jnp.bincount(e_flat, length=N_EXPERTS)
    padded = ((counts + G - 1) // G) * G
    off = jnp.cumsum(counts) - counts
    pcum = jnp.cumsum(padded)
    poff = pcum - padded
    dest = poff[e_s] + (jnp.arange(P) - off[e_s])
    nb = -(-P // G) + N_EXPERTS
    xbuf = jnp.zeros((nb * G, D), hf.dtype).at[dest].set(hf[tok_s])
    block_expert = jnp.minimum(jnp.searchsorted(pcum, jnp.arange(nb) * G, side='right'), N_EXPERTS - 1)

    def expert_block(args):
        xb, e = args
        g = xb @ w_gate[e] + b_gate[e]
        u = xb @ w_up[e] + b_up[e]
        g = jnp.minimum(g, SWIGLU_LIMIT)
        u = jnp.clip(u, -SWIGLU_LIMIT, SWIGLU_LIMIT)
        a = g * jax.nn.sigmoid(SWIGLU_ALPHA * g) * (u + 1.0)
        return a @ w_down[e] + b_down[e]

    ybuf = lax.map(expert_block, (xbuf.reshape(nb, G, D), block_expert)).reshape(nb * G, D)
    contrib = ybuf[dest].astype(jnp.float32) * g_s[:, None]
    y = jax.ops.segment_sum(contrib, tok_s, num_segments=T)
    return y.astype(h.dtype).reshape(B, S, D)

def setup_inputs(seed: int = 0) -> dict:
    key = jax.random.key(seed)
    ks = jax.random.split(key, 24)

    def nrm(k, shape, scale):
        return jax.random.normal(k, shape, jnp.float32) * scale

    D = D_MODEL
    return {
        "x": nrm(ks[0], (BATCH, SEQ, D), 1.0),
        "c": nrm(ks[1], (BATCH, D), 1.0),
        "norm1_g": 1.0 + nrm(ks[2], (DEPTH, D), 0.02),
        "norm2_g": 1.0 + nrm(ks[3], (DEPTH, D), 0.02),
        "w_ada": nrm(ks[4], (DEPTH, D, 6 * D), D ** -0.5),
        "b_ada": nrm(ks[5], (DEPTH, 6 * D), 0.02),
        "w_in": nrm(ks[6], (DEPTH, D, N_IN), D ** -0.5),
        "w_out": nrm(ks[7], (DEPTH, MIX_WIDTH, D), MIX_WIDTH ** -0.5),
        "a_q_norm_g": 1.0 + nrm(ks[8], (DEPTH, A_QK_DIM), 0.02),
        "a_k_norm_g": 1.0 + nrm(ks[9], (DEPTH, A_QK_DIM), 0.02),
        "a_lambda": nrm(ks[10], (DEPTH, 4, A_QK_DIM), 0.1),
        "a_sub_g": 1.0 + nrm(ks[11], (DEPTH, A_V_DIM), 0.02),
        "b_q_norm_g": 1.0 + nrm(ks[12], (DEPTH, B_QK_DIM), 0.02),
        "b_k_norm_g": 1.0 + nrm(ks[13], (DEPTH, B_QK_DIM), 0.02),
        "b_kv_norm_g": 1.0 + nrm(ks[14], (DEPTH, B_LATENT), 0.02),
        "b_w_uv": nrm(ks[15], (DEPTH, B_HEADS, B_LATENT, B_OUT_DIM), B_LATENT ** -0.5),
        "router_w": nrm(ks[16], (DEPTH, D, N_EXPERTS), D ** -0.5),
        "router_b": nrm(ks[17], (DEPTH, N_EXPERTS), 0.01),
        "w_gate": nrm(ks[18], (DEPTH, N_EXPERTS, D, D_FF), D ** -0.5),
        "b_gate": nrm(ks[19], (DEPTH, N_EXPERTS, D_FF), 0.01),
        "w_up": nrm(ks[20], (DEPTH, N_EXPERTS, D, D_FF), D ** -0.5),
        "b_up": nrm(ks[21], (DEPTH, N_EXPERTS, D_FF), 0.01),
        "w_down": nrm(ks[22], (DEPTH, N_EXPERTS, D_FF, D), D_FF ** -0.5),
        "b_down": nrm(ks[23], (DEPTH, N_EXPERTS, D), 0.01),
    }

def reference(x, c, norm1_g, norm2_g, w_ada, b_ada, w_in, w_out, a_q_norm_g, a_k_norm_g,
              a_lambda, a_sub_g, b_q_norm_g, b_k_norm_g, b_kv_norm_g, b_w_uv, router_w, router_b,
              w_gate, b_gate, w_up, b_up, w_down, b_down):
    B, S, D = x.shape
    cos, sin = rope_tables(S)
    split_pts = [int(v) for v in np.cumsum(IN_SIZES)[:-1]]
    for l in range(DEPTH):
        lambda_init = 0.8 - 0.6 * math.exp(-0.3 * l)
        mod = jax.nn.silu(c) @ w_ada[l] + b_ada[l]
        sh1, sc1, g1, sh2, sc2, g2 = jnp.split(mod[:, None, :], 6, axis=-1)

        h = rms_norm(x, norm1_g[l]) * (1.0 + sc1) + sh1
        proj = h @ w_in[l]
        aq1, aq2, ak1, ak2, av, bq, bk, blat, iq, ik, iw = jnp.split(proj, split_pts, axis=-1)

        def a_heads(t, g):
            t = rms_norm(t.reshape(B, S, A_HEADS, A_QK_DIM), g)
            return apply_partial_rope(t, cos, sin)

        a_out = diff_attention(a_heads(aq1, a_q_norm_g[l]), a_heads(aq2, a_q_norm_g[l]),
                               a_heads(ak1, a_k_norm_g[l]), a_heads(ak2, a_k_norm_g[l]),
                               av.reshape(B, S, A_HEADS, A_V_DIM), a_lambda[l], a_sub_g[l],
                               lambda_init)

        bq = apply_partial_rope(rms_norm(bq.reshape(B, S, B_HEADS, B_QK_DIM), b_q_norm_g[l]), cos, sin)
        bk = apply_partial_rope(rms_norm(bk, b_k_norm_g[l]), cos, sin)
        blat = rms_norm(blat, b_kv_norm_g[l])
        iq = apply_partial_rope(iq.reshape(B, S, IDX_HEADS, IDX_DIM), cos, sin)
        ik = apply_partial_rope(ik, cos, sin)
        b_out = dsa_attention(bq, bk, blat, iq, ik, iw, b_w_uv[l])

        mix = jnp.concatenate([a_out, b_out], axis=-1) @ w_out[l]
        x = x + g1 * mix

        h2 = rms_norm(x, norm2_g[l]) * (1.0 + sc2) + sh2
        x = x + g2 * moe(h2, router_w[l], router_b[l], w_gate[l], b_gate[l], w_up[l], b_up[l],
                         w_down[l], b_down[l])
    return x


_drawn_inputs = setup_inputs


def setup_inputs(seed=0):
    import zlib

    import numpy as np

    out = dict(_drawn_inputs(seed))
    spreads = {}
    factors = {'a_q_norm_g': 5.706,
     'a_k_norm_g': 6.586,
     'b_q_norm_g': 8.0,
     'b_k_norm_g': 8.0,
     'b_kv_norm_g': 4.006,
     'router_b': 3.878,
     'b_gate': 28.45,
     'b_up': 35.23,
     'b_down': 31.874,
     'norm2_g': 2.901,
     'a_sub_g': 6.411}
    for name, (base, spread) in spreads.items():
        noise = np.random.default_rng([zlib.crc32(name.encode()), seed]).standard_normal(out[name].shape)
        drawn = base * np.exp(spread * noise) if base else spread * noise
        out[name] = __import__('jax').numpy.asarray(drawn.astype(out[name].dtype))
    for name, factor in factors.items():
        out[name] = (out[name] * factor).astype(out[name].dtype)
    return out
```

```python
import math
from contextlib import ExitStack

import concourse.bass as bass
import numpy as np
from concourse import mybir

F32 = mybir.dt.float32
I32 = mybir.dt.int32
U32 = mybir.dt.uint32
ALU = mybir.AluOpType
ACT = mybir.ActivationFunctionType
AX = mybir.AxisListType.X

P = 128
T = 512
NT = T // P
D = 1024
KT = D // P
HD = 64
NE = 32
TOPK = 4
BS = 64
MAXB = 64
LIMIT = 7.0
ALPHA = 1.702
NEG = -1.0e30
TAKEN = -3.0e38
EPS = 1e-6
LAM0 = 0.8 - 0.6 * math.exp(-0.3 * 0)
NO_ROW = 4096.0
SCALE = HD ** -0.5

C_ID, C_TRI, C_ONE, C_IOTA = 0, 128, 256, 384
C_COS, C_SIN, C_TOK, C_PAIR = 448, 512, 576, 580
C_ALL = 584


def constants():
    c = np.zeros((P, C_ALL), np.float32)
    c[:, C_ID:C_ID + P] = np.eye(P)
    c[:, C_TRI:C_TRI + P] = np.triu(np.ones((P, P)), 1)
    c[:, C_ONE:C_ONE + P] = 1
    c[:, C_IOTA:C_IOTA + 64] = np.arange(64)
    pos = np.arange(T, dtype=np.float32)
    rot = HD // 4
    inv = np.float32(500000.0) ** (-np.arange(0, rot, 2, dtype=np.float32) / np.float32(rot))
    ang = pos[:, None] * inv.astype(np.float32)[None, :]
    for base, f in ((C_COS, np.cos), (C_SIN, np.sin)):
        tab = f(ang).astype(np.float32).reshape(NT, P, rot // 2)
        for t in range(NT):
            c[:, base + 16 * t:base + 16 * t + 16] = np.concatenate([tab[t], tab[t]], axis=1)
    for t in range(NT):
        c[:, C_TOK + t] = t * P + np.arange(P)
        c[:, C_PAIR + t] = TOPK * (t * P + np.arange(P)) - NO_ROW
    return c


def build(nc, consts, x, c, norm1_g, norm2_g, w_ada, b_ada, w_in, w_out, a_q_norm_g, a_k_norm_g, a_lambda,
          a_sub_g, b_q_norm_g, b_k_norm_g, b_kv_norm_g, b_w_uv, router_w, router_b, w_gate, b_gate, w_up,
          b_up, w_down, b_down, out):
    with ExitStack() as ctx:
        sems = {}

        def sem(name):
            if name not in sems:
                sems[name] = ctx.enter_context(nc.semaphore(name))
            return sems[name]

        def sb(name, cols, dt=F32):
            return ctx.enter_context(nc.sbuf_tensor(name, [P, cols], dt))

        xhat_dram = nc.dram_tensor("xhat_scratch", (T, D), F32, kind="Internal").ap()
        x2_dram = nc.dram_tensor("x2_scratch", (T, D), F32, kind="Internal").ap()
        pair_dram = nc.dram_tensor("pair_scratch", (T * TOPK, D), F32, kind="Internal").ap()

        W = sb("W", 5 * 8192)
        X = sb("X", 4096)
        H = sb("H", 4096)
        CT = sb("CT", C_ALL)
        slot = [W[:, i * 8192:(i + 1) * 8192].rearrange("p (k n) -> p k n", k=KT) for i in range(5)]
        GATE, UP, DOWN = (slot[0], slot[3]), (slot[1], slot[4]), slot[2]
        ident = CT[:, C_ID:C_ID + P]
        tri = CT[:, C_TRI:C_TRI + P]
        ones = CT[:, C_ONE:C_ONE + P]
        iota = CT[:, C_IOTA:C_IOTA + 64]

        gains = sb("gains", 4 * HD + 2 * P)
        cols = sb("cols", 72)
        mod = sb("mod", 48)
        silu = sb("silu", 8)
        amp = sb("amp", 16)
        sm = sb("sm", 128)
        iw = sb("iw", NT * 8)
        uv = sb("uv", 8 * HD)
        rw = sb("rw", KT * NE)
        rb = sb("rb", NE)
        route = sb("route", 4 * 128 + 5 * 16 + 3 * 32)
        tab = sb("tab", 3 * MAXB)
        tabi = sb("tabi", 2 * MAXB, U32)
        cum = sb("cum", NE + 1, I32)
        gidx = sb("gidx", 2, U32)
        biasT = sb("biasT", 3 * KT * NE)

        A0 = 3 * 8192
        QKT = W[:, A0:A0 + 18 * 512].rearrange("p (h t) -> p h t", h=18)
        o = A0 + 18 * 512
        V = W[:, o:o + 2048].rearrange("p (t n) -> p t n", t=NT)
        LAT = W[:, o + 2048:o + 2560].rearrange("p (t n) -> p t n", t=NT)
        P1 = W[:, o + 2560:o + 3584].rearrange("p (b n) -> p b n", b=2)
        P2 = W[:, o + 3584:o + 4608].rearrange("p (b n) -> p b n", b=2)
        TMP = W[:, o + 2560:o + 4096].rearrange("p (b n) -> p b n", b=3)
        SQ = W[:, o + 4096:o + 4608]
        AT = W[:, o + 4608:o + 5632].rearrange("p (b n) -> p b n", b=2)
        OT = W[:, o + 5632:o + 5888].rearrange("p (b n) -> p b n", b=2)
        amo = [o + 5888, o + 6016, o + 6272, o + 6656]
        AM = [W[:, amo[i]:amo[i] + (i + 1) * P] for i in range(NT)]
        RT = SQ
        AQ, AK, BQ, IQ, BK, IK = 0, 4, 8, 12, 16, 17

        WIN = W[:, 2 * 8192:3 * 8192].rearrange("p (b k n) -> p b k n", b=2, k=KT)
        hT = H[:, :].rearrange("p (k t) -> p k t", k=KT)
        xt = X[:, :].rearrange("p (t d) -> p t d", t=NT)
        MIX = H[:, :].rearrange("p (t d) -> p t d", t=NT)
        mixT = X[:, :].rearrange("p (k t) -> p k t", k=KT)
        x2 = MIX
        XH2 = slot[3].rearrange("p k n -> p (k n)")[:, 0:4096].rearrange("p (t d) -> p t d", t=NT)
        h2T = slot[3].rearrange("p k n -> p (k n)")[:, 4096:8192].rearrange("p (k t) -> p k t", k=KT)
        s4 = slot[4].rearrange("p k n -> p (k n)")
        G1B = s4[:, 0:1024]
        DIAG = s4[:, 1024:2048].rearrange("p (k n) -> p k n", k=KT)
        BROW = s4[0:NE, 2048:5120].rearrange("p (m n) -> p m n", m=3)
        LH = s4[:, 1024:2048].rearrange("p (j s) -> p j s", j=16)
        RH = s4[:, 5120:8192].rearrange("p (j s) -> p j s", j=16)

        rows = H[0:72, 0:P]
        lamb = H[:, 1024:1280]

        xg = X[0:BS, 0:1024]
        ysb = X[0:BS, 1024:2048]
        xT = X[:, 2048:2560].rearrange("p (k s) -> p k s", k=KT)
        gc = X[:, 2560:3072].rearrange("p (k s) -> p k s", k=KT)
        ex = X[:, 3072:3584].rearrange("p (k s) -> p k s", k=KT)
        uc = X[:, 3584:4096].rearrange("p (k s) -> p k s", k=KT)
        aT = H[:, 0:512].rearrange("p (k s) -> p k s", k=KT)
        yT = H[:, 512:1024].rearrange("p (k s) -> p k s", k=KT)
        bgT, buT, bdT = [biasT[:, m * KT * NE:(m + 1) * KT * NE].rearrange("p (k e) -> p k e", k=KT)
                         for m in range(3)]

        bank = [ctx.enter_context(nc.psum_tensor(f"bank{i}", [P, 512], F32)) for i in range(8)]

        def settle(eng, name):
            eng.sem_inc(sem(name + "_settled"), 1)

        IQc, MISC, BQc, AQc, AKc, AVc = range(6)
        CSRC = {IQc: 2240, BQc: 1536, AQc: 0, AKc: 512, AVc: 1024}
        PAIR0 = {IQc: IQ, BQc: BQ, AQc: AQ, AKc: AK, MISC: BK}
        GAIN = {BQc: 2, AQc: 0, AKc: 1}
        steps = [(ch, t) for ch in range(6) for t in range(NT)]
        NST = len(steps)
        NTR = 5 * NT
        normed = [ch in (MISC, BQc, AQc, AKc) for ch, _ in steps]
        nth_norm = [sum(normed[:n + 1]) for n in range(NST)]

        units_c = [(i, h) for i in range(1, NT) for h in range(8)]
        units_d = [(i, h) for i in range(NT) for h in range(4)]
        units_e = [(i, h) for i in range(NT) for h in range(8)]
        ROUNDS = [(i, r) for i in range(1, NT) for r in range(16)]

        block = ctx.enter_context(nc.Block())

        @block.sync
        def _(sp):
            def ada(j, s):
                sp.dma_start(slot[s], w_ada[:, j * D:(j + 1) * D].rearrange("(k p) n -> p k n", p=P)) \
                    .then_inc(sem(f"ada_loaded{s}"), 16)

            def win(ch):
                buf = WIN[:, ch % 2]
                if ch >= 2:
                    sp.wait_ge(sem("proj_done"), 4 * (ch - 1))
                if ch == MISC:
                    sp.dma_start(buf[:, :, 0:192], w_in[:, 2048:2240].rearrange("(k p) n -> p k n", p=P)) \
                        .then_inc(sem("win_loaded1"), 16)
                    sp.dma_start(buf[:, :, 192:264], w_in[:, 2752:2824].rearrange("(k p) n -> p k n", p=P)) \
                        .then_inc(sem("win_loaded_misc"), 16)
                else:
                    sp.dma_start(buf, w_in[:, CSRC[ch]:CSRC[ch] + 512].rearrange("(k p) n -> p k n", p=P)) \
                        .then_inc(sem(f"win_loaded{ch % 2}"), 16)

            sp.dma_start(CT[:, :], consts).then_inc(sem("const_loaded"), 16)
            for i, (src, n) in enumerate(((c, 8), (norm1_g, 8), (norm2_g, 8), (b_ada, 48))):
                sp.dma_start(H[8 * i:8 * i + n, 0:P], src.rearrange("a (r q) -> (a r) q", q=P)) \
                    .then_inc(sem("rows_loaded"), 16)
            for t in range(NT):
                sp.dma_start(xt[:, t, :], x[t * P:(t + 1) * P, :]).then_inc(sem(f"x_loaded{t}"), 16)
            ada(1, 1)
            ada(0, 0)
            win(0)
            win(1)
            for j, s in ((2, 0), (3, 1), (4, 0), (5, 1)):
                sp.wait_ge(sem("mod_done"), max(2, j - 1))
                ada(j, s)
                win(j)
            sp.wait_ge(sem("proj_done"), NST)
            sp.dma_start(slot[2], w_out.rearrange("(k p) n -> p k n", p=P)).then_inc(sem("wout_loaded"), 16)
            sp.wait_ge(sem("mod_done"), 6)
            e_src = {"gate": w_gate, "up": w_up, "down": w_down}

            def expert(kind, e, dst, s):
                sp.dma_start(dst, e_src[kind][bass.ds(e, 1), :, :].rearrange("e (k p) n -> p (e k) n", p=P)) \
                    .then_inc(sem(f"{kind}_loaded{s}"), 16)

            expert("gate", 0, GATE[0], 0)
            expert("up", 0, UP[0], 0)
            sp.wait_ge(sem("mixT_done"), KT)
            sp.dma_start(x2, x.rearrange("(t p) d -> p t d", p=P)).then_inc(sem("x_again"), 16)
            sp.wait_ge(sem("sparse_out_done"), len(units_e))
            sp.dma_start(BROW[:, 0, :], b_gate).then_inc(sem("brow_loaded"), 16)
            sp.dma_start(BROW[:, 1, :], b_up).then_inc(sem("brow_loaded"), 16)
            sp.dma_start(BROW[:, 2, :], b_down).then_inc(sem("brow_loaded"), 16)
            sp.wait_ge(sem("wout_done"), 2 * NT)
            expert("down", 0, DOWN, 0)
            for t in range(NT):
                sp.wait_ge(sem("x2_ready"), t + 1)
                sp.dma_start(x2_dram[t * P:(t + 1) * P, :], x2[:, t, :]).then_inc(sem("x2_stored"), 16)
                sp.wait_ge(sem("xhat2_ready"), t + 1)
                sp.dma_start(xhat_dram[t * P:(t + 1) * P, :], XH2[:, t, :]).then_inc(sem("xhat_stored"), 16)
            sp.wait_ge(sem("router_done"), 1)
            sp.wait_ge(sem("xhat_stored"), 16 * NT)
            expert("gate", 1, GATE[1], 1)
            sp.wait_ge(sem("tables_done"), 1)
            sp.wait_ge(sem("biasT_done"), 1)
            expert("up", 1, UP[1], 1)
            sp.wait_ge(sem("cum_ready"), 1)

            def blocks_before(e):
                return sp.value_load(cum[0:1, bass.ds(e, 1)], min_val=1, max_val=MAXB - 1)

            sp.wait_ge(sem("down_done"), blocks_before(1))
            expert("down", 1, DOWN, 0)
            with sp.Fori(1, NE // 2) as pr:
                for s in range(2):
                    e = pr * 2 + s
                    last = sp.snap(blocks_before(e - 1))
                    sp.wait_ge(sem("gate_done"), last)
                    expert("gate", e, GATE[s], s)
                    sp.wait_ge(sem("up_done"), last)
                    expert("up", e, UP[s], s)
                    before = sp.snap(blocks_before(e))
                    sp.wait_ge(sem("down_done"), before)
                    expert("down", e, DOWN, 0)
            total = sp.snap(blocks_before(NE))
            sp.wait_ge(sem("down_done"), total)
            settle(sp, "sp")
            sp.wait_ge(sem("scattered"), total * 16)
            for t in range(NT):
                if t >= 2:
                    sp.wait_ge(sem("final_ready"), t - 1)
                dst = W[:, (t % 2) * 8192:(t % 2) * 8192 + 4096].rearrange("p (k d) -> p k d", k=TOPK)
                sp.dma_start(dst, pair_dram[t * P * TOPK:(t + 1) * P * TOPK, :].rearrange(
                    "(p k) d -> p k d", k=TOPK)).then_inc(sem(f"pairs_loaded{t % 2}"), 16)
                sp.dma_start(W[:, (t % 2) * 8192 + 4096:(t % 2) * 8192 + 5120], x2_dram[t * P:(t + 1) * P, :]) \
                    .then_inc(sem(f"pairs_loaded{t % 2}"), 16)
            for t in range(NT):
                sp.wait_ge(sem("final_ready"), t + 1)
                sp.dma_start(out[t * P:(t + 1) * P, :], H[:, 1024 * t:1024 * t + 1024]).then_inc(sem("out_stored"), 16)
            sp.wait_ge(sem("out_stored"), 16 * NT)
            sp.wait_ge(sem("x2_stored"), 16 * NT)

        @block.gpsimd
        def _(pool):
            small = [(gains[:, 0:64], a_q_norm_g), (gains[:, 64:128], a_k_norm_g), (gains[:, 128:192], b_q_norm_g),
                     (gains[:, 192:256], b_k_norm_g), (gains[:, 256:384], b_kv_norm_g),
                     (gains[:, 384:512], a_sub_g), (rb[:, :], router_b)]
            pool.dma_start(lamb, a_lambda.rearrange("a l q -> a (l q)").to_broadcast([P, 256])) \
                .then_inc(sem("small_loaded"), 16)
            for dst, src in small:
                pool.dma_start(dst, src.to_broadcast([P, src.shape[1]])).then_inc(sem("small_loaded"), 16)
            pool.dma_start(uv[:, :].rearrange("p (h n) -> p h n", h=8), b_w_uv.rearrange("h c n -> c h n")) \
                .then_inc(sem("small_loaded"), 16)
            pool.dma_start(rw[:, :].rearrange("p (k e) -> p k e", k=KT),
                           router_w.rearrange("(k p) e -> p k e", p=P)).then_inc(sem("small_loaded"), 16)

            pool.wait_ge(sem("cum_ready"), 1)
            pool.wait_ge(sem("tabi_ready"), 1)
            pool.wait_ge(sem("xhat_stored"), 16 * NT)
            total = pool.value_load(cum[0:1, NE:NE + 1], min_val=NE, max_val=MAXB - 1)

            def gather():
                settle(pool, "pool")
                pool.indirect_dma_start(out=xg, out_offset=None, in_=xhat_dram,
                                        in_offset=bass.IndirectOffsetOnAxis(ap=gidx[0:BS, 0:1], axis=0),
                                        bounds_check=T - 1, oob_is_err=False).then_inc(sem("gathered"), 16)

            pool.sem_inc(sem("ysb_free"), 1)
            pool.tensor_copy(gidx[0:BS, 0:1], tabi[0:BS, 0:1]).then_inc(sem("gidx_ready"), 1)
            pool.wait_ge(sem("gidx_ready"), 1)
            gather()
            with pool.Fori(0, total) as b:
                b1 = pool.snap(b + 1)
                pool.wait_ge(sem("xg_used"), b1)
                pool.wait_ge(sem("gathered"), b1 * 16)
                pool.tensor_copy(gidx[0:BS, 0:1], tabi[0:BS, bass.ds(b1, 1)]).then_inc(sem("gidx_ready"), 1)
                pool.wait_ge(sem("gidx_ready"), b1 + 1)
                gather()
                pool.wait_ge(sem("ysb_ready"), b1)
                pool.tensor_copy(gidx[0:BS, 1:2], tabi[0:BS, bass.ds(b + MAXB, 1)]).then_inc(sem("sidx_ready"), 1)
                pool.wait_ge(sem("sidx_ready"), b1)
                settle(pool, "pool")
                pool.indirect_dma_start(out=pair_dram, out_offset=bass.IndirectOffsetOnAxis(
                    ap=gidx[0:BS, 1:2], axis=0), in_=ysb, in_offset=None,
                    bounds_check=T * TOPK - 1, oob_is_err=False).then_inc(sem("scattered"), 16)
                pool.wait_ge(sem("scattered"), b1 * 16)
                pool.sem_inc(sem("ysb_free"), 1)
            pool.wait_ge(sem("gathered"), total * 16 + 16)

        @block.scalar
        def _(act):
            act.wait_ge(sem("cols_ready"), 1)
            act.activation(silu[:, :], cols[:, 0:8], ACT.Exp, scale=-1.0).then_inc(sem("exp_c"), 1)
            act.wait_ge(sem("lam_dot"), 2)
            act.activation(sm[:, 2:4], sm[:, 0:2], ACT.Exp).then_inc(sem("lam_exp"), 1)

            def rms_tiles(src, n, name, ready):
                for t in range(NT):
                    ready(t)
                    if t:
                        act.wait_ge(sem(f"{name}_ssq"), t)
                    act.activation(W[:, A0 + 8192 + 6144:A0 + 8192 + 7168] if name == "n1" else
                                   s4[:, 5120:6144], src[:, t, :], ACT.Square,
                                   accum_out=sm[:, n + t:n + t + 1]).then_inc(sem(f"{name}_ssq"), 1)

            rms_tiles(xt, 4, "n1", lambda t: act.wait_ge(sem(f"x_loaded{t}"), 16))
            act.wait_ge(sem("n1_ms"), 1)
            act.activation(sm[:, 12:16], sm[:, 8:12], ACT.Sqrt).then_inc(sem("n1_sd"), 1)
            act.wait_ge(sem("amp1_ready"), 1)
            for k in range(0, KT, 2):
                act.wait_ge(sem("xT_done"), k + 1)
                act.activation(hT[:, k, :], bank[k % 4][:, :], ACT.Identity, bias=mod[:, k:k + 1],
                               scale=amp[:, k:k + 1]).then_inc(sem("hT_act"), 1)

            def evac_heads(n):
                ch, t = steps[n]
                act.wait_ge(sem("qt_done"), n + 1)
                m = 2 if ch == MISC else 4
                act.activation(QKT[:, PAIR0[ch]:PAIR0[ch] + m, t * P:(t + 1) * P],
                               bank[4 + n % 2][:, 0:m * P].rearrange("p (m q) -> p m q", m=m),
                               ACT.Copy).then_inc(sem("qt_evac"), 1)

            for n, (ch, t) in enumerate(steps):
                act.wait_ge(sem("proj_done"), n + 1)
                if n >= 3:
                    act.wait_ge(sem("qt_done"), min(n - 2, NTR))
                tmp = TMP[:, n % 3]
                ps = bank[n % 4]
                if ch == AVc:
                    act.activation(V[:, t, :], ps[:, :], ACT.Copy).then_inc(sem("proj_evac"), 1)
                elif ch == MISC:
                    two = [P, 2, HD]
                    act.activation(tmp[:, 0:128].rearrange("p (a q) -> p a q", a=2),
                                   ps[:, 0:64].unsqueeze(1).to_broadcast(two), ACT.Copy)
                    act.activation(tmp[:, 128:256].rearrange("p (a q) -> p a q", a=2),
                                   ps[:, 192:256].unsqueeze(1).to_broadcast(two), ACT.Copy)
                    act.activation(tmp[:, 256:384], ps[:, 64:192], ACT.Copy)
                    act.activation(tmp[:, 384:392], ps[:, 256:264], ACT.Copy).then_inc(sem("proj_evac"), 1)
                else:
                    act.activation(tmp, ps[:, :], ACT.Copy).then_inc(sem("proj_evac"), 1)
                if normed[n]:
                    act.wait_ge(sem("head_ms"), nth_norm[n])
                    act.activation(sm[:, 24:32], sm[:, 16:24], ACT.Sqrt).then_inc(sem("head_sd"), 1)
                if 2 <= n < NTR + 2:
                    evac_heads(n - 2)

            act.wait_ge(sem("qt_done"), NTR)
            for n, (i, h) in enumerate(units_c):
                nk = (i + 1) * P
                act.wait_ge(sem("iqk_done"), n + 1)
                if n >= 2:
                    act.wait_ge(sem("rel_used"), n - 1)
                act.activation(P1[:, n % 2, 0:nk], bank[n % 2][:, 0:nk], ACT.Relu).then_inc(sem("rel_ready"), 1)

            def diff_exp(n):
                i, h = units_d[n]
                nk = (i + 1) * P
                act.wait_ge(sem("diff_max"), n + 1)
                if n == 0:
                    act.wait_ge(sem("rel_used"), len(units_c))
                if n >= 2:
                    act.wait_ge(sem("diff_T"), n - 1)
                for j, Pj in enumerate((P1, P2)):
                    ins = act.activation(Pj[:, n % 2, 0:nk], bank[2 + 2 * (n % 2) + j][:, 0:nk], ACT.Exp,
                                         bias=sm[:, 36 + 2 * (n % 2) + j:37 + 2 * (n % 2) + j], scale=SCALE,
                                         accum_out=sm[:, 40 + 2 * (n % 4) + j:41 + 2 * (n % 4) + j])
                ins.then_inc(sem("diff_exp"), 1)

            def diff_evac(n):
                nk = (units_d[n][0] + 1) * P
                act.wait_ge(sem("diff_T"), n + 1)
                if n >= 2:
                    act.wait_ge(sem("diff_pv"), n - 1)
                act.activation(AT[:, n % 2, 0:nk], bank[6][:, 0:nk], ACT.Copy).then_inc(sem("diff_Te"), 1)

            for n in range(len(units_d) + 1):
                if n < len(units_d):
                    diff_exp(n)
                if n >= 1:
                    diff_evac(n - 1)

            def sparse_exp(n):
                i, h = units_e[n]
                nk = (i + 1) * P
                act.wait_ge(sem("sparse_max"), n + 1)
                if n >= 2:
                    act.wait_ge(sem("sparse_T"), n - 1)
                act.activation(P1[:, n % 2, 0:nk], P2[:, n % 2, 0:nk], ACT.Exp, bias=sm[:, 52 + n % 2:53 + n % 2],
                               scale=SCALE, accum_out=sm[:, 56 + n % 4:57 + n % 4]).then_inc(sem("sparse_exp"), 1)

            def sparse_evac(n):
                act.wait_ge(sem("sparse_oT"), n + 1)
                if n >= 2:
                    act.wait_ge(sem("sparse_out_done"), n - 1)
                act.activation(OT[:, n % 2, :], bank[5 + 2 * (n % 2)][:, 0:P], ACT.Copy) \
                    .then_inc(sem("sparse_oTe"), 1)

            for n in range(len(units_e) + 2):
                if n < len(units_e):
                    sparse_exp(n)
                if n >= 2:
                    sparse_evac(n - 2)

            act.wait_ge(sem("sub_ms"), 1)
            act.activation(sm[:, 80:96], sm[:, 64:80], ACT.Sqrt).then_inc(sem("sub_sd"), 1)
            act.wait_ge(sem("g1b_done"), 1)
            for j in range(2):
                act.activation(G1B[:, j * 512:(j + 1) * 512], bank[4 + j][:, :], ACT.Copy).then_inc(sem("g1b_ready"), 1)
            for k in range(0, KT, 2):
                act.wait_ge(sem("mixT_done"), k + 1)
                act.activation(mixT[:, k, :], bank[k % 4][:, :], ACT.Copy).then_inc(sem("mixT_act"), 1)
            for t in range(NT):
                act.wait_ge(sem("x2_ready"), t + 1)
                act.activation(s4[:, 5120:6144], x2[:, t, :], ACT.Square,
                               accum_out=sm[:, 4 + t:5 + t]).then_inc(sem("n2_ssq"), 1)
                act.wait_ge(sem("n2_ms"), t + 1)
                act.activation(sm[:, 12 + t:13 + t], sm[:, 8 + t:9 + t], ACT.Sqrt).then_inc(sem("n2_sd"), 1)
            for k in range(0, KT, 2):
                act.wait_ge(sem("xT2_done"), k + 1)
                act.activation(h2T[:, k, :], bank[k % 4][:, :], ACT.Identity, bias=mod[:, 24 + k:25 + k],
                               scale=amp[:, 8 + k:9 + k]).then_inc(sem("h2T_act"), 1)
            act.wait_ge(sem("gate_sub"), 1)
            act.activation(route[:, 528:544], route[:, 512:528], ACT.Exp).then_inc(sem("gate_exp"), 1)

            act.wait_ge(sem("cum_ready"), 1)
            act.wait_ge(sem("tabi_ready"), 1)

            def scale_shift():
                for k in range(KT):
                    ins = act.activation(xT[:, k, :], bank[7][:, k * BS:(k + 1) * BS], ACT.Identity,
                                         bias=mod[:, 24 + k:25 + k], scale=amp[:, 8 + k:9 + k])
                ins.then_inc(sem("xTb_ready"), 1)

            act.wait_ge(sem("xg_used"), 1)
            scale_shift()
            total = act.value_load(cum[0:1, NE:NE + 1], min_val=NE, max_val=MAXB - 1)
            with act.Fori(0, total) as b:
                b1 = act.snap(b + 1)
                b2 = act.snap(b + 2)
                for hf in range(2):
                    act.wait_ge(sem(f"gclip{hf}"), b1)
                    hs = slice(4 * hf, 4 * hf + 4)
                    act.activation(ex[:, hs, :], gc[:, hs, :], ACT.Exp, scale=-ALPHA).then_inc(sem(f"gexp{hf}"), 1)
                act.wait_ge(sem("up_done"), b1)
                act.wait_ge(sem("xg_used"), b2)
                scale_shift()
                act.wait_ge(sem("yt_done"), b1)
                act.wait_ge(sem("ysb_free"), b1)
                for j in range(2):
                    ins = act.activation(ysb[:, j * 512:(j + 1) * 512], bank[4 + j][0:BS, :], ACT.Copy,
                                         scale=tab[0:BS, bass.ds(b, 1)])
                ins.then_inc(sem("ysb_ready"), 1)

        @block.tensor
        def _(pe):
            pe.wait_ge(sem("const_loaded"), 16)
            pe.wait_ge(sem("rows_loaded"), 64)
            pe.transpose(bank[7][:, 0:72], rows, ident[0:72, 0:72]).then_inc(sem("rowsT"), 1)
            pe.wait_ge(sem("silu_ready"), 1)

            def mod_part(j):
                s = j % 2
                if j >= 2:
                    pe.wait_ge(sem("mod_read"), j)
                pe.wait_ge(sem(f"ada_loaded{s}"), 16 * (j // 2 + 1))
                for m in range(8):
                    for k in range(KT):
                        ins = pe.matmul(bank[7][:, 128 + 8 * j + m:129 + 8 * j + m], slot[s][:, k, m * P:(m + 1) * P],
                                        silu[:, k:k + 1], start=(k == 0), stop=(k == KT - 1))
                ins.then_inc(sem("mod_done"), 1)

            def tile_transposes(src, done, act_sem, dve_sem, first_wait):
                for k in range(KT):
                    if k >= 4:
                        pe.wait_ge(sem(act_sem if k % 2 == 0 else dve_sem), (k - 4) // 2 + 1)
                    for t in range(NT):
                        if k == 0:
                            first_wait(t)
                        ins = pe.transpose(bank[k % 4][:, t * P:(t + 1) * P], src[:, t, k * P:(k + 1) * P], ident)
                    ins.then_inc(sem(done), 1)

            mod_part(1)
            mod_part(0)
            tile_transposes(xt, "xT_done", "hT_act", "hT_dve", lambda t: pe.wait_ge(sem("xhat_ready"), t + 1))
            pe.wait_ge(sem("hT_act"), 4)
            pe.wait_ge(sem("hT_dve"), 4)

            def heads(n):
                ch, t = steps[n]
                pe.wait_ge(sem("heads_ready"), n + 1)
                if n >= 2:
                    pe.wait_ge(sem("qt_evac"), n - 1)
                for m in range(2 if ch == MISC else 4):
                    ins = pe.transpose(bank[4 + n % 2][:, m * P:(m + 1) * P], TMP[:, n % 3, m * P:(m + 1) * P], ident)
                ins.then_inc(sem("qt_done"), 1)

            for n, (ch, t) in enumerate(steps):
                if t == 0:
                    pe.wait_ge(sem(f"win_loaded{ch % 2}"), 16 * (ch // 2 + 1))
                    if ch == MISC:
                        pe.wait_ge(sem("win_loaded_misc"), 16)
                if n >= 4:
                    pe.wait_ge(sem("proj_evac"), n - 3)
                w = 264 if ch == MISC else 512
                for k in range(KT):
                    ins = pe.matmul(bank[n % 4][:, 0:w], hT[:, k, t * P:(t + 1) * P], WIN[:, ch % 2, k, 0:w],
                                    start=(k == 0), stop=(k == KT - 1))
                ins.then_inc(sem("proj_done"), 1)
                if 2 <= n < NTR + 2:
                    heads(n - 2)
                if t == 3 and 1 <= ch <= 4:
                    mod_part(ch + 1)
            pe.wait_ge(sem("proj_evac"), NST)
            pe.wait_ge(sem("qt_evac"), NTR)

            def half(h):
                return slice(HD * (h % 2), HD * (h % 2) + HD)

            for n, (i, h) in enumerate(units_c):
                if n >= 2:
                    pe.wait_ge(sem("rel_ready"), n - 1)
                pe.matmul(bank[n % 2][:, 0:(i + 1) * P], QKT[half(h), IQ + h // 2, i * P:(i + 1) * P],
                          QKT[half(h), IK, 0:(i + 1) * P], start=True, stop=True).then_inc(sem("iqk_done"), 1)

            for n in range(len(units_d) + 2):
                if n < len(units_d):
                    i, h = units_d[n]
                    if n >= 2:
                        pe.wait_ge(sem("diff_exp"), n - 1)
                    for j in range(2):
                        ins = pe.matmul(bank[2 + 2 * (n % 2) + j][:, 0:(i + 1) * P],
                                        QKT[half(h), AQ + 2 * j + h // 2, i * P:(i + 1) * P],
                                        QKT[half(h), AK + 2 * j + h // 2, 0:(i + 1) * P], start=True, stop=True)
                    ins.then_inc(sem("diff_qk"), 1)
                if 1 <= n <= len(units_d):
                    m = n - 1
                    pe.wait_ge(sem("diff_a"), m + 1)
                    if m >= 1:
                        pe.wait_ge(sem("diff_Te"), m)
                    for kb in range(units_d[m][0] + 1):
                        ins = pe.transpose(bank[6][:, kb * P:(kb + 1) * P], P1[:, m % 2, kb * P:(kb + 1) * P], ident)
                    ins.then_inc(sem("diff_T"), 1)
                if n >= 2:
                    m = n - 2
                    i, h = units_d[m]
                    pe.wait_ge(sem("diff_Te"), m + 1)
                    if m >= 2:
                        pe.wait_ge(sem("diff_out"), m - 1)
                    for kb in range(i + 1):
                        ins = pe.matmul(bank[7 * (m % 2)][:, 0:P], AT[:, m % 2, kb * P:(kb + 1) * P],
                                        V[:, kb, h * P:(h + 1) * P], start=(kb == 0), stop=(kb == i))
                    ins.then_inc(sem("diff_pv"), 1)

            pe.wait_ge(sem("diff_out"), len(units_d))
            pe.wait_ge(sem("small_loaded"), 16 * 10)
            NEU = len(units_e)
            for n in range(NEU + 3):
                if n < NEU:
                    i, h = units_e[n]
                    if n >= 2:
                        pe.wait_ge(sem("sparse_max"), n - 1)
                    pe.matmul(bank[2 + n % 2][:, 0:(i + 1) * P], QKT[half(h), BQ + h // 2, i * P:(i + 1) * P],
                              QKT[half(h), BK, 0:(i + 1) * P], start=True, stop=True).then_inc(sem("sparse_qk"), 1)
                if 1 <= n <= NEU:
                    m = n - 1
                    pe.wait_ge(sem("sparse_exp"), m + 1)
                    if m >= 2:
                        pe.wait_ge(sem("sparse_Te"), m - 1)
                    for kb in range(units_e[m][0] + 1):
                        ins = pe.transpose(bank[6 * (m % 2)][:, kb * P:(kb + 1) * P],
                                           P1[:, m % 2, kb * P:(kb + 1) * P], ident)
                    ins.then_inc(sem("sparse_T"), 1)
                if 2 <= n <= NEU + 1:
                    m = n - 2
                    i = units_e[m][0]
                    pe.wait_ge(sem("sparse_Te"), m + 1)
                    if m >= 2:
                        pe.wait_ge(sem("sparse_oTe"), m - 1)
                    for kb in range(i + 1):
                        ins = pe.matmul(bank[5 + 2 * (m % 2)][:, 0:P], LAT[:, kb, :],
                                        AT[:, m % 2, kb * P:(kb + 1) * P], start=(kb == 0), stop=(kb == i))
                    ins.then_inc(sem("sparse_oT"), 1)
                if n >= 3:
                    m = n - 3
                    pe.wait_ge(sem("sparse_oTe"), m + 1)
                    if m >= 2:
                        pe.wait_ge(sem("sparse_out"), m - 1)
                    pe.matmul(bank[1 + 3 * (m % 2)][:, 0:HD], OT[:, m % 2, :],
                              uv[:, units_e[m][1] * HD:(units_e[m][1] + 1) * HD],
                              start=True, stop=True).then_inc(sem("sparse_out_done"), 1)

            pe.wait_ge(sem("diag_ready"), 1)
            for k in range(KT):
                ins = pe.matmul(bank[4 + k // 4][:, (k % 4) * P:(k % 4 + 1) * P], ones, DIAG[:, k, :],
                                start=True, stop=True)
            ins.then_inc(sem("g1b_done"), 1)
            pe.wait_ge(sem("mix_ready"), 1)
            tile_transposes(MIX, "mixT_done", "mixT_act", "mixT_dve", lambda t: None)
            pe.wait_ge(sem("mixT_act"), 4)
            pe.wait_ge(sem("mixT_dve"), 4)
            pe.wait_ge(sem("wout_loaded"), 16)
            for t in range(NT):
                for hf in range(2):
                    n = 2 * t + hf
                    if n >= 4:
                        pe.wait_ge(sem("mix_added"), n - 3)
                    for k in range(KT):
                        ins = pe.matmul(bank[n % 4][:, :], mixT[:, k, t * P:(t + 1) * P],
                                        slot[2][:, k, hf * 512:(hf + 1) * 512], start=(k == 0), stop=(k == KT - 1))
                    ins.then_inc(sem("wout_done"), 1)
            pe.wait_ge(sem("brow_loaded"), 48)
            for m in range(3):
                for k in range(KT):
                    ins = pe.transpose(bank[5 + m][:, k * NE:(k + 1) * NE], BROW[:, m, k * P:(k + 1) * P],
                                       ident[0:NE, 0:NE])
            ins.then_inc(sem("brow_T"), 1)
            pe.wait_ge(sem("mix_added"), 2 * NT)
            tile_transposes(XH2, "xT2_done", "h2T_act", "h2T_dve", lambda t: pe.wait_ge(sem("xhat2_ready"), t + 1))
            pe.wait_ge(sem("h2T_act"), 4)
            pe.wait_ge(sem("h2T_dve"), 4)
            for t in range(NT):
                for k in range(KT):
                    ins = pe.matmul(bank[4][:, t * NE:(t + 1) * NE], h2T[:, k, t * P:(t + 1) * P],
                                    rw[:, k * NE:(k + 1) * NE], start=(k == 0), stop=(k == KT - 1))
            ins.then_inc(sem("router_done"), 1)
            pe.wait_ge(sem("mask_ready"), 1)
            for t in range(NT):
                for u in range(t + 1):
                    pe.matmul(bank[0][:, t * NE:(t + 1) * NE], tri if u == t else ones,
                              route[:, u * NE:(u + 1) * NE], start=(u == 0), stop=(u == t))
            for u in range(NT):
                ins = pe.matmul(bank[0][:, 128:160], ones, route[:, u * NE:(u + 1) * NE],
                                start=(u == 0), stop=(u == NT - 1))
            ins.then_inc(sem("rank_done"), 1)
            for j in range(16):
                pe.wait_ge(sem("onehot_ready"), j + 1)
                ins = pe.matmul(bank[1][0:BS, 0:3 * MAXB], LH[:, j, :], RH[:, j, :], start=(j == 0), stop=(j == 15))
            ins.then_inc(sem("tables_done"), 1)

            def rows_in():
                settle(pe, "pe")
                for k in range(KT):
                    ins = pe.transpose(bank[7][:, k * BS:(k + 1) * BS], xg[:, k * P:(k + 1) * P], ident[0:BS, 0:BS])
                ins.then_inc(sem("xg_used"), 1)

            pe.wait_ge(sem("cum_ready"), 1)
            pe.wait_ge(sem("tabi_ready"), 1)
            pe.wait_ge(sem("gathered"), 16)
            rows_in()

            with pe.Fori(0, NE // 2) as pr:
                for s in range(2):
                    e = pr * 2 + s
                    first = pe.value_load(cum[0:1, bass.ds(e, 1)], min_val=0, max_val=MAXB - 1)
                    end = pe.value_load(cum[0:1, bass.ds(e + 1, 1)], min_val=1, max_val=MAXB - 1)
                    loads = pe.snap((pr + 1) * 16)
                    pe.wait_ge(sem(f"gate_loaded{s}"), loads)
                    pe.wait_ge(sem(f"up_loaded{s}"), loads)
                    pe.wait_ge(sem("down_loaded0"), (e + 1) * 16)
                    settle(pe, "pe")
                    with pe.Fori(first, end) as b:
                        b1 = pe.snap(b + 1)
                        pe.wait_ge(sem("xTb_ready"), b1)
                        for hf in range(2):
                            for nm, wt, bk in (("gate", GATE[s], 0), ("up", UP[s], 2)):
                                for m in range(4 * hf, 4 * hf + 4):
                                    for k in range(KT):
                                        ins = pe.matmul(bank[bk + hf][:, (m % 4) * BS:(m % 4 + 1) * BS],
                                                        wt[:, k, m * P:(m + 1) * P], xT[:, k, :],
                                                        start=(k == 0), stop=(k == KT - 1))
                                if hf == 0:
                                    ins.then_inc(sem(f"{nm}_half"), 1)
                                else:
                                    ins.then_inc(sem(f"{nm}_done"), 1)
                        pe.wait_ge(sem("gathered"), b1 * 16 + 16)
                        rows_in()
                        for hf in range(2):
                            pe.wait_ge(sem(f"aT_ready{hf}"), b1)
                            for m in range(KT):
                                for k in range(4 * hf, 4 * hf + 4):
                                    ins = pe.matmul(bank[6][:, m * BS:(m + 1) * BS], DOWN[:, k, m * P:(m + 1) * P],
                                                    aT[:, k, :], start=(m == 0 and k == 0),
                                                    stop=(m == KT - 1 and k == KT - 1), skip_group_check=True)
                        ins.then_inc(sem("down_done"), 1)
                        pe.wait_ge(sem("yT_ready"), b1)
                        settle(pe, "pe")
                        for m in range(KT):
                            ins = pe.transpose(bank[4 + m // 4][0:BS, (m % 4) * P:(m % 4 + 1) * P], yT[:, m, :], ident)
                        ins.then_inc(sem("yt_done"), 1)

        @block.vector
        def _(dve):
            chain = [0]

            def link(ins):
                chain[0] += 1
                ins.then_inc(sem("dve_step"), 1)
                dve.wait_ge(sem("dve_step"), chain[0])

            def own(ins, name, n):
                ins.then_inc(sem(name), 1)
                dve.wait_ge(sem(name), n)

            tt, ts, stt = dve.tensor_tensor, dve.tensor_scalar, dve.scalar_tensor_tensor

            dve.wait_ge(sem("rowsT"), 1)
            dve.tensor_copy(cols[:, :], bank[7][:, 0:72]).then_inc(sem("cols_ready"), 1)
            dve.wait_ge(sem("cols_ready"), 1)
            dve.wait_ge(sem("exp_c"), 1)
            link(ts(silu[:, :], silu[:, :], 1.0, None, ALU.add))
            link(dve.reciprocal(silu[:, :], silu[:, :]))
            tt(silu[:, :], silu[:, :], cols[:, 0:8], ALU.mult).then_inc(sem("silu_ready"), 1)
            dve.wait_ge(sem("small_loaded"), 16 * 10)
            for j in range(2):
                dve.tensor_tensor_reduce(lamb[:, 128 * j:128 * j + 64], lamb[:, 128 * j:128 * j + 64],
                                         lamb[:, 128 * j + 64:128 * j + 128], 1.0, 0.0, ALU.mult, ALU.add,
                                         sm[:, j:j + 1]).then_inc(sem("lam_dot"), 1)
            dve.wait_ge(sem("lam_exp"), 1)
            link(tt(sm[:, 34:35], sm[:, 3:4], sm[:, 2:3], ALU.subtract))
            link(ts(sm[:, 34:35], sm[:, 34:35], -LAM0, None, ALU.add))
            link(ts(gains[:, 384:512], gains[:, 384:512], 1.0 - LAM0, None, ALU.mult))
            dve.wait_ge(sem("n1_ssq"), NT)
            ts(sm[:, 8:12], sm[:, 4:8], 1.0 / D, EPS, ALU.mult, ALU.add).then_inc(sem("n1_ms"), 1)
            dve.wait_ge(sem("n1_sd"), 1)
            link(dve.reciprocal(sm[:, 12:16], sm[:, 12:16]))
            for t in range(NT):
                ts(xt[:, t, :], xt[:, t, :], sm[:, 12 + t:13 + t], None, ALU.mult).then_inc(sem("xhat_ready"), 1)

            def mod_evac(j):
                dve.wait_ge(sem("mod_done"), j + 1)
                own(tt(mod[:, 8 * j:8 * j + 8], bank[7][:, 128 + 8 * j:136 + 8 * j], cols[:, 24 + 8 * j:32 + 8 * j],
                       ALU.add), "mod_read", j + 1)

            dve.wait_ge(sem("mod_done"), 2)
            mod_evac(0)
            mod_evac(1)
            stt(amp[:, 0:8], mod[:, 8:16], 1.0, cols[:, 8:16], ALU.add, ALU.mult).then_inc(sem("amp1_ready"), 1)
            dve.wait_ge(sem("amp1_ready"), 1)
            for k in range(1, KT, 2):
                dve.wait_ge(sem("xT_done"), k + 1)
                ts(hT[:, k, :], bank[k % 4][:, :], amp[:, k:k + 1], mod[:, k:k + 1], ALU.mult, ALU.add) \
                    .then_inc(sem("hT_dve"), 1)

            def rope(tmp, t, nh, n):
                heads = tmp.rearrange("p (h q) -> p h q", q=HD)
                xr = heads[:, :, 0:16]
                cs = CT[:, C_COS + 16 * t:C_COS + 16 * t + 16].unsqueeze(1).to_broadcast([P, nh, 16])
                sn = CT[:, C_SIN + 16 * t:C_SIN + 16 * t + 16].unsqueeze(1).to_broadcast([P, nh, 16])
                ta = RT[:, 0:128].rearrange("p (h q) -> p h q", q=16)[:, 0:nh, :]
                tb = RT[:, 128:256].rearrange("p (h q) -> p h q", q=16)[:, 0:nh, :]
                tt(ta, xr, cs, ALU.mult)
                link(tt(tb, xr, sn, ALU.mult))
                tt(heads[:, :, 0:8], ta[:, :, 0:8], tb[:, :, 8:16], ALU.subtract)
                own(tt(heads[:, :, 8:16], ta[:, :, 8:16], tb[:, :, 0:8], ALU.add), "heads_ready", n + 1)


            dve.wait_ge(sem("const_loaded"), 16)
            for n, (ch, t) in enumerate(steps[:NTR]):
                dve.wait_ge(sem("proj_evac"), n + 1)
                tmp = TMP[:, n % 3]
                if ch == IQc:
                    rope(tmp, t, 8, n)
                    continue
                nh = 2 if ch == MISC else 8
                hv = tmp[:, 0:nh * HD].rearrange("p (h q) -> p h q", q=HD)
                sq = SQ[:, 0:nh * HD].rearrange("p (h q) -> p h q", q=HD)
                link(tt(sq, hv, hv, ALU.mult))
                if ch == MISC:
                    link(tt(SQ[:, 128:256], tmp[:, 256:384], tmp[:, 256:384], ALU.mult))
                    link(dve.memset(sm[:, 16:24], 64.0))
                    link(dve.tensor_reduce(sm[:, 16:18], sq, AX, ALU.add))
                    link(dve.tensor_reduce(sm[:, 18:19], SQ[:, 128:256], AX, ALU.add))
                    link(ts(sm[:, 18:19], sm[:, 18:19], 0.5, None, ALU.mult))
                    link(ts(iw[:, 8 * t:8 * t + 8], tmp[:, 384:392], 8 ** -0.5, 64 ** -0.5, ALU.mult, ALU.mult))
                else:
                    link(dve.tensor_reduce(sm[:, 16:24], sq, AX, ALU.add))
                ts(sm[:, 16:24], sm[:, 16:24], 1.0 / HD, EPS, ALU.mult, ALU.add).then_inc(sem("head_ms"), 1)
                dve.wait_ge(sem("head_sd"), nth_norm[n])
                link(dve.reciprocal(sm[:, 24:32], sm[:, 24:32]))
                link(tt(hv, hv, sm[:, 24:24 + nh].unsqueeze(2).to_broadcast([P, nh, HD]), ALU.mult))
                g = 3 if ch == MISC else GAIN[ch]
                link(tt(hv, hv, gains[:, HD * g:HD * g + HD].unsqueeze(1).to_broadcast([P, nh, HD]), ALU.mult))
                if ch == MISC:
                    link(stt(LAT[:, t, :], tmp[:, 256:384], sm[:, 26:27], gains[:, 256:384], ALU.mult, ALU.mult))
                rope(tmp[:, 0:256] if ch == MISC else tmp, t, 4 if ch == MISC else 8, n)
                if t == 3:
                    mod_evac(ch + 1)
            stt(amp[:, 8:16], mod[:, 32:40], 1.0, cols[:, 16:24], ALU.add, ALU.mult).then_inc(sem("amp2_ready"), 1)
            link(dve.memset(AM[0], 0.0))
            link(dve.memset(AM[0][0:64, 64:128], NEG))
            for n, (i, h) in enumerate(units_c):
                nk = (i + 1) * P
                dve.wait_ge(sem("rel_ready"), n + 1)
                w = iw[:, 8 * i + h:8 * i + h + 1]
                if h == 0:
                    ins = ts(AM[i], P1[:, n % 2, 0:nk], w, None, ALU.mult)
                else:
                    ins = stt(AM[i], P1[:, n % 2, 0:nk], w, AM[i], ALU.mult, ALU.add)
                ins.then_inc(sem("rel_used"), 1)
                dve.wait_ge(sem("rel_used"), n + 1)
                if h == 7:
                    link(dve.memset(AM[i][0:64, nk - 64:nk], NEG))

            def topk_round(i, r):
                link(dve.max(sm[:, 96:104], AM[i]))
                link(dve.match_replace(AM[i], sm[:, 96:104], AM[i], TAKEN))
                if r == 15:
                    link(ts(AM[i], AM[i], TAKEN, NEG, ALU.not_equal, ALU.mult))

            ND = len(units_d)
            rounds = list(ROUNDS)
            for n in range(ND + 2):
                if n < ND:
                    i, h = units_d[n]
                    nk = (i + 1) * P
                    dve.wait_ge(sem("diff_qk"), n + 1)
                    for j in range(2):
                        ps = bank[2 + 2 * (n % 2) + j]
                        link(dve.memset(ps[0:64, nk - 64:nk], NEG))
                        link(dve.tensor_reduce(sm[:, 32 + j:33 + j], ps[:, 0:nk], AX, ALU.max))
                    own(ts(sm[:, 36 + 2 * (n % 2):38 + 2 * (n % 2)], sm[:, 32:34], -SCALE, None, ALU.mult),
                        "diff_max", n + 1)
                if 1 <= n <= ND:
                    m = n - 1
                    nk = (units_d[m][0] + 1) * P
                    s0 = 40 + 2 * (m % 4)
                    dve.wait_ge(sem("diff_exp"), m + 1)
                    link(stt(sm[:, 35:36], sm[:, s0:s0 + 1], sm[:, 34:35], sm[:, s0:s0 + 1], ALU.mult, ALU.bypass))
                    link(dve.reciprocal(sm[:, s0:s0 + 2], sm[:, s0:s0 + 2]))
                    link(tt(sm[:, 35:36], sm[:, 35:36], sm[:, s0 + 1:s0 + 2], ALU.mult))
                    own(stt(P1[:, m % 2, 0:nk], P2[:, m % 2, 0:nk], sm[:, 35:36], P1[:, m % 2, 0:nk], ALU.mult,
                            ALU.add), "diff_a", m + 1)
                if n >= 2:
                    m = n - 2
                    i, h = units_d[m]
                    dve.wait_ge(sem("diff_pv"), m + 1)
                    s0 = 40 + 2 * (m % 4)
                    own(ts(MIX[:, i, h * P:(h + 1) * P], bank[7 * (m % 2)][:, 0:P], sm[:, s0:s0 + 1],
                           None, ALU.mult), "diff_out", m + 1)
                for _ in range(3):
                    if rounds:
                        topk_round(*rounds.pop(0))
            assert not rounds

            NEU = len(units_e)
            for n in range(NEU + 3):
                if n < NEU:
                    i, h = units_e[n]
                    nk = (i + 1) * P
                    dve.wait_ge(sem("sparse_qk"), n + 1)
                    if n >= 2:
                        dve.wait_ge(sem("sparse_exp"), n - 1)
                    if n == 0:
                        dve.wait_ge(sem("diff_a"), ND)
                    link(dve.tensor_tensor_reduce(P2[:, n % 2, 0:nk], bank[2 + n % 2][:, 0:nk], AM[i], 1.0,
                                                  2 * NEG, ALU.add, ALU.max, sm[:, 54:55]))
                    own(ts(sm[:, 52 + n % 2:53 + n % 2], sm[:, 54:55], -SCALE, None, ALU.mult), "sparse_max", n + 1)
                if 1 <= n <= NEU:
                    m = n - 1
                    nk = (units_e[m][0] + 1) * P
                    dve.wait_ge(sem("sparse_T"), m + 1)
                    if m >= 2:
                        dve.wait_ge(sem("sparse_oT"), m - 1)
                    own(dve.tensor_copy(AT[:, m % 2, 0:nk], bank[6 * (m % 2)][:, 0:nk]), "sparse_Te", m + 1)
                if n >= 3:
                    m = n - 3
                    i, h = units_e[m]
                    link(dve.reciprocal(sm[:, 60 + m % 4:61 + m % 4], sm[:, 56 + m % 4:57 + m % 4]))
                    dve.wait_ge(sem("sparse_out_done"), m + 1)
                    own(ts(MIX[:, i, 512 + h * HD:512 + (h + 1) * HD], bank[1 + 3 * (m % 2)][:, 0:HD],
                           sm[:, 60 + m % 4:61 + m % 4], None, ALU.mult), "sparse_out", m + 1)

            for k in range(KT):
                ins = ts(DIAG[:, k, :], ident, mod[:, 16 + k:17 + k], None, ALU.mult)
            ins.then_inc(sem("diag_ready"), 1)
            dve.wait_ge(sem("diff_out"), ND)
            for n, (i, h) in enumerate(units_d):
                a = MIX[:, i, h * P:(h + 1) * P]
                link(dve.tensor_tensor_reduce(P1[:, 0, 0:P], a, a, 1.0, 0.0, ALU.mult, ALU.add, sm[:, 64 + n:65 + n]))
            ts(sm[:, 64:80], sm[:, 64:80], 1.0 / P, EPS, ALU.mult, ALU.add).then_inc(sem("sub_ms"), 1)
            dve.wait_ge(sem("sub_sd"), 1)
            link(dve.reciprocal(sm[:, 80:96], sm[:, 80:96]))
            for n, (i, h) in enumerate(units_d):
                a = MIX[:, i, h * P:(h + 1) * P]
                ins = stt(a, a, sm[:, 80 + n:81 + n], gains[:, 384:512], ALU.mult, ALU.mult)
            own(ins, "mix_ready", 1)
            for k in range(1, KT, 2):
                dve.wait_ge(sem("mixT_done"), k + 1)
                dve.tensor_copy(mixT[:, k, :], bank[k % 4][:, :]).then_inc(sem("mixT_dve"), 1)
            dve.wait_ge(sem("x_again"), 16)
            dve.wait_ge(sem("g1b_ready"), 2)
            for t in range(NT):
                for hf in range(2):
                    n = 2 * t + hf
                    cs = slice(hf * 512, hf * 512 + 512)
                    dve.wait_ge(sem("wout_done"), n + 1)
                    tt(s4[:, 6144 + hf * 512:6656 + hf * 512], bank[n % 4][:, :], G1B[:, cs], ALU.mult) \
                        .then_inc(sem("mix_added"), 1)
                    dve.wait_ge(sem("mix_added"), n + 1)
                    ins = tt(x2[:, t, cs], x2[:, t, cs], s4[:, 6144 + hf * 512:6656 + hf * 512], ALU.add)
                own(ins, "x2_ready", t + 1)
                dve.wait_ge(sem("n2_ssq"), t + 1)
                ts(sm[:, 8 + t:9 + t], sm[:, 4 + t:5 + t], 1.0 / D, EPS, ALU.mult, ALU.add).then_inc(sem("n2_ms"), 1)
                dve.wait_ge(sem("n2_sd"), t + 1)
                link(dve.reciprocal(sm[:, 12 + t:13 + t], sm[:, 12 + t:13 + t]))
                ts(XH2[:, t, :], x2[:, t, :], sm[:, 12 + t:13 + t], None, ALU.mult).then_inc(sem("xhat2_ready"), 1)
            for k in range(1, KT, 2):
                dve.wait_ge(sem("xT2_done"), k + 1)
                ts(h2T[:, k, :], bank[k % 4][:, :], amp[:, 8 + k:9 + k], mod[:, 24 + k:25 + k], ALU.mult, ALU.add) \
                    .then_inc(sem("h2T_dve"), 1)
            dve.wait_ge(sem("brow_T"), 1)
            for m in range(2):
                dve.tensor_copy(biasT[:, m * 256:(m + 1) * 256], bank[5 + m][:, 0:256])
            tt(bdT, bank[7][:, 0:256].rearrange("p (k e) -> p k e", k=KT),
               mod[:, 40:48].unsqueeze(2).to_broadcast([P, KT, NE]), ALU.mult).then_inc(sem("biasT_done"), 1)

            lg = X[:, 0:128]
            top = X[:, 128:160]
            topi = X[:, 160:192].bitcast(U32)
            topf = X[:, 192:224]
            OH = [X[:, 256 + 128 * k:384 + 128 * k] for k in range(TOPK)]
            fl = X[:, 768:896]
            sl = X[:, 896:1024]
            rk = X[:, 1024:1152]
            pr_ = X[:, 1152:1280]
            sel = X[:, 1280:1312]
            nb = X[:, 1312:1344]
            cumf = X[:, 1344:1377]
            one32 = ones[:, 0:NE]
            mask = route[:, 0:128]
            gs = route[:, 512:528]
            ge = route[:, 528:544]
            gsum = route[:, 544:548]
            t3 = lambda a: a.rearrange("p (t e) -> p t e", t=NT)
            dve.wait_ge(sem("router_done"), 1)
            link(tt(t3(lg), t3(bank[4][:, 0:128]), rb[:, :].unsqueeze(1).to_broadcast([P, NT, NE]), ALU.add))
            for t in range(NT):
                link(dve.max(top[:, 8 * t:8 * t + 8], lg[:, NE * t:NE * t + NE]))
                link(dve.max_index(topi[:, 8 * t:8 * t + 8], top[:, 8 * t:8 * t + 8], lg[:, NE * t:NE * t + NE]))
            link(dve.tensor_copy(topf, topi))
            top3, topf3 = t3(top), t3(topf)
            for k in range(TOPK):
                link(tt(t3(OH[k]), iota[:, 0:NE].unsqueeze(1).to_broadcast([P, NT, NE]),
                        topf3[:, :, k:k + 1].to_broadcast([P, NT, NE]), ALU.is_equal))
            link(tt(mask, OH[0], OH[1], ALU.add))
            link(tt(mask, mask, OH[2], ALU.add))
            tt(mask, mask, OH[3], ALU.add).then_inc(sem("mask_ready"), 1)
            tt(t3(gs), top3[:, :, 0:TOPK], top3[:, :, 0:1].to_broadcast([P, NT, TOPK]), ALU.subtract) \
                .then_inc(sem("gate_sub"), 1)
            dve.wait_ge(sem("gate_exp"), 1)
            link(dve.tensor_reduce(gsum, t3(ge), AX, ALU.add))
            link(dve.reciprocal(gsum, gsum))
            link(tt(t3(ge), t3(ge), gsum.unsqueeze(2).to_broadcast([P, NT, TOPK]), ALU.mult))
            dve.wait_ge(sem("rank_done"), 1)
            link(dve.tensor_copy(rk, bank[0][:, 0:128]))
            link(ts(nb, bank[0][:, 128:160], float(BS), 1.0, ALU.is_gt, ALU.add))
            for j in range(2, T // BS):
                link(stt(nb, bank[0][:, 128:160], float(BS * j), nb, ALU.is_gt, ALU.add))
            link(dve.memset(cumf[:, 0:1], 0.0))
            link(dve.tensor_tensor_scan(cumf[:, 1:33], one32, nb, 0.0, ALU.mult, ALU.add))
            dve.tensor_copy(cum[:, :], cumf).then_inc(sem("cum_ready"), 1)
            link(ts(fl, rk, float(BS), None, ALU.is_ge))
            for j in range(2, T // BS):
                link(stt(fl, rk, float(BS * j), fl, ALU.is_ge, ALU.add))
            link(stt(sl, fl, -float(BS), rk, ALU.mult, ALU.add))
            link(tt(t3(fl), t3(fl), cumf[:, 0:NE].unsqueeze(1).to_broadcast([P, NT, NE]), ALU.add))
            for k in range(TOPK):
                for q, src in enumerate((fl, sl)):
                    link(tt(pr_, OH[k], src, ALU.mult))
                    link(dve.tensor_reduce(sel[:, 16 * q:16 * q + 16].rearrange("p (t k) -> p t k", k=TOPK)[:, :, k],
                                           t3(pr_), AX, ALU.add))
            for j in range(16):
                t, k = j // TOPK, j % TOPK
                blk = sel[:, j:j + 1]
                ts(LH[:, j, :], iota, sel[:, 16 + j:17 + j], None, ALU.is_equal)
                ts(RH[:, j, 0:64], iota, blk, ge[:, j:j + 1], ALU.is_equal, ALU.mult)
                ts(RH[:, j, 64:128], iota, blk, CT[:, C_TOK + t:C_TOK + t + 1], ALU.is_equal, ALU.mult)
                link(ts(RH[:, j, 128:192], iota, blk, None, ALU.is_equal))
                link(ts(pr_[:, 0:1], CT[:, C_PAIR + t:C_PAIR + t + 1], float(k), None,
                        ALU.add))
                own(ts(RH[:, j, 128:192], RH[:, j, 128:192], pr_[:, 0:1], None, ALU.mult), "onehot_ready", j + 1)
            dve.wait_ge(sem("tables_done"), 1)
            dve.tensor_copy(tab[0:BS, 0:64], bank[1][0:BS, 0:64])
            dve.tensor_copy(tabi[0:BS, 0:64], bank[1][0:BS, 64:128])
            ts(tabi[0:BS, 64:128], bank[1][0:BS, 128:192], NO_ROW, None, ALU.add).then_inc(sem("tabi_ready"), 1)

            dve.wait_ge(sem("cum_ready"), 1)

            def half_act(hf, e, b1):
                hs = slice(4 * hf, 4 * hf + 4)
                q = [P, 4, BS]
                gp = bank[hf][:, 0:256].rearrange("p (m s) -> p m s", m=4)
                up = bank[2 + hf][:, 0:256].rearrange("p (m s) -> p m s", m=4)

                def after(ins, name):
                    ins.then_inc(sem(f"{name}{hf}"), 1)
                    dve.wait_ge(sem(f"{name}{hf}"), b1)

                dve.wait_ge(sem("gate_half" if hf == 0 else "gate_done"), b1)
                after(tt(gc[:, hs, :], gp, bgT[:, hs, bass.ds(e, 1)].to_broadcast(q), ALU.add), "gbias")
                after(ts(gc[:, hs, :], gc[:, hs, :], LIMIT, None, ALU.min), "gclip")
                dve.wait_ge(sem("up_half" if hf == 0 else "up_done"), b1)
                after(tt(uc[:, hs, :], up, buT[:, hs, bass.ds(e, 1)].to_broadcast(q), ALU.add), "ubias")
                after(ts(uc[:, hs, :], uc[:, hs, :], -LIMIT, LIMIT, ALU.max, ALU.min), "uclip")
                after(stt(uc[:, hs, :], uc[:, hs, :], 1.0, gc[:, hs, :], ALU.add, ALU.mult), "ug")
                dve.wait_ge(sem(f"gexp{hf}"), b1)
                after(ts(ex[:, hs, :], ex[:, hs, :], 1.0, None, ALU.add), "onep")
                after(dve.reciprocal(ex[:, hs, :], ex[:, hs, :]), "sigm")
                tt(aT[:, hs, :], uc[:, hs, :], ex[:, hs, :], ALU.mult).then_inc(sem(f"aT_ready{hf}"), 1)

            with dve.Fori(0, NE) as e:
                first = dve.value_load(cum[0:1, bass.ds(e, 1)], min_val=0, max_val=MAXB - 1)
                end = dve.value_load(cum[0:1, bass.ds(e + 1, 1)], min_val=1, max_val=MAXB - 1)
                with dve.Fori(first, end) as b:
                    b1 = dve.snap(b + 1)
                    half_act(0, e, b1)
                    half_act(1, e, b1)
                    dve.wait_ge(sem("down_done"), b1)
                    tt(yT, bank[6][:, :].rearrange("p (k s) -> p k s", k=KT),
                       mod[:, 40:48].unsqueeze(2).to_broadcast([P, KT, BS]), ALU.mult).then_inc(sem("ymul"), 1)
                    dve.wait_ge(sem("ymul"), b1)
                    tt(yT, yT, bdT[:, :, bass.ds(e, 1)].to_broadcast([P, KT, BS]), ALU.add).then_inc(sem("yT_ready"), 1)
            for t in range(NT):
                base = (t % 2) * 8192
                dve.wait_ge(sem(f"pairs_loaded{t % 2}"), 32 * (t // 2 + 1))
                y = [W[:, base + 1024 * k:base + 1024 * (k + 1)] for k in range(5)]
                link(tt(y[0], y[0], y[1], ALU.add))
                link(tt(y[2], y[2], y[3], ALU.add))
                link(tt(y[0], y[0], y[2], ALU.add))
                if t == 0:
                    dve.wait_ge(sem("x2_stored"), 16 * NT)
                    dve.wait_ge(sem("yt_done"), 32)
                tt(H[:, 1024 * t:1024 * t + 1024], y[0], y[4], ALU.add).then_inc(sem("final_ready"), 1)


_ARGS = ["x", "c", "norm1_g", "norm2_g", "w_ada", "b_ada", "w_in", "w_out", "a_q_norm_g", "a_k_norm_g", "a_lambda",
         "a_sub_g", "b_q_norm_g", "b_k_norm_g", "b_kv_norm_g", "b_w_uv", "router_w", "router_b", "w_gate", "b_gate",
         "w_up", "b_up", "w_down", "b_down"]
_SQUEEZE = {"x", "w_ada", "w_in", "w_out", "b_w_uv", "router_w", "w_gate", "b_gate", "w_up", "b_up", "w_down",
            "b_down"}


def kernel(**inputs):
    import concourse.bacc as bacc
    from concourse.bass_utils import run_bass_kernel_spmd

    nc = bacc.Bacc("TRN2", target_bir_lowering=False, num_devices=1)
    arrays, args = {}, []
    for name in ["consts"] + _ARGS:
        a = constants() if name == "consts" else np.ascontiguousarray(inputs[name])
        if name in _SQUEEZE:
            a = a.reshape(a.shape[1:])
        arrays[name] = a
        args.append(nc.dram_tensor(name, a.shape, mybir.dt.from_np(a.dtype), kind="ExternalInput").ap())
    out = nc.dram_tensor("out", (T, D), F32, kind="ExternalOutput").ap()
    build(nc, *args, out)
    r = run_bass_kernel_spmd(nc, [arrays], core_ids=[0])
    return np.asarray(r.results[0]["out"]).reshape(1, T, D)
```

```python
import math
from contextlib import ExitStack

import concourse.bass as bass
import numpy as np
from concourse import mybir

F32 = mybir.dt.float32
I32 = mybir.dt.int32
U32 = mybir.dt.uint32
ALU = mybir.AluOpType
ACT = mybir.ActivationFunctionType
AX = mybir.AxisListType.X

P = 128
T = 512
NT = T // P
D = 1024
KT = D // P
HD = 64
NE = 32
TOPK = 4
BS = 64
WQ = 4
MAXB = 64
LIMIT = 7.0
ALPHA = 1.702
NEG = -1.0e30
TAKEN = -3.0e38
EPS = 1e-6
LAM0 = 0.8 - 0.6 * math.exp(-0.3 * 0)
SCALE = HD ** -0.5

C_ID, C_TRI, C_ONE, C_IOTA = 0, 128, 256, 384
C_COS, C_SIN, C_TOK, C_HALF = 512, 576, 640, 644
C_ALL = 646


def constants():
    c = np.zeros((P, C_ALL), np.float32)
    c[:, C_ID:C_ID + P] = np.eye(P)
    c[:, C_TRI:C_TRI + P] = np.triu(np.ones((P, P)), 1)
    c[:, C_ONE:C_ONE + P] = 1
    c[:, C_IOTA:C_IOTA + P] = np.arange(P) % BS
    pos = np.arange(T, dtype=np.float32)
    rot = HD // 4
    inv = np.float32(500000.0) ** (-np.arange(0, rot, 2, dtype=np.float32) / np.float32(rot))
    ang = pos[:, None] * inv.astype(np.float32)[None, :]
    for base, f in ((C_COS, np.cos), (C_SIN, np.sin)):
        tab = f(ang).astype(np.float32).reshape(NT, P, rot // 2)
        for t in range(NT):
            c[:, base + 16 * t:base + 16 * t + 16] = np.concatenate([tab[t], tab[t]], axis=1)
    for t in range(NT):
        c[:, C_TOK + t] = t * P + np.arange(P)
    half = np.arange(P) // BS
    c[:, C_HALF] = half
    c[:, C_HALF + 1] = 2 * T + np.arange(P) - half
    return c


def build(nc, consts, x, c, norm1_g, norm2_g, w_ada, b_ada, w_in, w_out, a_q_norm_g, a_k_norm_g, a_lambda,
          a_sub_g, b_q_norm_g, b_k_norm_g, b_kv_norm_g, b_w_uv, router_w, router_b, w_gate, b_gate, w_up,
          b_up, w_down, b_down, out):
    with ExitStack() as ctx:
        sems = {}

        def sem(name):
            if name not in sems:
                sems[name] = ctx.enter_context(nc.semaphore(name))
            return sems[name]

        def sb(name, cols, dt=F32):
            return ctx.enter_context(nc.sbuf_tensor(name, [P, cols], dt))

        xhat_dram = nc.dram_tensor("xhat_scratch", (2 * T, D // 2), F32, kind="Internal").ap()
        acc_dram = nc.dram_tensor("acc_scratch", (2 * T + P, D // 2), F32, kind="Internal").ap()

        W = sb("W", 5 * 8192)
        X = sb("X", 4096)
        H = sb("H", 4096)
        CT = sb("CT", C_ALL)
        slot = [W[:, i * 8192:(i + 1) * 8192].rearrange("p (k n) -> p k n", k=KT) for i in range(5)]
        GATE, UP, DOWN = (slot[0], slot[3]), (slot[1], slot[4]), slot[2]
        ident = CT[:, C_ID:C_ID + P]
        tri = CT[:, C_TRI:C_TRI + P]
        ones = CT[:, C_ONE:C_ONE + P]
        iota = CT[:, C_IOTA:C_IOTA + P]

        gains = sb("gains", 4 * HD + 2 * P)
        cols = sb("cols", 72)
        mod = sb("mod", 48)
        silu = sb("silu", 8)
        amp = sb("amp", 16)
        sm = sb("sm", 128)
        iw = sb("iw", NT * 8)
        uv = sb("uv", 8 * HD)
        rw = sb("rw", KT * NE)
        rb = sb("rb", NE)
        route = sb("route", 4 * 128 + 5 * 16 + 3 * 32)
        tab = sb("tab", 2 * MAXB)
        tabi = sb("tabi", 2 * MAXB + 1, U32)
        cum = sb("cum", NE + 1, I32)
        gidx = sb("gidx", 2, U32)
        biasT = sb("biasT", 2 * KT * NE)

        A0 = 3 * 8192
        QKT = W[:, A0:A0 + 18 * 512].rearrange("p (h t) -> p h t", h=18)
        o = A0 + 18 * 512
        V = W[:, o:o + 2048].rearrange("p (t n) -> p t n", t=NT)
        LAT = W[:, o + 2048:o + 2560].rearrange("p (t n) -> p t n", t=NT)
        P1 = W[:, o + 2560:o + 3584].rearrange("p (b n) -> p b n", b=2)
        P2 = W[:, o + 3584:o + 4608].rearrange("p (b n) -> p b n", b=2)
        TMP = W[:, o + 2560:o + 4096].rearrange("p (b n) -> p b n", b=3)
        SQ = W[:, o + 4096:o + 4608]
        AT = W[:, o + 4608:o + 5632].rearrange("p (b n) -> p b n", b=2)
        OT = W[:, o + 5632:o + 5888].rearrange("p (b n) -> p b n", b=2)
        amo = [o + 5888, o + 6016, o + 6272, o + 6656]
        AM = [W[:, amo[i]:amo[i] + (i + 1) * P] for i in range(NT)]
        RT = SQ
        AQ, AK, BQ, IQ, BK, IK = 0, 4, 8, 12, 16, 17

        WIN = W[:, 2 * 8192:3 * 8192].rearrange("p (b k n) -> p b k n", b=2, k=KT)
        hT = H[:, :].rearrange("p (k t) -> p k t", k=KT)
        xt = X[:, :].rearrange("p (t d) -> p t d", t=NT)
        MIX = H[:, :].rearrange("p (t d) -> p t d", t=NT)
        mixT = X[:, :].rearrange("p (k t) -> p k t", k=KT)
        x2 = MIX
        XH2 = slot[3].rearrange("p k n -> p (k n)")[:, 0:4096].rearrange("p (t d) -> p t d", t=NT)
        h2T = slot[3].rearrange("p k n -> p (k n)")[:, 4096:8192].rearrange("p (k t) -> p k t", k=KT)
        s4 = slot[4].rearrange("p k n -> p (k n)")
        G1B = s4[:, 0:1024]
        DIAG = s4[:, 1024:2048].rearrange("p (k n) -> p k n", k=KT)
        BROW = s4[0:NE, 2048:5120].rearrange("p (m n) -> p m n", m=3)
        GT = s4[0:NE, 5120:5632]
        G2B = s4[:, 5632:6656]
        LH = X[:, 1408:3456].rearrange("p (j s) -> p j s", j=16)
        s3 = slot[3].rearrange("p k n -> p (k n)")
        RH = s3[:, 4096:6144].rearrange("p (j s) -> p j s", j=16)
        OB = s3[:, 6144:7168].rearrange("p (j s) -> p j s", j=16)

        rows = H[0:72, 0:P]
        lamb = H[:, 1024:1280]

        xg = X[:, 0:512]
        ysb = X[:, 512:1024]
        xT = X[:, 1024:1536].rearrange("p (k s) -> p k s", k=KT)
        gsb = X[:, 1536:2048].rearrange("p (h n) -> p h n", h=2)
        usb = X[:, 2048:2560].rearrange("p (h n) -> p h n", h=2)
        gc = X[:, 2560:3072].rearrange("p (k s) -> p k s", k=KT)
        uc = X[:, 3072:3584].rearrange("p (k s) -> p k s", k=KT)
        sg = X[:, 3584:4096].rearrange("p (k s) -> p k s", k=KT)
        aT = H[:, 0:512].rearrange("p (k s) -> p k s", k=KT)
        bgT, buT = [biasT[:, m * KT * NE:(m + 1) * KT * NE].rearrange("p (k e) -> p k e", k=KT) for m in range(2)]

        lgT = X[:, 1152:1280]
        gmat = X[:, 3584:3712]
        tf, tf2 = X[:, 3456:3520], X[:, 3520:3584]
        G2H = H[:, 512:1024]
        silu32 = biasT[:, 0:256]
        MR = biasT[:, 256:512]

        bank = [ctx.enter_context(nc.psum_tensor(f"bank{i}", [P, 512], F32)) for i in range(8)]

        def settle(eng, name):
            eng.sem_inc(sem(name + "_settled"), 1)

        IQc, MISC, BQc, AQc, AKc, AVc = range(6)
        CSRC = {IQc: 2240, BQc: 1536, AQc: 0, AKc: 512, AVc: 1024}
        PAIR0 = {IQc: IQ, BQc: BQ, AQc: AQ, AKc: AK, MISC: BK}
        GAIN = {BQc: 2, AQc: 0, AKc: 1}
        steps = [(ch, t) for ch in range(6) for t in range(NT)]
        NST = len(steps)
        NTR = 5 * NT
        normed = [ch in (MISC, BQc, AQc, AKc) for ch, _ in steps]
        nth_norm = [sum(normed[:n + 1]) for n in range(NST)]

        order = [1, 0, 2, 3, 4, 5]
        units_c = [(i, h) for i in range(1, NT) for h in range(8)]
        units_d = [(i, h) for i in range(NT) for h in range(4)]
        units_e = [(i, h) for i in range(NT) for h in range(8)]
        ROUNDS = [(i, r) for i in range(1, NT) for r in range(16)]

        block = ctx.enter_context(nc.Block())

        @block.sync
        def _(sp):
            def ada(j, s):
                sp.dma_start(slot[s], w_ada[:, j * D:(j + 1) * D].rearrange("(k p) n -> p k n", p=P)) \
                    .then_inc(sem(f"ada_loaded{s}"), 16)

            def win(ch):
                buf = WIN[:, ch % 2]
                if ch >= 2:
                    sp.wait_ge(sem("proj_done"), 4 * (ch - 1))
                if ch == MISC:
                    sp.dma_start(buf[:, :, 0:192], w_in[:, 2048:2240].rearrange("(k p) n -> p k n", p=P)) \
                        .then_inc(sem("win_loaded1"), 16)
                    sp.dma_start(buf[:, :, 192:264], w_in[:, 2752:2824].rearrange("(k p) n -> p k n", p=P)) \
                        .then_inc(sem("win_loaded_misc"), 16)
                else:
                    sp.dma_start(buf, w_in[:, CSRC[ch]:CSRC[ch] + 512].rearrange("(k p) n -> p k n", p=P)) \
                        .then_inc(sem(f"win_loaded{ch % 2}"), 16)

            sp.dma_start(CT[:, :], consts).then_inc(sem("const_loaded"), 16)
            for i, (src, n) in enumerate(((c, 8), (norm1_g, 8), (norm2_g, 8), (b_ada, 48))):
                sp.dma_start(H[8 * i:8 * i + n, 0:P], src.rearrange("a (r q) -> (a r) q", q=P)) \
                    .then_inc(sem("rows_loaded"), 16)
            for t in range(NT):
                sp.dma_start(xt[:, t, :], x[t * P:(t + 1) * P, :]).then_inc(sem(f"x_loaded{t}"), 16)
            ada(1, 1)
            ada(0, 0)
            win(0)
            win(1)
            for j, s in ((2, 0), (3, 1), (4, 0), (5, 1)):
                sp.wait_ge(sem("mod_done"), max(2, j - 1))
                ada(j, s)
                win(j)
            sp.wait_ge(sem("proj_done"), NST)
            sp.dma_start(slot[2], w_out.rearrange("(k p) n -> p k n", p=P)).then_inc(sem("wout_loaded"), 16)
            sp.wait_ge(sem("mod_done"), 6)
            e_src = {"gate": w_gate, "up": w_up, "down": w_down}

            def expert(kind, e, dst, s):
                for q in range(WQ):
                    ks = slice(q * KT // WQ, (q + 1) * KT // WQ)
                    src = e_src[kind][bass.ds(e, 1), q * D // WQ:(q + 1) * D // WQ, :]
                    sp.dma_start(dst[:, ks, :], src.rearrange("e (k p) n -> p (e k) n", p=P)) \
                        .then_inc(sem(f"{kind}_loaded{s}_{q}"), 16)

            expert("gate", 0, GATE[0], 0)
            expert("up", 0, UP[0], 0)
            sp.wait_ge(sem("mixT_done"), KT)
            sp.dma_start(x2, x.rearrange("(t p) d -> p t d", p=P)).then_inc(sem("x_again"), 16)
            sp.wait_ge(sem("sparse_out_done"), len(units_e))
            sp.dma_start(BROW[:, 0, :], b_gate).then_inc(sem("brow_loaded"), 16)
            sp.dma_start(BROW[:, 1, :], b_up).then_inc(sem("brow_loaded"), 16)
            sp.dma_start(BROW[:, 2, :], b_down).then_inc(sem("brow_loaded"), 16)
            sp.wait_ge(sem("wout_done"), 2 * NT)
            expert("down", 0, DOWN, 0)
            for t in range(NT):
                sp.wait_ge(sem("xhat2_ready"), t + 1)
                sp.dma_start(xhat_dram[2 * t * P:2 * (t + 1) * P, :].rearrange("(p h) d -> p (h d)", h=2),
                             XH2[:, t, :]).then_inc(sem("xhat_stored"), 16)
            sp.wait_ge(sem("router_done"), 1)
            sp.wait_ge(sem("xhat_stored"), 16 * NT)
            for t in range(NT):
                sp.wait_ge(sem("start_ready"), t + 1)
                sp.dma_start(acc_dram[2 * t * P:2 * (t + 1) * P, :].rearrange("(p h) d -> p (h d)", h=2),
                             x2[:, t, :]).then_inc(sem("start_stored"), 16)
            sp.wait_ge(sem("tables_done"), 1)
            expert("gate", 1, GATE[1], 1)
            sp.wait_ge(sem("biasT_done"), 1)
            sp.wait_ge(sem("g2_copied"), 1)
            expert("up", 1, UP[1], 1)
            sp.wait_ge(sem("cum_ready"), 1)

            def blocks_before(e):
                return sp.value_load(cum[0:1, bass.ds(e, 1)], min_val=1, max_val=MAXB - 1)

            with sp.Fori(1, NE // 2) as pr:
                for s in range(2):
                    e = pr * 2 + s
                    last = sp.snap(blocks_before(e - 1))
                    sp.wait_ge(sem("gate_done1"), last)
                    expert("gate", e, GATE[s], s)
                    sp.wait_ge(sem("down_done"), last)
                    expert("down", e - 1, DOWN, 0)
                    expert("up", e, UP[s], s)
            sp.wait_ge(sem("down_done"), blocks_before(NE - 1))
            expert("down", NE - 1, DOWN, 0)
            total = sp.snap(blocks_before(NE))
            sp.wait_ge(sem("scattered"), total * 16 + 16)
            settle(sp, "sp")
            for q in range(4):
                sp.dma_start(out[q * P:(q + 1) * P, :].rearrange("t (h d) -> (t h) d", h=2),
                             acc_dram[2 * q * P:2 * (q + 1) * P, :]).then_inc(sem("out_stored"), 16)
            sp.wait_ge(sem("out_stored"), 64)

        @block.gpsimd
        def _(pool):
            small = [(gains[:, 0:64], a_q_norm_g), (gains[:, 64:128], a_k_norm_g), (gains[:, 128:192], b_q_norm_g),
                     (gains[:, 192:256], b_k_norm_g), (gains[:, 256:384], b_kv_norm_g),
                     (gains[:, 384:512], a_sub_g), (rb[:, :], router_b)]
            pool.dma_start(lamb, a_lambda.rearrange("a l q -> a (l q)").to_broadcast([P, 256])) \
                .then_inc(sem("small_loaded"), 16)
            for dst, src in small:
                pool.dma_start(dst, src.to_broadcast([P, src.shape[1]])).then_inc(sem("small_loaded"), 16)
            pool.dma_start(uv[:, :].rearrange("p (h n) -> p h n", h=8), b_w_uv.rearrange("h c n -> c h n")) \
                .then_inc(sem("small_loaded"), 16)
            pool.dma_start(rw[:, :].rearrange("p (k e) -> p k e", k=KT),
                           router_w.rearrange("(k p) e -> p k e", p=P)).then_inc(sem("small_loaded"), 16)

            pool.wait_ge(sem("cum_ready"), 1)
            pool.wait_ge(sem("tabi_ready"), 1)
            pool.wait_ge(sem("xhat_stored"), 16 * NT)
            total = pool.value_load(cum[0:1, NE:NE + 1], min_val=NE, max_val=MAXB - 1)

            def gather():
                settle(pool, "pool")
                pool.indirect_dma_start(out=xg, out_offset=None, in_=xhat_dram,
                                        in_offset=bass.IndirectOffsetOnAxis(ap=gidx[:, 0:1], axis=0),
                                        bounds_check=2 * T - 1, oob_is_err=True).then_inc(sem("gathered"), 16)

            pool.tensor_copy(gidx[:, 0:1], tabi[:, 0:1]).then_inc(sem("gidx_ready"), 1)
            pool.wait_ge(sem("gidx_ready"), 1)
            gather()
            pool.wait_ge(sem("start_ready"), 1)
            pool.dma_start(acc_dram[2 * T:2 * T + P, :], x2[:, 0, 0:512]).then_inc(sem("scattered"), 16)
            pool.wait_ge(sem("start_stored"), 16 * NT)
            pool.wait_ge(sem("xg_used"), 1)
            pool.tensor_copy(gidx[:, 0:1], tabi[:, 1:2]).then_inc(sem("gidx_ready"), 1)
            pool.wait_ge(sem("gidx_ready"), 2)
            gather()
            with pool.Fori(0, total) as b:
                b1 = pool.snap(b + 1)
                pool.wait_ge(sem("xg_used"), b + 2)
                pool.wait_ge(sem("gathered"), b * 16 + 32)
                pool.tensor_copy(gidx[:, 0:1], tabi[:, bass.ds(b + 2, 1)]).then_inc(sem("gidx_ready"), 1)
                pool.wait_ge(sem("gidx_ready"), b + 3)
                gather()
                pool.wait_ge(sem("scattered"), b1 * 16)
                pool.tensor_copy(gidx[:, 1:2], tabi[:, bass.ds(b + (MAXB + 1), 1)]).then_inc(sem("sidx_ready"), 1)
                pool.wait_ge(sem("sidx_ready"), b1)
                pool.wait_ge(sem("ysb_ready"), b1)
                pool.wait_ge(sem("scattered"), b1 * 16)
                settle(pool, "pool")
                pool.indirect_dma_start(out=acc_dram, out_offset=bass.IndirectOffsetOnAxis(ap=gidx[:, 1:2], axis=0),
                                        in_=ysb, in_offset=None, bounds_check=2 * T + P - 1, oob_is_err=True,
                                        compute_op=ALU.add).then_inc(sem("scattered"), 16)
            pool.wait_ge(sem("gathered"), total * 16 + 32)

        @block.scalar
        def _(act):
            act.wait_ge(sem("cols_ready"), 1)
            act.activation(silu[:, :], cols[:, 0:8], ACT.Exp, scale=-1.0).then_inc(sem("exp_c"), 1)

            def rms_tiles(src, n, name, ready):
                for t in range(NT):
                    ready(t)
                    if t:
                        act.wait_ge(sem(f"{name}_ssq"), t)
                    act.activation(W[:, A0 + 8192 + 6144:A0 + 8192 + 7168] if name == "n1" else
                                   s4[:, 5120:6144], src[:, t, :], ACT.Square,
                                   accum_out=sm[:, n + t:n + t + 1]).then_inc(sem(f"{name}_ssq"), 1)

            rms_tiles(xt, 4, "n1", lambda t: act.wait_ge(sem(f"x_loaded{t}"), 16))

            def mod_copy(j):
                act.wait_ge(sem("mod_done"), order.index(j) + 1)
                act.activation(MR, bank[7][:, 0:256], ACT.Copy).then_inc(sem("mod_rows"), 1)

            act.wait_ge(sem("n1_ms"), 1)
            act.activation(sm[:, 12:16], sm[:, 8:12], ACT.Sqrt).then_inc(sem("n1_sd"), 1)
            mod_copy(1)
            mod_copy(0)
            act.wait_ge(sem("lam_dot"), 2)
            act.activation(sm[:, 2:4], sm[:, 0:2], ACT.Exp).then_inc(sem("lam_exp"), 1)
            act.wait_ge(sem("amp1_ready"), 1)
            for k in range(0, KT, 2):
                act.wait_ge(sem("xT_done"), k + 1)
                act.activation(hT[:, k, :], bank[k % 4][:, :], ACT.Identity, bias=mod[:, k:k + 1],
                               scale=amp[:, k:k + 1]).then_inc(sem("hT_act"), 1)

            def evac_heads(n):
                ch, t = steps[n]
                act.wait_ge(sem("qt_done"), n + 1)
                m = 2 if ch == MISC else 4
                act.activation(QKT[:, PAIR0[ch]:PAIR0[ch] + m, t * P:(t + 1) * P],
                               bank[4 + n % 2][:, 0:m * P].rearrange("p (m q) -> p m q", m=m),
                               ACT.Copy).then_inc(sem("qt_evac"), 1)

            for n, (ch, t) in enumerate(steps):
                act.wait_ge(sem("proj_done"), n + 1)
                if n >= 3:
                    act.wait_ge(sem("qt_done"), min(n - 2, NTR))
                tmp = TMP[:, n % 3]
                ps = bank[n % 4]
                if ch == AVc:
                    act.activation(V[:, t, :], ps[:, :], ACT.Copy).then_inc(sem("proj_evac"), 1)
                elif ch == MISC:
                    two = [P, 2, HD]
                    act.activation(tmp[:, 0:128].rearrange("p (a q) -> p a q", a=2),
                                   ps[:, 0:64].unsqueeze(1).to_broadcast(two), ACT.Copy)
                    act.activation(tmp[:, 128:256].rearrange("p (a q) -> p a q", a=2),
                                   ps[:, 192:256].unsqueeze(1).to_broadcast(two), ACT.Copy)
                    act.activation(tmp[:, 256:384], ps[:, 64:192], ACT.Copy)
                    act.activation(tmp[:, 384:392], ps[:, 256:264], ACT.Copy).then_inc(sem("proj_evac"), 1)
                else:
                    act.activation(tmp, ps[:, :], ACT.Copy).then_inc(sem("proj_evac"), 1)
                if normed[n]:
                    act.wait_ge(sem("head_ms"), nth_norm[n])
                    act.activation(sm[:, 24:32], sm[:, 16:24], ACT.Sqrt).then_inc(sem("head_sd"), 1)
                if 2 <= n < NTR + 2:
                    evac_heads(n - 2)
                if t == 3 and 1 <= ch <= 4:
                    mod_copy(ch + 1)

            act.wait_ge(sem("qt_done"), NTR)
            for n, (i, h) in enumerate(units_c):
                nk = (i + 1) * P
                act.wait_ge(sem("iqk_done"), n + 1)
                if n >= 2:
                    act.wait_ge(sem("rel_used"), n - 1)
                act.activation(P1[:, n % 2, 0:nk], bank[n % 2][:, 0:nk], ACT.Relu).then_inc(sem("rel_ready"), 1)

            def diff_exp(n):
                i, h = units_d[n]
                nk = (i + 1) * P
                act.wait_ge(sem("diff_max"), n + 1)
                if n == 0:
                    act.wait_ge(sem("rel_used"), len(units_c))
                if n >= 2:
                    act.wait_ge(sem("diff_T"), n - 1)
                for j, Pj in enumerate((P1, P2)):
                    ins = act.activation(Pj[:, n % 2, 0:nk], bank[2 + 2 * (n % 2) + j][:, 0:nk], ACT.Exp,
                                         bias=sm[:, 36 + 2 * (n % 2) + j:37 + 2 * (n % 2) + j], scale=SCALE,
                                         accum_out=sm[:, 40 + 2 * (n % 4) + j:41 + 2 * (n % 4) + j])
                ins.then_inc(sem("diff_exp"), 1)

            def diff_evac(n):
                nk = (units_d[n][0] + 1) * P
                act.wait_ge(sem("diff_T"), n + 1)
                if n >= 2:
                    act.wait_ge(sem("diff_pv"), n - 1)
                act.activation(AT[:, n % 2, 0:nk], bank[6][:, 0:nk], ACT.Copy).then_inc(sem("diff_Te"), 1)

            for n in range(len(units_d) + 1):
                if n < len(units_d):
                    diff_exp(n)
                if n >= 1:
                    diff_evac(n - 1)

            def sparse_exp(n):
                i, h = units_e[n]
                nk = (i + 1) * P
                act.wait_ge(sem("sparse_max"), n + 1)
                if n >= 2:
                    act.wait_ge(sem("sparse_T"), n - 1)
                act.activation(P1[:, n % 2, 0:nk], P2[:, n % 2, 0:nk], ACT.Exp, bias=sm[:, 52 + n % 2:53 + n % 2],
                               scale=SCALE, accum_out=sm[:, 56 + n % 4:57 + n % 4]).then_inc(sem("sparse_exp"), 1)

            def sparse_evac(n):
                act.wait_ge(sem("sparse_oT"), n + 1)
                if n >= 2:
                    act.wait_ge(sem("sparse_out_done"), n - 1)
                act.activation(OT[:, n % 2, :], bank[5 + 2 * (n % 2)][:, 0:P], ACT.Copy) \
                    .then_inc(sem("sparse_oTe"), 1)

            for n in range(len(units_e) + 2):
                if n < len(units_e):
                    sparse_exp(n)
                if n >= 2:
                    sparse_evac(n - 2)

            act.wait_ge(sem("sub_ms"), 1)
            act.activation(sm[:, 80:96], sm[:, 64:80], ACT.Sqrt).then_inc(sem("sub_sd"), 1)
            act.wait_ge(sem("g1b_done"), 1)
            for j in range(2):
                act.activation(G1B[:, j * 512:(j + 1) * 512], bank[4 + j][:, :], ACT.Copy).then_inc(sem("g1b_ready"), 1)
            for k in range(0, KT, 2):
                act.wait_ge(sem("mixT_done"), k + 1)
                act.activation(mixT[:, k, :], bank[k % 4][:, :], ACT.Copy).then_inc(sem("mixT_act"), 1)
            for t in range(NT):
                act.wait_ge(sem("x2_ready"), t + 1)
                act.activation(s4[:, 5120:6144], x2[:, t, :], ACT.Square,
                               accum_out=sm[:, 4 + t:5 + t]).then_inc(sem("n2_ssq"), 1)
                act.wait_ge(sem("n2_ms"), t + 1)
                act.activation(sm[:, 12 + t:13 + t], sm[:, 8 + t:9 + t], ACT.Sqrt).then_inc(sem("n2_sd"), 1)
            for k in range(0, KT, 2):
                act.wait_ge(sem("xT2_done"), k + 1)
                act.activation(h2T[:, k, :], bank[k % 4][:, :], ACT.Identity, bias=mod[:, 24 + k:25 + k],
                               scale=amp[:, 8 + k:9 + k]).then_inc(sem("h2T_act"), 1)
            act.wait_ge(sem("gate_sub"), 1)
            act.activation(route[:, 528:544], route[:, 512:528], ACT.Exp).then_inc(sem("gate_exp"), 1)

            act.wait_ge(sem("cum_ready"), 1)
            act.wait_ge(sem("tabi_ready"), 1)
            total = act.value_load(cum[0:1, NE:NE + 1], min_val=NE, max_val=MAXB - 1)
            with act.Fori(0, total) as b:
                halves = [act.snap(b * 2 + 1), act.snap(b * 2 + 2)]
                for hf in range(2):
                    hs = slice(4 * hf, 4 * hf + 4)
                    act.wait_ge(sem("gclip"), halves[hf])
                    act.activation(sg[:, hs, :], gc[:, hs, :], ACT.Sigmoid, scale=ALPHA).then_inc(sem("sig_ready"), 1)

        @block.tensor
        def _(pe):
            pe.wait_ge(sem("const_loaded"), 16)
            pe.wait_ge(sem("rows_loaded"), 64)
            pe.transpose(bank[7][:, 0:72], rows, ident[0:72, 0:72]).then_inc(sem("rowsT"), 1)
            pe.wait_ge(sem("silu_ready"), 1)

            def mod_part(j):
                s = j % 2
                n = order.index(j)
                pe.wait_ge(sem(f"ada_loaded{s}"), 16 * (j // 2 + 1))
                if n:
                    pe.wait_ge(sem("mod_rows"), n)
                for k in range(KT):
                    for q in range(4):
                        ins = pe.matmul(bank[7][32 * q:32 * q + 32, 0:256], silu32[:, 32 * k:32 * k + 32],
                                        slot[s][:, k, 256 * q:256 * q + 256], start=(k == 0), stop=(k == KT - 1))
                ins.then_inc(sem("mod_done"), 1)

            def mod_columns(j):
                n = order.index(j)
                pe.wait_ge(sem("mod_rows"), n + 1)
                if n:
                    pe.wait_ge(sem("mod_read"), n)
                for q in range(2):
                    ins = pe.transpose(bank[6][:, q * P:(q + 1) * P], MR[:, q * P:(q + 1) * P], ident)
                ins.then_inc(sem("mod_cols"), 1)

            def tile_transposes(src, done, act_sem, dve_sem, first_wait):
                for k in range(KT):
                    if k >= 4:
                        pe.wait_ge(sem(act_sem if k % 2 == 0 else dve_sem), (k - 4) // 2 + 1)
                    for t in range(NT):
                        if k == 0:
                            first_wait(t)
                        ins = pe.transpose(bank[k % 4][:, t * P:(t + 1) * P], src[:, t, k * P:(k + 1) * P], ident)
                    ins.then_inc(sem(done), 1)

            mod_part(1)
            mod_columns(1)
            mod_part(0)
            mod_columns(0)
            tile_transposes(xt, "xT_done", "hT_act", "hT_dve", lambda t: pe.wait_ge(sem("xhat_ready"), t + 1))
            pe.wait_ge(sem("hT_act"), 4)
            pe.wait_ge(sem("hT_dve"), 4)

            def heads(n):
                ch, t = steps[n]
                pe.wait_ge(sem("heads_ready"), n + 1)
                if n >= 2:
                    pe.wait_ge(sem("qt_evac"), n - 1)
                for m in range(2 if ch == MISC else 4):
                    ins = pe.transpose(bank[4 + n % 2][:, m * P:(m + 1) * P], TMP[:, n % 3, m * P:(m + 1) * P], ident)
                ins.then_inc(sem("qt_done"), 1)

            for n, (ch, t) in enumerate(steps):
                if t == 0:
                    pe.wait_ge(sem(f"win_loaded{ch % 2}"), 16 * (ch // 2 + 1))
                    if ch == MISC:
                        pe.wait_ge(sem("win_loaded_misc"), 16)
                if n >= 4:
                    pe.wait_ge(sem("proj_evac"), n - 3)
                w = 264 if ch == MISC else 512
                for k in range(KT):
                    ins = pe.matmul(bank[n % 4][:, 0:w], hT[:, k, t * P:(t + 1) * P], WIN[:, ch % 2, k, 0:w],
                                    start=(k == 0), stop=(k == KT - 1))
                ins.then_inc(sem("proj_done"), 1)
                if 2 <= n < NTR + 2:
                    heads(n - 2)
                if t == 3 and 1 <= ch <= 4:
                    mod_part(ch + 1)
                    mod_columns(ch + 1)
            pe.wait_ge(sem("proj_evac"), NST)
            pe.wait_ge(sem("qt_evac"), NTR)

            def half(h):
                return slice(HD * (h % 2), HD * (h % 2) + HD)

            for n, (i, h) in enumerate(units_c):
                if n >= 2:
                    pe.wait_ge(sem("rel_ready"), n - 1)
                pe.matmul(bank[n % 2][:, 0:(i + 1) * P], QKT[half(h), IQ + h // 2, i * P:(i + 1) * P],
                          QKT[half(h), IK, 0:(i + 1) * P], start=True, stop=True).then_inc(sem("iqk_done"), 1)

            for n in range(len(units_d) + 2):
                if n < len(units_d):
                    i, h = units_d[n]
                    if n >= 2:
                        pe.wait_ge(sem("diff_exp"), n - 1)
                    for j in range(2):
                        ins = pe.matmul(bank[2 + 2 * (n % 2) + j][:, 0:(i + 1) * P],
                                        QKT[half(h), AQ + 2 * j + h // 2, i * P:(i + 1) * P],
                                        QKT[half(h), AK + 2 * j + h // 2, 0:(i + 1) * P], start=True, stop=True)
                    ins.then_inc(sem("diff_qk"), 1)
                if 1 <= n <= len(units_d):
                    m = n - 1
                    pe.wait_ge(sem("diff_a"), m + 1)
                    if m >= 1:
                        pe.wait_ge(sem("diff_Te"), m)
                    for kb in range(units_d[m][0] + 1):
                        ins = pe.transpose(bank[6][:, kb * P:(kb + 1) * P], P1[:, m % 2, kb * P:(kb + 1) * P], ident)
                    ins.then_inc(sem("diff_T"), 1)
                if n >= 2:
                    m = n - 2
                    i, h = units_d[m]
                    pe.wait_ge(sem("diff_Te"), m + 1)
                    if m >= 2:
                        pe.wait_ge(sem("diff_out"), m - 1)
                    for kb in range(i + 1):
                        ins = pe.matmul(bank[7 * (m % 2)][:, 0:P], AT[:, m % 2, kb * P:(kb + 1) * P],
                                        V[:, kb, h * P:(h + 1) * P], start=(kb == 0), stop=(kb == i))
                    ins.then_inc(sem("diff_pv"), 1)

            pe.wait_ge(sem("diff_out"), len(units_d))
            pe.wait_ge(sem("small_loaded"), 16 * 10)
            NEU = len(units_e)
            for n in range(NEU + 3):
                if n < NEU:
                    i, h = units_e[n]
                    if n >= 2:
                        pe.wait_ge(sem("sparse_max"), n - 1)
                    pe.matmul(bank[2 + n % 2][:, 0:(i + 1) * P], QKT[half(h), BQ + h // 2, i * P:(i + 1) * P],
                              QKT[half(h), BK, 0:(i + 1) * P], start=True, stop=True).then_inc(sem("sparse_qk"), 1)
                if 1 <= n <= NEU:
                    m = n - 1
                    pe.wait_ge(sem("sparse_exp"), m + 1)
                    if m >= 2:
                        pe.wait_ge(sem("sparse_Te"), m - 1)
                    for kb in range(units_e[m][0] + 1):
                        ins = pe.transpose(bank[6 * (m % 2)][:, kb * P:(kb + 1) * P],
                                           P1[:, m % 2, kb * P:(kb + 1) * P], ident)
                    ins.then_inc(sem("sparse_T"), 1)
                if 2 <= n <= NEU + 1:
                    m = n - 2
                    i = units_e[m][0]
                    pe.wait_ge(sem("sparse_Te"), m + 1)
                    if m >= 2:
                        pe.wait_ge(sem("sparse_oTe"), m - 1)
                    for kb in range(i + 1):
                        ins = pe.matmul(bank[5 + 2 * (m % 2)][:, 0:P], LAT[:, kb, :],
                                        AT[:, m % 2, kb * P:(kb + 1) * P], start=(kb == 0), stop=(kb == i))
                    ins.then_inc(sem("sparse_oT"), 1)
                if n >= 3:
                    m = n - 3
                    pe.wait_ge(sem("sparse_oTe"), m + 1)
                    if m >= 2:
                        pe.wait_ge(sem("sparse_out"), m - 1)
                    pe.matmul(bank[1 + 3 * (m % 2)][:, 0:HD], OT[:, m % 2, :],
                              uv[:, units_e[m][1] * HD:(units_e[m][1] + 1) * HD],
                              start=True, stop=True).then_inc(sem("sparse_out_done"), 1)

            pe.wait_ge(sem("diag_ready"), 1)
            for k in range(KT):
                ins = pe.matmul(bank[4 + k // 4][:, (k % 4) * P:(k % 4 + 1) * P], ones, DIAG[:, k, :],
                                start=True, stop=True)
            ins.then_inc(sem("g1b_done"), 1)
            pe.wait_ge(sem("mix_ready"), 1)
            tile_transposes(MIX, "mixT_done", "mixT_act", "mixT_dve", lambda t: None)
            pe.wait_ge(sem("mixT_act"), 4)
            pe.wait_ge(sem("mixT_dve"), 4)
            pe.wait_ge(sem("wout_loaded"), 16)
            for t in range(NT):
                for hf in range(2):
                    n = 2 * t + hf
                    if n >= 4:
                        pe.wait_ge(sem("mix_added"), n - 3)
                    for k in range(KT):
                        ins = pe.matmul(bank[n % 4][:, :], mixT[:, k, t * P:(t + 1) * P],
                                        slot[2][:, k, hf * 512:(hf + 1) * 512], start=(k == 0), stop=(k == KT - 1))
                    ins.then_inc(sem("wout_done"), 1)
            pe.wait_ge(sem("brow_loaded"), 48)
            for m in range(2):
                for k in range(KT):
                    ins = pe.transpose(bank[5 + m][:, k * NE:(k + 1) * NE], BROW[:, m, k * P:(k + 1) * P],
                                       ident[0:NE, 0:NE])
            ins.then_inc(sem("brow_T"), 1)
            pe.wait_ge(sem("mix_added"), 2 * NT)
            tile_transposes(XH2, "xT2_done", "h2T_act", "h2T_dve", lambda t: pe.wait_ge(sem("xhat2_ready"), t + 1))
            pe.wait_ge(sem("h2T_act"), 4)
            pe.wait_ge(sem("h2T_dve"), 4)
            for k in range(KT):
                for t in range(NT):
                    ins = pe.matmul(bank[4][NE * t:NE * t + NE, 0:P], rw[:, k * NE:(k + 1) * NE],
                                    h2T[:, k, t * P:(t + 1) * P], start=(k == 0), stop=(k == KT - 1))
            ins.then_inc(sem("router_done"), 1)
            pe.wait_ge(sem("logits_sb"), 1)
            pe.transpose(bank[0][:, 0:P], lgT, ident).then_inc(sem("logits_T"), 1)
            pe.wait_ge(sem("mask_ready"), 1)
            for t in range(NT):
                for u in range(t + 1):
                    pe.matmul(bank[0][:, t * NE:(t + 1) * NE], tri if u == t else ones,
                              route[:, u * NE:(u + 1) * NE], start=(u == 0), stop=(u == t))
            for u in range(NT):
                ins = pe.matmul(bank[0][:, 128:160], ones, route[:, u * NE:(u + 1) * NE],
                                start=(u == 0), stop=(u == NT - 1))
            ins.then_inc(sem("rank_done"), 1)
            pe.wait_ge(sem("onehot_ready"), 1)
            for j in range(16):
                ins = pe.matmul(bank[1][:, 0:2 * MAXB], LH[:, j, :], RH[:, j, :], start=(j == 0), stop=(j == 15))
            ins.then_inc(sem("tables_done"), 1)
            pe.wait_ge(sem("gate_mat"), 1)
            for t in range(NT):
                ins = pe.transpose(bank[2][0:NE, t * P:(t + 1) * P], gmat[:, t * NE:(t + 1) * NE], ident)
            ins.then_inc(sem("gate_T"), 1)
            pe.wait_ge(sem("diag2_ready"), 1)
            for k in range(KT):
                ins = pe.matmul(bank[3 + k // 4][:, (k % 4) * P:(k % 4 + 1) * P], ones, DIAG[:, k, :],
                                start=True, stop=True)
            ins.then_inc(sem("g2b_done"), 1)
            pe.wait_ge(sem("gate_Te"), 1)
            for n in range(2 * NT):
                t, hf = n // 2, n % 2
                if n >= 2:
                    pe.wait_ge(sem("bias_added"), n - 1)
                pe.matmul(bank[5 + hf][:, :], GT[:, t * P:(t + 1) * P], BROW[:, 2, hf * 512:hf * 512 + 512],
                          start=True, stop=True).then_inc(sem("bias_done"), 1)

            def rows_in():
                settle(pe, "pe")
                out3 = bank[7][:, :].rearrange("p (h j s) -> p j h s", h=2, j=4)
                for j in range(4):
                    ins = pe.transpose(out3[:, j], xg[:, j * P:(j + 1) * P], ident)
                ins.then_inc(sem("xg_used"), 1)

            pe.wait_ge(sem("cum_ready"), 1)
            pe.wait_ge(sem("tabi_ready"), 1)
            pe.wait_ge(sem("gathered"), 16)
            rows_in()

            with pe.Fori(0, NE // 2) as pr:
                for s in range(2):
                    e = pr * 2 + s
                    first = pe.value_load(cum[0:1, bass.ds(e, 1)], min_val=0, max_val=MAXB - 1)
                    end = pe.value_load(cum[0:1, bass.ds(e + 1, 1)], min_val=1, max_val=MAXB - 1)
                    loads = pe.snap((pr + 1) * 16)
                    dloads = pe.snap((e + 1) * 16)
                    with pe.Fori(first, end) as b:
                        b1 = pe.snap(b + 1)

                        def product(bk, hf, wt, done, kind):
                            for k in range(KT):
                                if hf == 0 and k % (KT // WQ) == 0:
                                    pe.wait_ge(sem(f"{kind}_loaded{s}_{k * WQ // KT}"), loads)
                                for q in range(2):
                                    c0 = 512 * hf + 256 * q
                                    ins = pe.matmul(bank[bk][BS * q:BS * q + BS, 0:256], xT[:, k, :],
                                                    wt[:, k, c0:c0 + 256], start=(k == 0), stop=(k == KT - 1))
                            ins.then_inc(sem(f"{done}{hf}"), 1)

                        def turn(hf):
                            pe.wait_ge(sem(f"usb_ready{hf}"), b1)
                            settle(pe, "pe")
                            for c0, src in ((0, gsb), (256, usb)):
                                o3 = bank[4 + hf][:, c0:c0 + 256].rearrange("p (q c s) -> p c q s", q=2, c=2)
                                for cc in range(2):
                                    ins = pe.transpose(o3[:, cc], src[:, hf, cc * P:(cc + 1) * P], ident)
                            ins.then_inc(sem(f"turned{hf}"), 1)

                        pe.wait_ge(sem("xTb_ready"), b1)
                        product(0, 0, GATE[s], "gate_done", "gate")
                        product(2, 0, UP[s], "up_done", "up")
                        product(1, 1, GATE[s], "gate_done", "gate")
                        turn(0)
                        product(3, 1, UP[s], "up_done", "up")
                        pe.wait_ge(sem("gathered"), b1 * 16 + 16)
                        rows_in()
                        turn(1)
                        for hf in range(2):
                            pe.wait_ge(sem(f"aT_ready{hf}"), b1)
                            for k in range(4 * hf, 4 * hf + 4):
                                if k % (KT // WQ) == 0:
                                    pe.wait_ge(sem(f"down_loaded0_{k * WQ // KT}"), dloads)
                                for q in range(2):
                                    ins = pe.matmul(bank[6][BS * q:BS * q + BS, :], aT[:, k, :],
                                                    DOWN[:, k, 512 * q:512 * q + 512], start=(k == 0),
                                                    stop=(k == KT - 1))
                        ins.then_inc(sem("down_done"), 1)

        @block.vector
        def _(dve):
            chain = [0]

            def link(ins):
                chain[0] += 1
                ins.then_inc(sem("dve_step"), 1)
                dve.wait_ge(sem("dve_step"), chain[0])

            def own(ins, name, n):
                ins.then_inc(sem(name), 1)
                dve.wait_ge(sem(name), n)

            tt, ts, stt = dve.tensor_tensor, dve.tensor_scalar, dve.scalar_tensor_tensor

            dve.wait_ge(sem("rowsT"), 1)
            dve.tensor_copy(cols[:, :], bank[7][:, 0:72]).then_inc(sem("cols_ready"), 1)
            dve.wait_ge(sem("cols_ready"), 1)
            dve.wait_ge(sem("exp_c"), 1)
            link(ts(silu[:, :], silu[:, :], 1.0, None, ALU.add))
            link(dve.reciprocal(silu[:, :], silu[:, :]))
            link(tt(silu[:, :], silu[:, :], cols[:, 0:8], ALU.mult))
            dve.tensor_copy(silu32[:, :].rearrange("p (k r) -> p k r", k=KT),
                            silu[:, :].unsqueeze(2).to_broadcast([P, KT, 32])).then_inc(sem("silu_ready"), 1)
            dve.wait_ge(sem("n1_ssq"), NT)
            ts(sm[:, 8:12], sm[:, 4:8], 1.0 / D, EPS, ALU.mult, ALU.add).then_inc(sem("n1_ms"), 1)
            dve.wait_ge(sem("n1_sd"), 1)
            link(dve.reciprocal(sm[:, 12:16], sm[:, 12:16]))
            for t in range(NT):
                ts(xt[:, t, :], xt[:, t, :], sm[:, 12 + t:13 + t], None, ALU.mult).then_inc(sem("xhat_ready"), 1)

            def mod_evac(j):
                n = order.index(j)
                dve.wait_ge(sem("mod_cols"), n + 1)
                dst = mod[:, 8 * j:8 * j + 8].rearrange("p (q c) -> p q c", c=2)
                src = bank[6][:, 0:256].rearrange("p (c q r) -> p q c r", c=2, q=4)[:, :, :, 0]
                bias = cols[:, 24 + 8 * j:32 + 8 * j].rearrange("p (q c) -> p q c", c=2)
                own(tt(dst, src, bias, ALU.add), "mod_read", n + 1)

            mod_evac(1)
            mod_evac(0)
            dve.wait_ge(sem("small_loaded"), 16 * 10)
            for j in range(2):
                dve.tensor_tensor_reduce(lamb[:, 128 * j:128 * j + 64], lamb[:, 128 * j:128 * j + 64],
                                         lamb[:, 128 * j + 64:128 * j + 128], 1.0, 0.0, ALU.mult, ALU.add,
                                         sm[:, j:j + 1]).then_inc(sem("lam_dot"), 1)
            dve.wait_ge(sem("lam_exp"), 1)
            link(tt(sm[:, 34:35], sm[:, 3:4], sm[:, 2:3], ALU.subtract))
            link(ts(sm[:, 34:35], sm[:, 34:35], -LAM0, None, ALU.add))
            link(ts(gains[:, 384:512], gains[:, 384:512], 1.0 - LAM0, None, ALU.mult))
            stt(amp[:, 0:8], mod[:, 8:16], 1.0, cols[:, 8:16], ALU.add, ALU.mult).then_inc(sem("amp1_ready"), 1)
            dve.wait_ge(sem("amp1_ready"), 1)
            for k in range(1, KT, 2):
                dve.wait_ge(sem("xT_done"), k + 1)
                ts(hT[:, k, :], bank[k % 4][:, :], amp[:, k:k + 1], mod[:, k:k + 1], ALU.mult, ALU.add) \
                    .then_inc(sem("hT_dve"), 1)

            def rope(tmp, t, nh, n):
                heads = tmp.rearrange("p (h q) -> p h q", q=HD)
                xr = heads[:, :, 0:16]
                cs = CT[:, C_COS + 16 * t:C_COS + 16 * t + 16].unsqueeze(1).to_broadcast([P, nh, 16])
                sn = CT[:, C_SIN + 16 * t:C_SIN + 16 * t + 16].unsqueeze(1).to_broadcast([P, nh, 16])
                ta = RT[:, 0:128].rearrange("p (h q) -> p h q", q=16)[:, 0:nh, :]
                tb = RT[:, 128:256].rearrange("p (h q) -> p h q", q=16)[:, 0:nh, :]
                tt(ta, xr, cs, ALU.mult)
                link(tt(tb, xr, sn, ALU.mult))
                tt(heads[:, :, 0:8], ta[:, :, 0:8], tb[:, :, 8:16], ALU.subtract)
                own(tt(heads[:, :, 8:16], ta[:, :, 8:16], tb[:, :, 0:8], ALU.add), "heads_ready", n + 1)


            dve.wait_ge(sem("const_loaded"), 16)
            for n, (ch, t) in enumerate(steps[:NTR]):
                dve.wait_ge(sem("proj_evac"), n + 1)
                tmp = TMP[:, n % 3]
                if ch == IQc:
                    rope(tmp, t, 8, n)
                    continue
                nh = 2 if ch == MISC else 8
                hv = tmp[:, 0:nh * HD].rearrange("p (h q) -> p h q", q=HD)
                sq = SQ[:, 0:nh * HD].rearrange("p (h q) -> p h q", q=HD)
                link(tt(sq, hv, hv, ALU.mult))
                if ch == MISC:
                    link(tt(SQ[:, 128:256], tmp[:, 256:384], tmp[:, 256:384], ALU.mult))
                    link(dve.memset(sm[:, 16:24], 64.0))
                    link(dve.tensor_reduce(sm[:, 16:18], sq, AX, ALU.add))
                    link(dve.tensor_reduce(sm[:, 18:19], SQ[:, 128:256], AX, ALU.add))
                    link(ts(sm[:, 18:19], sm[:, 18:19], 0.5, None, ALU.mult))
                    link(ts(iw[:, 8 * t:8 * t + 8], tmp[:, 384:392], 8 ** -0.5, 64 ** -0.5, ALU.mult, ALU.mult))
                else:
                    link(dve.tensor_reduce(sm[:, 16:24], sq, AX, ALU.add))
                ts(sm[:, 16:24], sm[:, 16:24], 1.0 / HD, EPS, ALU.mult, ALU.add).then_inc(sem("head_ms"), 1)
                dve.wait_ge(sem("head_sd"), nth_norm[n])
                link(dve.reciprocal(sm[:, 24:32], sm[:, 24:32]))
                link(tt(hv, hv, sm[:, 24:24 + nh].unsqueeze(2).to_broadcast([P, nh, HD]), ALU.mult))
                g = 3 if ch == MISC else GAIN[ch]
                link(tt(hv, hv, gains[:, HD * g:HD * g + HD].unsqueeze(1).to_broadcast([P, nh, HD]), ALU.mult))
                if ch == MISC:
                    link(stt(LAT[:, t, :], tmp[:, 256:384], sm[:, 26:27], gains[:, 256:384], ALU.mult, ALU.mult))
                rope(tmp[:, 0:256] if ch == MISC else tmp, t, 4 if ch == MISC else 8, n)
                if t == 3:
                    mod_evac(ch + 1)
            stt(amp[:, 8:16], mod[:, 32:40], 1.0, cols[:, 16:24], ALU.add, ALU.mult).then_inc(sem("amp2_ready"), 1)
            link(dve.memset(AM[0], 0.0))
            link(dve.memset(AM[0][0:64, 64:128], NEG))
            for n, (i, h) in enumerate(units_c):
                nk = (i + 1) * P
                dve.wait_ge(sem("rel_ready"), n + 1)
                w = iw[:, 8 * i + h:8 * i + h + 1]
                if h == 0:
                    ins = ts(AM[i], P1[:, n % 2, 0:nk], w, None, ALU.mult)
                else:
                    ins = stt(AM[i], P1[:, n % 2, 0:nk], w, AM[i], ALU.mult, ALU.add)
                ins.then_inc(sem("rel_used"), 1)
                dve.wait_ge(sem("rel_used"), n + 1)
                if h == 7:
                    link(dve.memset(AM[i][0:64, nk - 64:nk], NEG))

            def topk_round(i, r):
                link(dve.max(sm[:, 96:104], AM[i]))
                link(dve.match_replace(AM[i], sm[:, 96:104], AM[i], TAKEN))
                if r == 15:
                    link(ts(AM[i], AM[i], TAKEN, NEG, ALU.not_equal, ALU.mult))

            ND = len(units_d)
            rounds = list(ROUNDS)
            for n in range(ND + 2):
                if n < ND:
                    i, h = units_d[n]
                    nk = (i + 1) * P
                    dve.wait_ge(sem("diff_qk"), n + 1)
                    for j in range(2):
                        ps = bank[2 + 2 * (n % 2) + j]
                        link(dve.memset(ps[0:64, nk - 64:nk], NEG))
                        link(dve.tensor_reduce(sm[:, 32 + j:33 + j], ps[:, 0:nk], AX, ALU.max))
                    own(ts(sm[:, 36 + 2 * (n % 2):38 + 2 * (n % 2)], sm[:, 32:34], -SCALE, None, ALU.mult),
                        "diff_max", n + 1)
                if 1 <= n <= ND:
                    m = n - 1
                    nk = (units_d[m][0] + 1) * P
                    s0 = 40 + 2 * (m % 4)
                    dve.wait_ge(sem("diff_exp"), m + 1)
                    link(stt(sm[:, 35:36], sm[:, s0:s0 + 1], sm[:, 34:35], sm[:, s0:s0 + 1], ALU.mult, ALU.bypass))
                    link(dve.reciprocal(sm[:, s0:s0 + 2], sm[:, s0:s0 + 2]))
                    link(tt(sm[:, 35:36], sm[:, 35:36], sm[:, s0 + 1:s0 + 2], ALU.mult))
                    own(stt(P1[:, m % 2, 0:nk], P2[:, m % 2, 0:nk], sm[:, 35:36], P1[:, m % 2, 0:nk], ALU.mult,
                            ALU.add), "diff_a", m + 1)
                if n >= 2:
                    m = n - 2
                    i, h = units_d[m]
                    dve.wait_ge(sem("diff_pv"), m + 1)
                    s0 = 40 + 2 * (m % 4)
                    own(ts(MIX[:, i, h * P:(h + 1) * P], bank[7 * (m % 2)][:, 0:P], sm[:, s0:s0 + 1],
                           None, ALU.mult), "diff_out", m + 1)
                for _ in range(3):
                    if rounds:
                        topk_round(*rounds.pop(0))
            assert not rounds

            NEU = len(units_e)
            for n in range(NEU + 3):
                if n < NEU:
                    i, h = units_e[n]
                    nk = (i + 1) * P
                    dve.wait_ge(sem("sparse_qk"), n + 1)
                    if n >= 2:
                        dve.wait_ge(sem("sparse_exp"), n - 1)
                    if n == 0:
                        dve.wait_ge(sem("diff_a"), ND)
                    link(dve.tensor_tensor_reduce(P2[:, n % 2, 0:nk], bank[2 + n % 2][:, 0:nk], AM[i], 1.0,
                                                  2 * NEG, ALU.add, ALU.max, sm[:, 54:55]))
                    own(ts(sm[:, 52 + n % 2:53 + n % 2], sm[:, 54:55], -SCALE, None, ALU.mult), "sparse_max", n + 1)
                if 1 <= n <= NEU:
                    m = n - 1
                    nk = (units_e[m][0] + 1) * P
                    dve.wait_ge(sem("sparse_T"), m + 1)
                    if m >= 2:
                        dve.wait_ge(sem("sparse_oT"), m - 1)
                    own(dve.tensor_copy(AT[:, m % 2, 0:nk], bank[6 * (m % 2)][:, 0:nk]), "sparse_Te", m + 1)
                if n >= 3:
                    m = n - 3
                    i, h = units_e[m]
                    link(dve.reciprocal(sm[:, 60 + m % 4:61 + m % 4], sm[:, 56 + m % 4:57 + m % 4]))
                    dve.wait_ge(sem("sparse_out_done"), m + 1)
                    own(ts(MIX[:, i, 512 + h * HD:512 + (h + 1) * HD], bank[1 + 3 * (m % 2)][:, 0:HD],
                           sm[:, 60 + m % 4:61 + m % 4], None, ALU.mult), "sparse_out", m + 1)

            for k in range(KT):
                ins = ts(DIAG[:, k, :], ident, mod[:, 16 + k:17 + k], None, ALU.mult)
            ins.then_inc(sem("diag_ready"), 1)
            dve.wait_ge(sem("diff_out"), ND)
            for n, (i, h) in enumerate(units_d):
                a = MIX[:, i, h * P:(h + 1) * P]
                link(dve.tensor_tensor_reduce(P1[:, 0, 0:P], a, a, 1.0, 0.0, ALU.mult, ALU.add, sm[:, 64 + n:65 + n]))
            ts(sm[:, 64:80], sm[:, 64:80], 1.0 / P, EPS, ALU.mult, ALU.add).then_inc(sem("sub_ms"), 1)
            dve.wait_ge(sem("sub_sd"), 1)
            link(dve.reciprocal(sm[:, 80:96], sm[:, 80:96]))
            for n, (i, h) in enumerate(units_d):
                a = MIX[:, i, h * P:(h + 1) * P]
                ins = stt(a, a, sm[:, 80 + n:81 + n], gains[:, 384:512], ALU.mult, ALU.mult)
            own(ins, "mix_ready", 1)
            for k in range(1, KT, 2):
                dve.wait_ge(sem("mixT_done"), k + 1)
                dve.tensor_copy(mixT[:, k, :], bank[k % 4][:, :]).then_inc(sem("mixT_dve"), 1)
            dve.wait_ge(sem("x_again"), 16)
            dve.wait_ge(sem("g1b_ready"), 2)
            for t in range(NT):
                for hf in range(2):
                    n = 2 * t + hf
                    cs = slice(hf * 512, hf * 512 + 512)
                    dve.wait_ge(sem("wout_done"), n + 1)
                    tt(s4[:, 6144 + hf * 512:6656 + hf * 512], bank[n % 4][:, :], G1B[:, cs], ALU.mult) \
                        .then_inc(sem("mix_added"), 1)
                    dve.wait_ge(sem("mix_added"), n + 1)
                    ins = tt(x2[:, t, cs], x2[:, t, cs], s4[:, 6144 + hf * 512:6656 + hf * 512], ALU.add)
                own(ins, "x2_ready", t + 1)
                dve.wait_ge(sem("n2_ssq"), t + 1)
                ts(sm[:, 8 + t:9 + t], sm[:, 4 + t:5 + t], 1.0 / D, EPS, ALU.mult, ALU.add).then_inc(sem("n2_ms"), 1)
                dve.wait_ge(sem("n2_sd"), t + 1)
                link(dve.reciprocal(sm[:, 12 + t:13 + t], sm[:, 12 + t:13 + t]))
                ts(XH2[:, t, :], x2[:, t, :], sm[:, 12 + t:13 + t], None, ALU.mult).then_inc(sem("xhat2_ready"), 1)
            for k in range(1, KT, 2):
                dve.wait_ge(sem("xT2_done"), k + 1)
                ts(h2T[:, k, :], bank[k % 4][:, :], amp[:, 8 + k:9 + k], mod[:, 24 + k:25 + k], ALU.mult, ALU.add) \
                    .then_inc(sem("h2T_dve"), 1)
            dve.wait_ge(sem("brow_T"), 1)
            for m in range(2):
                ins = dve.tensor_copy(biasT[:, m * 256:(m + 1) * 256], bank[5 + m][:, 0:256])
            ins.then_inc(sem("biasT_done"), 1)

            lg = X[:, 0:128]
            top = X[:, 128:160]
            topi = X[:, 160:192].bitcast(U32)
            topf = X[:, 192:224]
            OH = [X[:, 256 + 128 * k:384 + 128 * k] for k in range(TOPK)]
            fl = X[:, 768:896]
            sl = X[:, 896:1024]
            rk = X[:, 1024:1152]
            pr_ = X[:, 1152:1280]
            sel = X[:, 1280:1312]
            nb = X[:, 1312:1344]
            cumf = X[:, 1344:1377]
            one32 = ones[:, 0:NE]
            mask = route[:, 0:128]
            gs = route[:, 512:528]
            ge = route[:, 528:544]
            gsum = route[:, 544:548]
            t3 = lambda a: a.rearrange("p (t e) -> p t e", t=NT)
            dve.wait_ge(sem("router_done"), 1)
            dve.tensor_copy(lgT, bank[4][:, 0:P]).then_inc(sem("logits_sb"), 1)
            dve.wait_ge(sem("logits_T"), 1)
            link(tt(t3(lg), t3(bank[0][:, 0:128]), rb[:, :].unsqueeze(1).to_broadcast([P, NT, NE]), ALU.add))
            for t in range(NT):
                link(dve.max(top[:, 8 * t:8 * t + 8], lg[:, NE * t:NE * t + NE]))
                link(dve.max_index(topi[:, 8 * t:8 * t + 8], top[:, 8 * t:8 * t + 8], lg[:, NE * t:NE * t + NE]))
            link(dve.tensor_copy(topf, topi))
            top3, topf3 = t3(top), t3(topf)
            for k in range(TOPK):
                link(tt(t3(OH[k]), iota[:, 0:NE].unsqueeze(1).to_broadcast([P, NT, NE]),
                        topf3[:, :, k:k + 1].to_broadcast([P, NT, NE]), ALU.is_equal))
            link(tt(mask, OH[0], OH[1], ALU.add))
            link(tt(mask, mask, OH[2], ALU.add))
            tt(mask, mask, OH[3], ALU.add).then_inc(sem("mask_ready"), 1)
            tt(t3(gs), top3[:, :, 0:TOPK], top3[:, :, 0:1].to_broadcast([P, NT, TOPK]), ALU.subtract) \
                .then_inc(sem("gate_sub"), 1)
            dve.wait_ge(sem("gate_exp"), 1)
            link(dve.tensor_reduce(gsum, t3(ge), AX, ALU.add))
            link(dve.reciprocal(gsum, gsum))
            link(tt(t3(ge), t3(ge), gsum.unsqueeze(2).to_broadcast([P, NT, TOPK]), ALU.mult))
            dve.wait_ge(sem("rank_done"), 1)
            link(dve.tensor_copy(rk, bank[0][:, 0:128]))
            link(ts(nb, bank[0][:, 128:160], float(BS), 1.0, ALU.is_gt, ALU.add))
            for j in range(2, T // BS):
                link(stt(nb, bank[0][:, 128:160], float(BS * j), nb, ALU.is_gt, ALU.add))
            link(dve.memset(cumf[:, 0:1], 0.0))
            link(dve.tensor_tensor_scan(cumf[:, 1:33], one32, nb, 0.0, ALU.mult, ALU.add))
            dve.tensor_copy(cum[:, :], cumf).then_inc(sem("cum_ready"), 1)
            link(ts(fl, rk, float(BS), None, ALU.is_ge))
            for j in range(2, T // BS):
                link(stt(fl, rk, float(BS * j), fl, ALU.is_ge, ALU.add))
            link(stt(sl, fl, -float(BS), rk, ALU.mult, ALU.add))
            link(tt(t3(fl), t3(fl), cumf[:, 0:NE].unsqueeze(1).to_broadcast([P, NT, NE]), ALU.add))
            for k in range(TOPK):
                for q, src in enumerate((fl, sl)):
                    link(tt(pr_, OH[k], src, ALU.mult))
                    link(dve.tensor_reduce(sel[:, 16 * q:16 * q + 16].rearrange("p (t k) -> p t k", k=TOPK)[:, :, k],
                                           t3(pr_), AX, ALU.add))
            g3 = lambda n: [P, 16, n]
            link(tt(LH, iota.unsqueeze(1).to_broadcast(g3(P)), sel[:, 16:32].unsqueeze(2).to_broadcast(g3(P)),
                    ALU.is_equal))
            link(tt(OB, iota[:, 0:64].unsqueeze(1).to_broadcast(g3(64)), sel[:, 0:16].unsqueeze(2).to_broadcast(g3(64)),
                    ALU.is_equal))
            link(tt(RH[:, :, 0:64], OB, ge.unsqueeze(2).to_broadcast(g3(64)), ALU.mult))
            link(ts(pr_[:, 0:NT], CT[:, C_TOK:C_TOK + NT], -float(T), None, ALU.add))
            link(dve.tensor_copy(sl[:, 0:16].rearrange("p (t k) -> p t k", k=TOPK),
                                 pr_[:, 0:NT].unsqueeze(2).to_broadcast([P, NT, TOPK])))
            own(tt(RH[:, :, 64:128], OB, sl[:, 0:16].unsqueeze(2).to_broadcast(g3(64)), ALU.mult), "onehot_ready", 1)
            for k in range(TOPK):
                w = t3(ge)[:, :, k:k + 1].to_broadcast([P, NT, NE])
                link(tt(t3(OH[k]), t3(OH[k]), w, ALU.mult))
            link(tt(gmat, OH[0], OH[1], ALU.add))
            link(tt(gmat, gmat, OH[2], ALU.add))
            own(tt(gmat, gmat, OH[3], ALU.add), "gate_mat", 1)
            dve.wait_ge(sem("tables_done"), 1)
            tk = bank[1][:, 64:128]
            emp = tab[:, 64:128]
            link(dve.tensor_copy(tab[:, 0:64], bank[1][:, 0:64]))
            link(ts(emp, tk, 0.0, None, ALU.is_equal))
            link(ts(tf, tk, 2.0, 2.0 * T, ALU.mult, ALU.add))
            link(ts(tf, tf, CT[:, C_HALF:C_HALF + 1], None, ALU.add))
            link(stt(tf2, emp, -2.0 * T, tf, ALU.mult, ALU.add))
            dve.tensor_copy(tabi[:, 0:64], tf2)
            dve.tensor_copy(tabi[:, 64:65], CT[:, C_HALF:C_HALF + 1])
            link(ts(emp, emp, CT[:, C_HALF + 1:C_HALF + 2], -2.0 * T, ALU.mult, ALU.add))
            link(ts(emp, emp, 0.0, None, ALU.max))
            link(tt(tf, tf, emp, ALU.add))
            dve.tensor_copy(tabi[:, 65:129], tf).then_inc(sem("tabi_ready"), 1)

            for k in range(KT):
                ins = ts(DIAG[:, k, :], ident, mod[:, 40 + k:41 + k], None, ALU.mult)
            ins.then_inc(sem("diag2_ready"), 1)
            dve.wait_ge(sem("gate_T"), 1)
            dve.tensor_copy(GT, bank[2][0:NE, :]).then_inc(sem("gate_Te"), 1)
            dve.wait_ge(sem("g2b_done"), 1)
            for j in range(2):
                link(dve.tensor_copy(G2B[:, j * 512:(j + 1) * 512], bank[3 + j][:, :]))

            def scale_shift(n):
                q = [P, KT, BS]
                ps = bank[7][:, :].rearrange("p (k s) -> p k s", k=KT)
                ins = tt(xT, ps, amp[:, 8:16].unsqueeze(2).to_broadcast(q), ALU.mult)
                ins.then_inc(sem("xT_scaled"), 1)
                dve.wait_ge(sem("xT_scaled"), n)
                tt(xT, xT, mod[:, 24:32].unsqueeze(2).to_broadcast(q), ALU.add).then_inc(sem("xTb_ready"), 1)

            for n in range(2 * NT):
                t, hf = n // 2, n % 2
                cs = slice(hf * 512, hf * 512 + 512)
                dve.wait_ge(sem("bias_done"), n + 1)
                own(tt(s4[:, 6656:7168], bank[5 + hf][:, :], G2B[:, cs], ALU.mult), "bias_added", n + 1)
                ins = tt(x2[:, t, cs], x2[:, t, cs], s4[:, 6656:7168], ALU.add)
                if hf:
                    own(ins, "start_ready", t + 1)
                else:
                    link(ins)
            dve.wait_ge(sem("xg_used"), 1)
            scale_shift(1)
            dve.wait_ge(sem("start_stored"), 16 * NT)
            dve.wait_ge(sem("scattered"), 16)
            dve.tensor_copy(G2H[0:64, :], G2B[0:64, 0:512])
            link(dve.tensor_copy(G2H[64:128, :], G2B[64:128, 512:1024]))
            dve.sem_inc(sem("g2_copied"), 1)
            dve.wait_ge(sem("cum_ready"), 1)

            def half_act(hf, e, b1, h1):
                hs = slice(4 * hf, 4 * hf + 4)
                q = [P, 4, BS]
                gp = bank[4 + hf][:, 0:256].rearrange("p (m s) -> p m s", m=4)
                up = bank[4 + hf][:, 256:512].rearrange("p (m s) -> p m s", m=4)

                def after(ins, name):
                    ins.then_inc(sem(name), 1)
                    dve.wait_ge(sem(name), h1)

                dve.wait_ge(sem(f"gate_done{hf}"), b1)
                dve.tensor_copy(gsb[:, hf, :], bank[hf][:, 0:256])
                dve.wait_ge(sem(f"up_done{hf}"), b1)
                dve.tensor_copy(usb[:, hf, :], bank[2 + hf][:, 0:256]).then_inc(sem(f"usb_ready{hf}"), 1)
                dve.wait_ge(sem(f"turned{hf}"), b1)
                after(tt(gc[:, hs, :], gp, bgT[:, hs, bass.ds(e, 1)].to_broadcast(q), ALU.add), "gbias")
                after(ts(gc[:, hs, :], gc[:, hs, :], LIMIT, None, ALU.min), "gclip")
                after(tt(uc[:, hs, :], up, buT[:, hs, bass.ds(e, 1)].to_broadcast(q), ALU.add), "ubias")
                after(ts(uc[:, hs, :], uc[:, hs, :], -LIMIT, LIMIT, ALU.max, ALU.min), "uclip")
                after(stt(uc[:, hs, :], uc[:, hs, :], 1.0, gc[:, hs, :], ALU.add, ALU.mult), "ug")
                dve.wait_ge(sem("sig_ready"), h1)
                tt(aT[:, hs, :], uc[:, hs, :], sg[:, hs, :], ALU.mult).then_inc(sem(f"aT_ready{hf}"), 1)

            with dve.Fori(0, NE) as e:
                first = dve.value_load(cum[0:1, bass.ds(e, 1)], min_val=0, max_val=MAXB - 1)
                end = dve.value_load(cum[0:1, bass.ds(e + 1, 1)], min_val=1, max_val=MAXB - 1)
                with dve.Fori(first, end) as b:
                    b1 = dve.snap(b + 1)
                    half_act(0, e, b1, dve.snap(b * 2 + 1))
                    half_act(1, e, b1, dve.snap(b * 2 + 2))
                    dve.wait_ge(sem("xg_used"), b1 + 1)
                    scale_shift(b1 + 1)
                    dve.wait_ge(sem("down_done"), b1)
                    dve.wait_ge(sem("scattered"), b1 * 16)
                    stt(ysb, bank[6][:, :], tab[:, bass.ds(b, 1)], G2H[:, :], ALU.mult, ALU.mult) \
                        .then_inc(sem("ysb_ready"), 1)


_ARGS = ["x", "c", "norm1_g", "norm2_g", "w_ada", "b_ada", "w_in", "w_out", "a_q_norm_g", "a_k_norm_g", "a_lambda",
         "a_sub_g", "b_q_norm_g", "b_k_norm_g", "b_kv_norm_g", "b_w_uv", "router_w", "router_b", "w_gate", "b_gate",
         "w_up", "b_up", "w_down", "b_down"]
_SQUEEZE = {"x", "w_ada", "w_in", "w_out", "b_w_uv", "router_w", "w_gate", "b_gate", "w_up", "b_up", "w_down",
            "b_down"}


def kernel(**inputs):
    import concourse.bacc as bacc
    from concourse.bass_utils import run_bass_kernel_spmd

    nc = bacc.Bacc("TRN2", target_bir_lowering=False, num_devices=1)
    arrays, args = {}, []
    for name in ["consts"] + _ARGS:
        a = constants() if name == "consts" else np.ascontiguousarray(inputs[name])
        if name in _SQUEEZE:
            a = a.reshape(a.shape[1:])
        arrays[name] = a
        args.append(nc.dram_tensor(name, a.shape, mybir.dt.from_np(a.dtype), kind="ExternalInput").ap())
    out = nc.dram_tensor("out", (T, D), F32, kind="ExternalOutput").ap()
    build(nc, *args, out)
    r = run_bass_kernel_spmd(nc, [arrays], core_ids=[0])
    return np.asarray(r.results[0]["out"]).reshape(1, T, D)
```

```python
import math
from contextlib import ExitStack

import concourse.bass as bass
import numpy as np
from concourse import mybir

F32 = mybir.dt.float32
I32 = mybir.dt.int32
U32 = mybir.dt.uint32
ALU = mybir.AluOpType
ACT = mybir.ActivationFunctionType
AX = mybir.AxisListType.X

P = 128
T = 512
NT = T // P
D = 1024
KT = D // P
HD = 64
NE = 32
TOPK = 4
BS = 64
AHEAD = 3
WQ = 4
MAXB = 64
LIMIT = 7.0
ALPHA = 1.702
NEG = -1.0e30
TAKEN = -3.0e38
EPS = 1e-6
LAM0 = 0.8 - 0.6 * math.exp(-0.3 * 0)
SCALE = HD ** -0.5

C_ID, C_TRI, C_ONE, C_IOTA = 0, 128, 256, 384
C_COS, C_SIN, C_TOK, C_HALF = 512, 576, 640, 644
C_ALL = 646


def constants():
    c = np.zeros((P, C_ALL), np.float32)
    c[:, C_ID:C_ID + P] = np.eye(P)
    c[:, C_TRI:C_TRI + P] = np.triu(np.ones((P, P)), 1)
    c[:, C_ONE:C_ONE + P] = 1
    c[:, C_IOTA:C_IOTA + P] = np.arange(P) % BS
    pos = np.arange(T, dtype=np.float32)
    rot = HD // 4
    inv = np.float32(500000.0) ** (-np.arange(0, rot, 2, dtype=np.float32) / np.float32(rot))
    ang = pos[:, None] * inv.astype(np.float32)[None, :]
    for base, f in ((C_COS, np.cos), (C_SIN, np.sin)):
        tab = f(ang).astype(np.float32).reshape(NT, P, rot // 2)
        for t in range(NT):
            c[:, base + 16 * t:base + 16 * t + 16] = np.concatenate([tab[t], tab[t]], axis=1)
    for t in range(NT):
        c[:, C_TOK + t] = t * P + np.arange(P)
    half = np.arange(P) // BS
    c[:, C_HALF] = half
    c[:, C_HALF + 1] = 2 * T + np.arange(P) - half
    return c


def build(nc, consts, x, c, norm1_g, norm2_g, w_ada, b_ada, w_in, w_out, a_q_norm_g, a_k_norm_g, a_lambda,
          a_sub_g, b_q_norm_g, b_k_norm_g, b_kv_norm_g, b_w_uv, router_w, router_b, w_gate, b_gate, w_up,
          b_up, w_down, b_down, out):
    with ExitStack() as ctx:
        sems = {}

        def sem(name):
            if name not in sems:
                sems[name] = ctx.enter_context(nc.semaphore(name))
            return sems[name]

        def sb(name, cols, dt=F32):
            return ctx.enter_context(nc.sbuf_tensor(name, [P, cols], dt))

        xhat_dram = nc.dram_tensor("xhat_scratch", (2 * T, D // 2), F32, kind="Internal").ap()
        acc_dram = nc.dram_tensor("acc_scratch", (2 * T + P, D // 2), F32, kind="Internal").ap()

        W = sb("W", 5 * 8192)
        X = sb("X", 4096)
        H = sb("H", 4096)
        CT = sb("CT", C_ALL)
        slot = [W[:, i * 8192:(i + 1) * 8192].rearrange("p (k n) -> p k n", k=KT) for i in range(5)]
        GATE, UP, DOWN = (slot[0], slot[1]), (slot[3], slot[4]), slot[2]
        ident = CT[:, C_ID:C_ID + P]
        tri = CT[:, C_TRI:C_TRI + P]
        ones = CT[:, C_ONE:C_ONE + P]
        iota = CT[:, C_IOTA:C_IOTA + P]

        gains = sb("gains", 4 * HD + 2 * P)
        cols = sb("cols", 72)
        mod = sb("mod", 48)
        silu = sb("silu", 8)
        amp = sb("amp", 16)
        sm = sb("sm", 128)
        iw = sb("iw", NT * 8)
        uv = sb("uv", 8 * HD)
        rw = sb("rw", KT * NE)
        rb = sb("rb", NE)
        route = sb("route", 4 * 128 + 5 * 16 + 3 * 32)
        tab = sb("tab", 2 * MAXB)
        tabi = sb("tabi", 2 * MAXB + AHEAD - 1, U32)
        cum = sb("cum", NE + 1, I32)
        gidx = sb("gidx", 2, U32)
        biasT = sb("biasT", 2 * KT * NE)

        A0 = 3 * 8192
        QKT = W[:, A0:A0 + 20 * 512].rearrange("p (h t) -> p h t", h=20)
        AQ, BQ, IQ, BK, IK, AK1 = 0, 4, 8, 12, 14, 16
        o = A0 + 20 * 512
        V = W[:, o:o + 2048].rearrange("p (t n) -> p t n", t=NT)
        LAT = W[:, o + 2048:o + 2560].rearrange("p (t n) -> p t n", t=NT)
        P1 = W[:, o + 2560:o + 3584].rearrange("p (b n) -> p b n", b=2)
        P2 = W[:, o + 3584:o + 4608].rearrange("p (b n) -> p b n", b=2)
        TMP = W[:, o + 2560:o + 4096].rearrange("p (b n) -> p b n", b=3)
        SQ = W[:, o + 4096:o + 4608]
        OT = W[:, o + 4608:o + 4864].rearrange("p (b n) -> p b n", b=2)
        amo = [o + 4864, o + 4992, o + 5248, o + 5632]
        AM = [W[:, amo[i]:amo[i] + (i + 1) * P] for i in range(NT)]
        RT = SQ
        AK2 = X[:, 2048:4096].rearrange("p (h t) -> p h t", h=4)
        REL = X[:, 0:1024].rearrange("p (b n) -> p b n", b=2)
        mixT = X[:, 0:2048].rearrange("p (b k t) -> p b k t", b=2, k=KT)
        MIX = H[:, 0:2048].rearrange("p (b d) -> p b d", b=2)
        AT = H[:, 2048:3072].rearrange("p (b n) -> p b n", b=2)

        WIN = W[:, 2 * 8192:3 * 8192].rearrange("p (b k n) -> p b k n", b=2, k=KT)
        hT = H[:, :].rearrange("p (k t) -> p k t", k=KT)
        xt = X[:, :].rearrange("p (t d) -> p t d", t=NT)
        x2 = W[:, 8192:12288].rearrange("p (t d) -> p t d", t=NT)
        XH2 = W[:, 12288:16384].rearrange("p (t d) -> p t d", t=NT)
        h2T = W[:, 0:4096].rearrange("p (k t) -> p k t", k=KT)
        G1B = W[:, 4096:5120]
        DIAG = W[:, 5120:6144].rearrange("p (k n) -> p k n", k=KT)
        SQ2 = W[:, 6144:7168]
        WTMP = W[:, 7168:7680]
        s4 = slot[4].rearrange("p k n -> p (k n)")
        DIAG2 = s4[:, 1024:2048].rearrange("p (k n) -> p k n", k=KT)
        BROW = s4[0:NE, 2048:5120].rearrange("p (m n) -> p m n", m=3)
        GT = s4[0:NE, 5120:5632]
        G2B = s4[:, 5632:6656]
        LH = X[:, 1408:3456].rearrange("p (j s) -> p j s", j=16)
        RH = H[:, 1024:3072].rearrange("p (j s) -> p j s", j=16)
        OB = H[:, 3072:4096].rearrange("p (j s) -> p j s", j=16)

        rows = H[0:72, 0:P]
        lamb = H[:, 1024:1280]

        xg = X[:, 0:512]
        xgc = H[:, 1024:1536]
        ysb = X[:, 512:1024]
        yv = H[:, 1536:2048]
        xT = X[:, 1024:1536].rearrange("p (k s) -> p k s", k=KT)
        gsb = X[:, 1536:2048].rearrange("p (h n) -> p h n", h=2)
        usb = X[:, 2048:2560].rearrange("p (h n) -> p h n", h=2)
        gc = X[:, 2560:3072].rearrange("p (k s) -> p k s", k=KT)
        uc = X[:, 3072:3584].rearrange("p (k s) -> p k s", k=KT)
        sg = X[:, 3584:4096].rearrange("p (k s) -> p k s", k=KT)
        aT = H[:, 0:512].rearrange("p (k s) -> p k s", k=KT)
        bgT, buT = [biasT[:, m * KT * NE:(m + 1) * KT * NE].rearrange("p (k e) -> p k e", k=KT) for m in range(2)]

        lgT = X[:, 1152:1280]
        gmat = X[:, 3584:3712]
        tf, tf2 = X[:, 3456:3520], X[:, 3520:3584]
        G2H = H[:, 512:1024]
        silu32 = biasT[:, 0:256]
        MR = biasT[:, 256:512]

        psum = ctx.enter_context(nc.psum_tensor("psum", [P, 8 * 512], F32))
        bank = [psum[:, i * 512:(i + 1) * 512] for i in range(8)]

        def settle(eng, name):
            eng.sem_inc(sem(name + "_settled"), 1)

        IQc, MISC, BQc, AQc, AKc, AVc = range(6)
        CSRC = {IQc: 2240, BQc: 1536, AQc: 0, AKc: 512, AVc: 1024}
        PAIR0 = {IQc: IQ, BQc: BQ, AQc: AQ}
        GAIN = {BQc: 2, AQc: 0, AKc: 1}
        steps = [(ch, t) for ch in range(6) for t in range(NT)]
        NST = len(steps)
        NTR = 5 * NT
        normed = [ch in (MISC, BQc, AQc, AKc) for ch, _ in steps]
        nth_norm = [sum(normed[:n + 1]) for n in range(NST)]

        order = [1, 0, 2, 3, 4, 5]
        units_c = [(i, h) for i in range(1, NT) for h in range(8)]
        C_STEP = {n: range(4 * (n - 10), 4 * (n - 10) + 4) for n in range(10, 16)}
        units = [(kind, i, h) for i in range(NT) for kind, nh in (("diff", 4), ("sparse", 8)) for h in range(nh)]
        NU = len(units)
        ND, NS = 4 * NT, 8 * NT
        JOB0 = lambda i: 12 * (i + 1) + 3
        NSTEP = JOB0(NT - 1) + 12

        def unit(n, kind):
            if 0 <= n < NU and units[n][0] == kind:
                _, i, h = units[n]
                return (i, h, (4 if kind == "diff" else 8) * i + h)
            return None

        def job(n):
            i = (n - 3) // 12 - 1
            return (i, n - JOB0(i)) if 0 <= i < NT else None

        block = ctx.enter_context(nc.Block())

        @block.sync
        def _(sp):
            def ada(j, s):
                sp.dma_start(slot[s], w_ada[:, j * D:(j + 1) * D].rearrange("(k p) n -> p k n", p=P)) \
                    .then_inc(sem(f"ada_loaded{s}"), 16)

            def win(ch):
                buf = WIN[:, ch % 2]
                if ch >= 2:
                    sp.wait_ge(sem("proj_done"), 4 * (ch - 1))
                if ch == MISC:
                    sp.dma_start(buf[:, :, 0:192], w_in[:, 2048:2240].rearrange("(k p) n -> p k n", p=P)) \
                        .then_inc(sem("win_loaded1"), 16)
                    sp.dma_start(buf[:, :, 192:264], w_in[:, 2752:2824].rearrange("(k p) n -> p k n", p=P)) \
                        .then_inc(sem("win_loaded_misc"), 16)
                else:
                    sp.dma_start(buf, w_in[:, CSRC[ch]:CSRC[ch] + 512].rearrange("(k p) n -> p k n", p=P)) \
                        .then_inc(sem(f"win_loaded{ch % 2}"), 16)

            sp.dma_start(CT[:, :], consts).then_inc(sem("const_loaded"), 16)
            for i, (src, n) in enumerate(((c, 8), (norm1_g, 8), (norm2_g, 8), (b_ada, 48))):
                sp.dma_start(H[8 * i:8 * i + n, 0:P], src.rearrange("a (r q) -> (a r) q", q=P)) \
                    .then_inc(sem("rows_loaded"), 16)
            for t in range(NT):
                sp.dma_start(xt[:, t, :], x[t * P:(t + 1) * P, :]).then_inc(sem(f"x_loaded{t}"), 16)
            ada(1, 1)
            ada(0, 0)
            win(0)
            win(1)
            for j, s in ((2, 0), (3, 1), (4, 0), (5, 1)):
                sp.wait_ge(sem("mod_done"), max(2, j - 1))
                ada(j, s)
                win(j)
            sp.wait_ge(sem("proj_done"), NST)
            sp.wait_ge(sem("mod_done"), 6)
            sp.dma_start(x2, x.rearrange("(t p) d -> p t d", p=P)).then_inc(sem("x_again"), 16)
            sp.dma_start(slot[2], w_out.rearrange("(k p) n -> p k n", p=P)).then_inc(sem("wout_loaded"), 16)
            e_src = {"gate": w_gate, "up": w_up, "down": w_down}

            def expert(kind, e, dst, s, parts=range(WQ)):
                for q in parts:
                    ks = slice(q * KT // WQ, (q + 1) * KT // WQ)
                    src = e_src[kind][bass.ds(e, 1), q * D // WQ:(q + 1) * D // WQ, :]
                    sp.dma_start(dst[:, ks, :], src.rearrange("e (k p) n -> p (e k) n", p=P)) \
                        .then_inc(sem(f"{kind}_loaded{s}_{q}"), 16)

            for t in range(NT):
                sp.wait_ge(sem("xhat2_ready"), t + 1)
                sp.dma_start(xhat_dram[2 * t * P:2 * (t + 1) * P, :].rearrange("(p h) d -> p (h d)", h=2),
                             XH2[:, t, :]).then_inc(sem("xhat_stored"), 16)
                if t == NT - 2:
                    sp.wait_ge(sem("sparse_out"), NS)
                    sp.dma_start(BROW[:, 0, :], b_gate).then_inc(sem("brow_loaded"), 16)
                    sp.dma_start(BROW[:, 1, :], b_up).then_inc(sem("brow_loaded"), 16)
                    sp.dma_start(BROW[:, 2, :], b_down).then_inc(sem("brow_loaded"), 16)
                    sp.wait_ge(sem("wout_done"), 2 * NT)
                    expert("down", 0, DOWN, 0)
            sp.wait_ge(sem("router_done"), 1)
            expert("gate", 0, GATE[0], 0)
            expert("up", 0, UP[0], 0)
            for t in range(NT):
                sp.wait_ge(sem("start_ready"), t + 1)
                sp.dma_start(acc_dram[2 * t * P:2 * (t + 1) * P, :].rearrange("(p h) d -> p (h d)", h=2),
                             x2[:, t, :]).then_inc(sem("start_stored"), 16)
            sp.wait_ge(sem("xhat_stored"), 16 * NT)
            sp.wait_ge(sem("start_stored"), 16 * NT)
            sp.wait_ge(sem("spare_stored"), 1)
            expert("gate", 1, GATE[1], 1)
            sp.wait_ge(sem("biasT_done"), 1)
            sp.wait_ge(sem("g2_copied"), 1)
            expert("up", 1, UP[1], 1)
            sp.wait_ge(sem("cum_ready"), 1)

            def blocks_before(e):
                return sp.value_load(cum[0:1, bass.ds(e, 1)], min_val=1, max_val=MAXB - 1)

            def down_again(e, last):
                sp.wait_ge(sem("down_half"), last)
                expert("down", e, DOWN, 0, range(WQ // 2))
                sp.wait_ge(sem("down_done"), last)
                expert("down", e, DOWN, 0, range(WQ // 2, WQ))

            with sp.Fori(1, NE // 2) as pr:
                for s in range(2):
                    e = pr * 2 + s
                    last = sp.snap(blocks_before(e - 1))
                    sp.wait_ge(sem("gate_done"), last)
                    expert("gate", e, GATE[s], s)
                    down_again(e - 1, last)
                    expert("up", e, UP[s], s)
            down_again(NE - 1, sp.snap(blocks_before(NE - 1)))
            total = sp.snap(blocks_before(NE))
            sp.wait_ge(sem("scattered"), total * 16 + 16)
            settle(sp, "sp")
            for q in range(4):
                sp.dma_start(out[q * P:(q + 1) * P, :].rearrange("t (h d) -> (t h) d", h=2),
                             acc_dram[2 * q * P:2 * (q + 1) * P, :]).then_inc(sem("out_stored"), 16)
            sp.wait_ge(sem("out_stored"), 64)

        @block.gpsimd
        def _(pool):
            small = [(gains[:, 0:64], a_q_norm_g), (gains[:, 64:128], a_k_norm_g), (gains[:, 128:192], b_q_norm_g),
                     (gains[:, 192:256], b_k_norm_g), (gains[:, 256:384], b_kv_norm_g),
                     (gains[:, 384:512], a_sub_g), (rb[:, :], router_b)]
            pool.dma_start(lamb, a_lambda.rearrange("a l q -> a (l q)").to_broadcast([P, 256])) \
                .then_inc(sem("small_loaded"), 16)
            for dst, src in small:
                pool.dma_start(dst, src.to_broadcast([P, src.shape[1]])).then_inc(sem("small_loaded"), 16)
            pool.dma_start(uv[:, :].rearrange("p (h n) -> p h n", h=8), b_w_uv.rearrange("h c n -> c h n")) \
                .then_inc(sem("small_loaded"), 16)
            pool.dma_start(rw[:, :].rearrange("p (k e) -> p k e", k=KT),
                           router_w.rearrange("(k p) e -> p k e", p=P)).then_inc(sem("small_loaded"), 16)

            for tile in [BK, IK, AK1, AK1 + 2]:
                pool.memset(QKT[64:128, tile, :], 0.0)
                ins = pool.memset(QKT[0:64, tile + 1, :], 0.0)
            pool.wait_ge(sem("xT_done"), KT)
            for h in range(4):
                ins = pool.memset(AK2[64:128, h, :] if h % 2 == 0 else AK2[0:64, h, :], 0.0)
            ins.then_inc(sem("zeros_ready"), 1)

            pool.wait_ge(sem("cum_ready"), 1)
            pool.wait_ge(sem("tabi_ready"), 1)
            pool.wait_ge(sem("xhat_stored"), 16 * NT)
            total = pool.value_load(cum[0:1, NE:NE + 1], min_val=NE, max_val=MAXB - 1)

            def gather():
                settle(pool, "pool")
                pool.indirect_dma_start(out=xg, out_offset=None, in_=xhat_dram,
                                        in_offset=bass.IndirectOffsetOnAxis(ap=gidx[:, 0:1], axis=0),
                                        bounds_check=2 * T - 1, oob_is_err=True).then_inc(sem("gathered"), 16)

            pool.tensor_copy(gidx[:, 0:1], tabi[:, 0:1]).then_inc(sem("gidx_ready"), 1)
            pool.wait_ge(sem("gidx_ready"), 1)
            gather()
            pool.wait_ge(sem("start_ready"), 1)
            pool.dma_start(acc_dram[2 * T:2 * T + P, :], x2[:, 0, 0:512]).then_inc(sem("scattered"), 16)
            pool.wait_ge(sem("scattered"), 16)
            pool.sem_inc(sem("spare_stored"), 1)
            pool.sem_inc(sem("ysb_ready"), 1)
            for n in (1, 2):
                pool.wait_ge(sem("gathered"), 16 * n)
                if n == 2:
                    pool.wait_ge(sem("xg_used"), 1)
                pool.tensor_copy(xgc, xg).then_inc(sem("xg_ready"), 1)
                pool.wait_ge(sem("xg_ready"), n)
                pool.tensor_copy(gidx[:, 0:1], tabi[:, n:n + 1]).then_inc(sem("gidx_ready"), 1)
                pool.wait_ge(sem("gidx_ready"), n + 1)
                gather()
            pool.wait_ge(sem("start_stored"), 16 * NT)
            with pool.Fori(0, total) as b:
                b1 = pool.snap(b + 1)
                pool.wait_ge(sem("xg_used"), b + 2)
                pool.wait_ge(sem("gathered"), b * 16 + 48)
                settle(pool, "pool")
                pool.tensor_copy(xgc, xg).then_inc(sem("xg_ready"), 1)
                pool.tensor_copy(gidx[:, 0:1], tabi[:, bass.ds(b + AHEAD, 1)]).then_inc(sem("gidx_ready"), 1)
                pool.wait_ge(sem("xg_ready"), b + 3)
                pool.wait_ge(sem("gidx_ready"), b + 4)
                gather()
                pool.wait_ge(sem("scattered"), b1 * 16)
                pool.tensor_copy(gidx[:, 1:2], tabi[:, bass.ds(b + (MAXB + AHEAD - 1), 1)]).then_inc(sem("sidx_ready"), 1)
                pool.wait_ge(sem("sidx_ready"), b1)
                pool.wait_ge(sem("yv_ready"), b1)
                pool.wait_ge(sem("scattered"), b1 * 16)
                settle(pool, "pool")
                pool.tensor_copy(ysb, yv).then_inc(sem("ysb_ready"), 1)
                pool.wait_ge(sem("ysb_ready"), b + 2)
                settle(pool, "pool")
                pool.indirect_dma_start(out=acc_dram, out_offset=bass.IndirectOffsetOnAxis(ap=gidx[:, 1:2], axis=0),
                                        in_=ysb, in_offset=None, bounds_check=2 * T + P - 1, oob_is_err=True,
                                        compute_op=ALU.add).then_inc(sem("scattered"), 16)
            pool.wait_ge(sem("gathered"), total * 16 + 48)

        @block.scalar
        def _(act):
            act.wait_ge(sem("cols_ready"), 1)
            act.activation(silu[:, :], cols[:, 0:8], ACT.Exp, scale=-1.0).then_inc(sem("exp_c"), 1)

            def rms_tiles(src, n, name, ready):
                for t in range(NT):
                    ready(t)
                    if t:
                        act.wait_ge(sem(f"{name}_ssq"), t)
                    act.activation(W[:, A0 + 14336:A0 + 15360], src[:, t, :], ACT.Square,
                                   accum_out=sm[:, n + t:n + t + 1]).then_inc(sem(f"{name}_ssq"), 1)

            rms_tiles(xt, 4, "n1", lambda t: act.wait_ge(sem(f"x_loaded{t}"), 16))

            def mod_copy(j):
                act.wait_ge(sem("mod_done"), order.index(j) + 1)
                act.activation(MR, bank[7][:, 0:256], ACT.Copy).then_inc(sem("mod_rows"), 1)

            act.wait_ge(sem("n1_ms"), 1)
            act.activation(sm[:, 12:16], sm[:, 8:12], ACT.Sqrt).then_inc(sem("n1_sd"), 1)
            mod_copy(1)
            mod_copy(0)
            act.wait_ge(sem("lam_dot"), 2)
            act.activation(sm[:, 2:4], sm[:, 0:2], ACT.Exp).then_inc(sem("lam_exp"), 1)
            act.wait_ge(sem("amp1_ready"), 1)
            for k in range(0, KT, 2):
                act.wait_ge(sem("xT_done"), k + 1)
                act.activation(hT[:, k, :], bank[k % 4][:, :], ACT.Identity, bias=mod[:, k:k + 1],
                               scale=amp[:, k:k + 1]).then_inc(sem("hT_act"), 1)

            def evac_heads(n):
                ch, t = steps[n]
                act.wait_ge(sem("qt_done"), n + 1)
                ps4 = bank[4 + n % 2].rearrange("p (m q) -> p m q", m=4)
                ts_ = slice(t * P, (t + 1) * P)
                if ch == MISC or ch == AKc:
                    for m in range(2):
                        for lo in (0, 64):
                            if ch == MISC:
                                dst, src = QKT[lo:lo + 64, (BK, IK)[m] + lo // 64, ts_], ps4[lo:lo + 64, m, :]
                            else:
                                tiles = QKT[:, AK1:AK1 + 4, :] if m == 0 else AK2
                                dst = tiles[lo:lo + 64, lo // 64::2, ts_]
                                src = ps4[lo:lo + 64, 2 * m:2 * m + 2, :]
                            ins = act.activation(dst, src, ACT.Copy)
                    ins.then_inc(sem("qt_evac"), 1)
                    return
                act.activation(QKT[:, PAIR0[ch]:PAIR0[ch] + 4, ts_], ps4, ACT.Copy).then_inc(sem("qt_evac"), 1)

            act.wait_ge(sem("zeros_ready"), 1)
            for n, (ch, t) in enumerate(steps):
                act.wait_ge(sem("proj_done"), n + 1)
                if n >= 3:
                    act.wait_ge(sem("qt_done"), min(n - 2, NTR))
                tmp = TMP[:, n % 3]
                ps = bank[n % 2]
                if ch == AVc:
                    act.activation(V[:, t, :], ps[:, :], ACT.Copy).then_inc(sem("proj_evac"), 1)
                elif ch == MISC:
                    two = [P, 2, HD]
                    act.activation(tmp[:, 0:128].rearrange("p (a q) -> p a q", a=2),
                                   ps[:, 0:64].unsqueeze(1).to_broadcast(two), ACT.Copy)
                    act.activation(tmp[:, 128:256].rearrange("p (a q) -> p a q", a=2),
                                   ps[:, 192:256].unsqueeze(1).to_broadcast(two), ACT.Copy)
                    act.activation(tmp[:, 256:384], ps[:, 64:192], ACT.Copy)
                    act.activation(tmp[:, 384:392], ps[:, 256:264], ACT.Copy).then_inc(sem("proj_evac"), 1)
                else:
                    act.activation(tmp, ps[:, :], ACT.Copy).then_inc(sem("proj_evac"), 1)
                if normed[n]:
                    act.wait_ge(sem("head_ms"), nth_norm[n])
                    act.activation(sm[:, 24:32], sm[:, 16:24], ACT.Sqrt).then_inc(sem("head_sd"), 1)
                if 2 <= n < NTR + 2:
                    evac_heads(n - 2)
                for m in C_STEP.get(n, ()):
                    nk = (units_c[m][0] + 1) * P
                    act.wait_ge(sem("iqk_done"), m + 1)
                    if m >= 2:
                        act.wait_ge(sem("rel_used"), m - 1)
                    act.activation(REL[:, m % 2, 0:nk], bank[2 + m % 2][:, 0:nk], ACT.Relu).then_inc(sem("rel_ready"), 1)
                if t == 3 and 1 <= ch <= 4:
                    mod_copy(ch + 1)

            act.wait_ge(sem("qt_done"), NTR)
            act.wait_ge(sem("g1b_done"), 1)
            for j in range(2):
                act.activation(G1B[:, j * 512:(j + 1) * 512], bank[j], ACT.Copy).then_inc(sem("g1b_ready"), 1)

            for n in range(NSTEP):
                if d := unit(n, "diff"):
                    i, h, m = d
                    nk = (i + 1) * P
                    act.wait_ge(sem("diff_max"), m + 1)
                    if m >= 2:
                        act.wait_ge(sem("diff_T"), m - 1)
                    if h < 2 and i:
                        act.wait_ge(sem("sparse_T"), 8 * i)
                    for j, Pj in enumerate((P1, P2)):
                        ins = act.activation(Pj[:, m % 2, 0:nk], bank[2 + 2 * (m % 2) + j][:, 0:nk], ACT.Exp,
                                             bias=sm[:, 36 + 2 * (m % 2) + j:37 + 2 * (m % 2) + j], scale=SCALE,
                                             accum_out=sm[:, 40 + 2 * (m % 4) + j:41 + 2 * (m % 4) + j])
                    ins.then_inc(sem("diff_exp"), 1)
                if e := unit(n, "sparse"):
                    i, h, m = e
                    nk = (i + 1) * P
                    act.wait_ge(sem("sparse_max"), m + 1)
                    if m >= 2:
                        act.wait_ge(sem("sparse_T"), m - 1)
                    if h < 2:
                        act.wait_ge(sem("diff_T"), 4 * i + 4)
                    act.activation(P1[:, m % 2, 0:nk], P2[:, m % 2, 0:nk], ACT.Exp, bias=sm[:, 52 + m % 2:53 + m % 2],
                                   scale=SCALE, accum_out=sm[:, 56 + m % 4:57 + m % 4]).then_inc(sem("sparse_exp"), 1)
                if n % 12 == 8 and n < NU:
                    act.wait_ge(sem("sub_ms"), n // 12 + 1)
                    act.activation(sm[:, 80:84], sm[:, 64:68], ACT.Sqrt).then_inc(sem("sub_sd"), 1)
                if jb := job(n):
                    i, j = jb
                    if j < 2:
                        act.wait_ge(sem("mixT_done"), 2 * i + j + 1)
                        act.activation(mixT[:, i % 2, 4 * j:4 * j + 4, :], bank[0].rearrange("p (k t) -> p k t", k=4),
                                       ACT.Copy).then_inc(sem("mixT_ready"), 1)
                    if j == 9:
                        act.wait_ge(sem("x2_ready"), i + 1)
                        act.activation(SQ2, x2[:, i, :], ACT.Square, accum_out=sm[:, 4 + i:5 + i]) \
                            .then_inc(sem("n2_ssq"), 1)
                        act.wait_ge(sem("n2_ms"), i + 1)
                        act.activation(sm[:, 12 + i:13 + i], sm[:, 8 + i:9 + i], ACT.Sqrt).then_inc(sem("n2_sd"), 1)
                if e := unit(n - 2, "sparse"):
                    m = e[2]
                    act.wait_ge(sem("sparse_oT"), m + 1)
                    if m >= 2:
                        act.wait_ge(sem("sparse_out_done"), m - 1)
                    act.activation(OT[:, m % 2, :], bank[1 + 6 * (n % 2)][:, 0:P], ACT.Copy).then_inc(sem("sparse_oTe"), 1)
                if d := unit(n - 1, "diff"):
                    i, h, m = d
                    nk = (i + 1) * P
                    act.wait_ge(sem("diff_T"), m + 1)
                    if m >= 2:
                        act.wait_ge(sem("diff_pv"), m - 1)
                    if h < 2 and i:
                        act.wait_ge(sem("sparse_oT"), 8 * i)
                    act.activation(AT[:, m % 2, 0:nk], bank[6][:, 0:nk], ACT.Copy).then_inc(sem("diff_Te"), 1)
            act.wait_ge(sem("gate_sub"), 1)
            act.activation(route[:, 528:544], route[:, 512:528], ACT.Exp).then_inc(sem("gate_exp"), 1)

            act.wait_ge(sem("cum_ready"), 1)
            act.wait_ge(sem("tabi_ready"), 1)
            total = act.value_load(cum[0:1, NE:NE + 1], min_val=NE, max_val=MAXB - 1)
            with act.Fori(0, total) as b:
                act.wait_ge(sem("gclip"), b + 1)
                act.activation(sg, gc, ACT.Sigmoid, scale=ALPHA).then_inc(sem("sig_ready"), 1)

        @block.tensor
        def _(pe):
            pe.wait_ge(sem("const_loaded"), 16)
            pe.wait_ge(sem("rows_loaded"), 64)
            pe.transpose(bank[7][:, 0:72], rows, ident[0:72, 0:72]).then_inc(sem("rowsT"), 1)
            pe.wait_ge(sem("silu_ready"), 1)

            def mod_part(j):
                s = j % 2
                n = order.index(j)
                pe.wait_ge(sem(f"ada_loaded{s}"), 16 * (j // 2 + 1))
                if n:
                    pe.wait_ge(sem("mod_rows"), n)
                for k in range(KT):
                    for q in range(4):
                        ins = pe.matmul(bank[7][32 * q:32 * q + 32, 0:256], silu32[:, 32 * k:32 * k + 32],
                                        slot[s][:, k, 256 * q:256 * q + 256], start=(k == 0), stop=(k == KT - 1))
                ins.then_inc(sem("mod_done"), 1)

            def mod_columns(j):
                n = order.index(j)
                pe.wait_ge(sem("mod_rows"), n + 1)
                if n:
                    pe.wait_ge(sem("mod_read"), n)
                for q in range(2):
                    ins = pe.transpose(bank[6][:, q * P:(q + 1) * P], MR[:, q * P:(q + 1) * P], ident)
                ins.then_inc(sem("mod_cols"), 1)

            def tile_transposes(src, done, act_sem, dve_sem, first_wait):
                for k in range(KT):
                    if k >= 4:
                        pe.wait_ge(sem(act_sem if k % 2 == 0 else dve_sem), (k - 4) // 2 + 1)
                    for t in range(NT):
                        if k == 0:
                            first_wait(t)
                        ins = pe.transpose(bank[k % 4][:, t * P:(t + 1) * P], src[:, t, k * P:(k + 1) * P], ident)
                    ins.then_inc(sem(done), 1)

            mod_part(1)
            mod_columns(1)
            mod_part(0)
            mod_columns(0)
            tile_transposes(xt, "xT_done", "hT_act", "hT_dve", lambda t: pe.wait_ge(sem("xhat_ready"), t + 1))
            pe.wait_ge(sem("hT_act"), 4)
            pe.wait_ge(sem("hT_dve"), 4)

            def heads(n):
                ch, t = steps[n]
                pe.wait_ge(sem("heads_ready"), n + 1)
                if n >= 2:
                    pe.wait_ge(sem("qt_evac"), n - 1)
                for m in range(2 if ch == MISC else 4):
                    ins = pe.transpose(bank[4 + n % 2][:, m * P:(m + 1) * P], TMP[:, n % 3, m * P:(m + 1) * P], ident)
                ins.then_inc(sem("qt_done"), 1)

            for n, (ch, t) in enumerate(steps):
                if t == 0:
                    pe.wait_ge(sem(f"win_loaded{ch % 2}"), 16 * (ch // 2 + 1))
                    if ch == MISC:
                        pe.wait_ge(sem("win_loaded_misc"), 16)
                if n >= 2:
                    pe.wait_ge(sem("proj_evac"), n - 1)
                w = 264 if ch == MISC else 512
                for k in range(KT):
                    ins = pe.matmul(bank[n % 2][:, 0:w], hT[:, k, t * P:(t + 1) * P], WIN[:, ch % 2, k, 0:w],
                                    start=(k == 0), stop=(k == KT - 1))
                ins.then_inc(sem("proj_done"), 1)
                if 2 <= n < NTR + 2:
                    heads(n - 2)
                for m in C_STEP.get(n, ()):
                    i, h = units_c[m]
                    if m == 0:
                        pe.wait_ge(sem("qt_evac"), 8)
                    if m >= 2:
                        pe.wait_ge(sem("rel_ready"), m - 1)
                    pe.matmul(bank[2 + m % 2][:, 0:(i + 1) * P], QKT[:, IQ + h // 2, i * P:(i + 1) * P],
                              QKT[:, IK + h % 2, 0:(i + 1) * P], start=True, stop=True).then_inc(sem("iqk_done"), 1)
                if t == 3 and 1 <= ch <= 4:
                    mod_part(ch + 1)
                    mod_columns(ch + 1)
            pe.wait_ge(sem("proj_evac"), NST)
            pe.wait_ge(sem("diag_ready"), 1)
            for k in range(KT):
                ins = pe.matmul(bank[k // 4][:, (k % 4) * P:(k % 4 + 1) * P], ones, DIAG[:, k, :],
                                start=True, stop=True)
            ins.then_inc(sem("g1b_done"), 1)
            pe.wait_ge(sem("qt_evac"), NTR)
            pe.wait_ge(sem("mod_read"), 6)
            pe.wait_ge(sem("small_loaded"), 16 * 10)

            def job_pe(i, j):
                if j < 2:
                    if j == 0:
                        pe.wait_ge(sem("sparse_out"), 8 * i + 8)
                        if i:
                            pe.wait_ge(sem("h2T_ready"), 2 * i)
                        else:
                            pe.wait_ge(sem("g1b_ready"), 2)
                    else:
                        pe.wait_ge(sem("mixT_ready"), 2 * i + 1)
                    for k in range(4):
                        ins = pe.transpose(bank[0][:, k * P:(k + 1) * P], MIX[:, i % 2, (4 * j + k) * P:(4 * j + k + 1) * P],
                                           ident)
                    ins.then_inc(sem("mixT_done"), 1)
                elif j < 10:
                    hf, q = (j - 2) // 4, (j - 2) % 4
                    if q == 0:
                        if hf == 0:
                            pe.wait_ge(sem("mixT_ready"), 2 * i + 2)
                            pe.wait_ge(sem("wout_loaded"), 16)
                        else:
                            pe.wait_ge(sem("mix_added"), 2 * i + 1)
                    for k in range(2 * q, 2 * q + 2):
                        ins = pe.matmul(bank[0], mixT[:, i % 2, k, :], slot[2][:, k, hf * 512:(hf + 1) * 512],
                                        start=(k == 0), stop=(k == KT - 1))
                    if q == 3:
                        ins.then_inc(sem("wout_done"), 1)
                else:
                    if j == 10:
                        pe.wait_ge(sem("mix_added"), 2 * i + 2)
                        pe.wait_ge(sem("xhat2_ready"), i + 1)
                    else:
                        pe.wait_ge(sem("h2T_ready"), 2 * i + 1)
                    for k in range(4):
                        c0 = (4 * (j - 10) + k) * P
                        ins = pe.transpose(bank[0][:, k * P:(k + 1) * P], XH2[:, i, c0:c0 + P], ident)
                    ins.then_inc(sem("xT2_done"), 1)

            def transposes(m_sem, buf, nk):
                for kb in range(nk // P):
                    ins = pe.transpose(bank[6][:, kb * P:(kb + 1) * P], P1[:, buf, kb * P:(kb + 1) * P], ident)
                ins.then_inc(sem(m_sem), 1)

            for n in range(NSTEP):
                if d := unit(n, "diff"):
                    i, h, m = d
                    if m >= 2:
                        pe.wait_ge(sem("diff_exp"), m - 1)
                    if h < 2 and i:
                        pe.wait_ge(sem("sparse_max"), 8 * i)
                    for j in range(2):
                        keys = QKT[:, AK1 + h, 0:(i + 1) * P] if j == 0 else AK2[:, h, 0:(i + 1) * P]
                        ins = pe.matmul(bank[2 + 2 * (m % 2) + j][:, 0:(i + 1) * P],
                                        QKT[:, AQ + 2 * j + h // 2, i * P:(i + 1) * P], keys, start=True, stop=True)
                    ins.then_inc(sem("diff_qk"), 1)
                if e := unit(n, "sparse"):
                    i, h, m = e
                    if h < 4:
                        pe.wait_ge(sem("diff_exp"), 4 * i + 4)
                    else:
                        pe.wait_ge(sem("sparse_max"), m - 3)
                    pe.matmul(bank[2 + m % 4][:, 0:(i + 1) * P], QKT[:, BQ + h // 2, i * P:(i + 1) * P],
                              QKT[:, BK + h % 2, 0:(i + 1) * P], start=True, stop=True).then_inc(sem("sparse_qk"), 1)
                if jb := job(n):
                    job_pe(*jb)
                if unit(n - 2, "diff") or unit(n - 2, "sparse"):
                    if d := unit(n - 4, "diff"):
                        pe.wait_ge(sem("diff_out"), d[2] + 1)
                    if e := unit(n - 4, "sparse"):
                        pe.wait_ge(sem("sparse_out"), e[2] + 1)
                if d := unit(n - 2, "diff"):
                    i, h, m = d
                    pe.wait_ge(sem("diff_Te"), m + 1)
                    for kb in range(i + 1):
                        ins = pe.matmul(bank[1 + 6 * (n % 2)][:, 0:P], AT[:, m % 2, kb * P:(kb + 1) * P],
                                        V[:, kb, h * P:(h + 1) * P], start=(kb == 0), stop=(kb == i))
                    ins.then_inc(sem("diff_pv"), 1)
                if e := unit(n - 2, "sparse"):
                    i, h, m = e
                    pe.wait_ge(sem("sparse_Te"), m + 1)
                    for kb in range(i + 1):
                        ins = pe.matmul(bank[1 + 6 * (n % 2)][:, 0:P], LAT[:, kb, :],
                                        AT[:, m % 2, kb * P:(kb + 1) * P], start=(kb == 0), stop=(kb == i))
                    ins.then_inc(sem("sparse_oT"), 1)
                if e := unit(n - 3, "sparse"):
                    i, h, m = e
                    pe.wait_ge(sem("sparse_oTe"), m + 1)
                    pe.matmul(bank[1 + 6 * ((n - 1) % 2)][:, P:P + HD], OT[:, m % 2, :], uv[:, h * HD:(h + 1) * HD],
                              start=True, stop=True).then_inc(sem("sparse_out_done"), 1)
                if d := unit(n - 1, "diff"):
                    i, h, m = d
                    pe.wait_ge(sem("diff_a"), m + 1)
                    if h:
                        pe.wait_ge(sem("diff_Te"), m)
                    elif i:
                        pe.wait_ge(sem("sparse_Te"), 8 * i)
                    transposes("diff_T", m % 2, (i + 1) * P)
                if e := unit(n - 1, "sparse"):
                    i, h, m = e
                    pe.wait_ge(sem("sparse_exp"), m + 1)
                    if h:
                        pe.wait_ge(sem("sparse_Te"), m)
                    else:
                        pe.wait_ge(sem("diff_Te"), 4 * i + 4)
                    transposes("sparse_T", m % 2, (i + 1) * P)
            pe.wait_ge(sem("h2T_ready"), 2 * NT)
            for k in range(KT):
                for t in range(NT):
                    ins = pe.matmul(bank[4][NE * t:NE * t + NE, 0:P], rw[:, k * NE:(k + 1) * NE],
                                    h2T[:, k, t * P:(t + 1) * P], start=(k == 0), stop=(k == KT - 1))
            ins.then_inc(sem("router_done"), 1)
            pe.wait_ge(sem("logits_sb"), 1)
            pe.transpose(bank[0][:, 0:P], lgT, ident).then_inc(sem("logits_T"), 1)
            pe.wait_ge(sem("brow_loaded"), 48)
            for m in range(2):
                for k in range(KT):
                    ins = pe.transpose(bank[5 + m][:, k * NE:(k + 1) * NE], BROW[:, m, k * P:(k + 1) * P],
                                       ident[0:NE, 0:NE])
            ins.then_inc(sem("brow_T"), 1)
            pe.wait_ge(sem("mask_ready"), 1)
            for t in range(NT):
                for u in range(t + 1):
                    pe.matmul(bank[0][:, t * NE:(t + 1) * NE], tri if u == t else ones,
                              route[:, u * NE:(u + 1) * NE], start=(u == 0), stop=(u == t))
            for u in range(NT):
                ins = pe.matmul(bank[0][:, 128:160], ones, route[:, u * NE:(u + 1) * NE],
                                start=(u == 0), stop=(u == NT - 1))
            ins.then_inc(sem("rank_done"), 1)
            pe.wait_ge(sem("onehot_ready"), 1)
            for j in range(16):
                ins = pe.matmul(bank[1][:, 0:2 * MAXB], LH[:, j, :], RH[:, j, :], start=(j == 0), stop=(j == 15))
            ins.then_inc(sem("tables_done"), 1)
            pe.wait_ge(sem("gate_mat"), 1)
            for t in range(NT):
                ins = pe.transpose(bank[2][0:NE, t * P:(t + 1) * P], gmat[:, t * NE:(t + 1) * NE], ident)
            ins.then_inc(sem("gate_T"), 1)
            pe.wait_ge(sem("diag2_ready"), 1)
            for k in range(KT):
                ins = pe.matmul(bank[3 + k // 4][:, (k % 4) * P:(k % 4 + 1) * P], ones, DIAG2[:, k, :],
                                start=True, stop=True)
            ins.then_inc(sem("g2b_done"), 1)
            pe.wait_ge(sem("gate_Te"), 1)
            for n in range(2 * NT):
                t, hf = n // 2, n % 2
                if n >= 2:
                    pe.wait_ge(sem("bias_added"), n - 1)
                pe.matmul(bank[5 + hf][:, :], GT[:, t * P:(t + 1) * P], BROW[:, 2, hf * 512:hf * 512 + 512],
                          start=True, stop=True).then_inc(sem("bias_done"), 1)

            def rows_in():
                settle(pe, "pe")
                out3 = bank[7][:, :].rearrange("p (h j s) -> p j h s", h=2, j=4)
                for j in range(4):
                    ins = pe.transpose(out3[:, j], xgc[:, j * P:(j + 1) * P], ident)
                ins.then_inc(sem("xg_used"), 1)

            pe.wait_ge(sem("cum_ready"), 1)
            pe.wait_ge(sem("tabi_ready"), 1)
            pe.wait_ge(sem("xg_ready"), 1)
            rows_in()

            with pe.Fori(0, NE // 2) as pr:
                for s in range(2):
                    e = pr * 2 + s
                    first = pe.value_load(cum[0:1, bass.ds(e, 1)], min_val=0, max_val=MAXB - 1)
                    end = pe.value_load(cum[0:1, bass.ds(e + 1, 1)], min_val=1, max_val=MAXB - 1)
                    loads = pe.snap((pr + 1) * 16)
                    dloads = pe.snap((e + 1) * 16)
                    with pe.Fori(first, end) as b:
                        b1 = pe.snap(b + 1)

                        def turn(bk, c0, src, done):
                            o3 = bank[bk][:, c0:c0 + 256].rearrange("p (q c s) -> p c q s", q=2, c=2)
                            for cc in range(2):
                                ins = pe.transpose(o3[:, cc], src[:, cc * P:(cc + 1) * P], ident)
                            if done:
                                ins.then_inc(sem(done), 1)

                        def turn_up(hf):
                            pe.wait_ge(sem(f"usb_ready{hf}"), b1)
                            settle(pe, "pe")
                            turn((5, 1)[hf], 0, usb[:, hf, :], f"up_turned{hf}")

                        def up(hf):
                            for k in range(KT):
                                if hf == 0 and k % (KT // WQ) == 0:
                                    pe.wait_ge(sem(f"up_loaded{s}_{k * WQ // KT}"), loads)
                                for q in range(2):
                                    c0 = 512 * hf + 256 * q
                                    ins = pe.matmul(bank[2 + hf][BS * q:BS * q + BS, 0:256], xT[:, k, :],
                                                    UP[s][:, k, c0:c0 + 256], start=(k == 0), stop=(k == KT - 1))
                                if hf == 1 and k == 3:
                                    turn_up(0)
                            ins.then_inc(sem(f"up_done{hf}"), 1)

                        pe.wait_ge(sem("xTb_ready"), b1)
                        for k in range(KT):
                            if k % (KT // WQ) == 0:
                                pe.wait_ge(sem(f"gate_loaded{s}_{k * WQ // KT}"), loads)
                            w = GATE[s][:, k, :].rearrange("p (h q n) -> p q h n", h=2, q=2)
                            for q in range(2):
                                ins = pe.matmul(bank[0][BS * q:BS * q + BS, :], xT[:, k, :], w[:, q],
                                                start=(k == 0), stop=(k == KT - 1))
                        ins.then_inc(sem("gate_done"), 1)
                        up(0)
                        pe.wait_ge(sem("gsb_ready"), b1)
                        settle(pe, "pe")
                        turn(4, 0, gsb[:, 0, :], None)
                        turn(4, 256, gsb[:, 1, :], "gate_turned")
                        up(1)
                        pe.wait_ge(sem("xg_ready"), b1 + 1)
                        rows_in()
                        turn_up(1)
                        for hf in range(2):
                            pe.wait_ge(sem(f"aT_ready{hf}"), b1)
                            for k in range(4 * hf, 4 * hf + 4):
                                if k % (KT // WQ) == 0:
                                    pe.wait_ge(sem(f"down_loaded0_{k * WQ // KT}"), dloads)
                                for q in range(2):
                                    ins = pe.matmul(bank[6][BS * q:BS * q + BS, :], aT[:, k, :],
                                                    DOWN[:, k, 512 * q:512 * q + 512], start=(k == 0),
                                                    stop=(k == KT - 1))
                            ins.then_inc(sem(("down_half", "down_done")[hf]), 1)

        @block.vector
        def _(dve):
            chain = [0]

            def link(ins):
                chain[0] += 1
                ins.then_inc(sem("dve_step"), 1)
                dve.wait_ge(sem("dve_step"), chain[0])

            def own(ins, name, n):
                ins.then_inc(sem(name), 1)
                dve.wait_ge(sem(name), n)

            tt, ts, stt = dve.tensor_tensor, dve.tensor_scalar, dve.scalar_tensor_tensor

            dve.wait_ge(sem("rowsT"), 1)
            dve.tensor_copy(cols[:, :], bank[7][:, 0:72]).then_inc(sem("cols_ready"), 1)
            dve.wait_ge(sem("cols_ready"), 1)
            dve.wait_ge(sem("exp_c"), 1)
            link(ts(silu[:, :], silu[:, :], 1.0, None, ALU.add))
            link(dve.reciprocal(silu[:, :], silu[:, :]))
            link(tt(silu[:, :], silu[:, :], cols[:, 0:8], ALU.mult))
            dve.tensor_copy(silu32[:, :].rearrange("p (k r) -> p k r", k=KT),
                            silu[:, :].unsqueeze(2).to_broadcast([P, KT, 32])).then_inc(sem("silu_ready"), 1)
            dve.wait_ge(sem("n1_ssq"), NT)
            ts(sm[:, 8:12], sm[:, 4:8], 1.0 / D, EPS, ALU.mult, ALU.add).then_inc(sem("n1_ms"), 1)
            dve.wait_ge(sem("n1_sd"), 1)
            link(dve.reciprocal(sm[:, 12:16], sm[:, 12:16]))
            for t in range(NT):
                ts(xt[:, t, :], xt[:, t, :], sm[:, 12 + t:13 + t], None, ALU.mult).then_inc(sem("xhat_ready"), 1)

            def mod_evac(j):
                n = order.index(j)
                dve.wait_ge(sem("mod_cols"), n + 1)
                dst = mod[:, 8 * j:8 * j + 8].rearrange("p (q c) -> p q c", c=2)
                src = bank[6][:, 0:256].rearrange("p (c q r) -> p q c r", c=2, q=4)[:, :, :, 0]
                bias = cols[:, 24 + 8 * j:32 + 8 * j].rearrange("p (q c) -> p q c", c=2)
                own(tt(dst, src, bias, ALU.add), "mod_read", n + 1)

            mod_evac(1)
            mod_evac(0)
            dve.wait_ge(sem("small_loaded"), 16 * 10)
            for j in range(2):
                dve.tensor_tensor_reduce(lamb[:, 128 * j:128 * j + 64], lamb[:, 128 * j:128 * j + 64],
                                         lamb[:, 128 * j + 64:128 * j + 128], 1.0, 0.0, ALU.mult, ALU.add,
                                         sm[:, j:j + 1]).then_inc(sem("lam_dot"), 1)
            dve.wait_ge(sem("lam_exp"), 1)
            link(tt(sm[:, 34:35], sm[:, 3:4], sm[:, 2:3], ALU.subtract))
            link(ts(sm[:, 34:35], sm[:, 34:35], -LAM0, None, ALU.add))
            link(ts(gains[:, 384:512], gains[:, 384:512], 1.0 - LAM0, None, ALU.mult))
            stt(amp[:, 0:8], mod[:, 8:16], 1.0, cols[:, 8:16], ALU.add, ALU.mult).then_inc(sem("amp1_ready"), 1)
            dve.wait_ge(sem("amp1_ready"), 1)
            for k in range(1, KT, 2):
                dve.wait_ge(sem("xT_done"), k + 1)
                ts(hT[:, k, :], bank[k % 4][:, :], amp[:, k:k + 1], mod[:, k:k + 1], ALU.mult, ALU.add) \
                    .then_inc(sem("hT_dve"), 1)

            def rope(tmp, t, nh, n):
                heads = tmp.rearrange("p (h q) -> p h q", q=HD)
                xr = heads[:, :, 0:16]
                cs = CT[:, C_COS + 16 * t:C_COS + 16 * t + 16].unsqueeze(1).to_broadcast([P, nh, 16])
                sn = CT[:, C_SIN + 16 * t:C_SIN + 16 * t + 16].unsqueeze(1).to_broadcast([P, nh, 16])
                ta = RT[:, 0:128].rearrange("p (h q) -> p h q", q=16)[:, 0:nh, :]
                tb = RT[:, 128:256].rearrange("p (h q) -> p h q", q=16)[:, 0:nh, :]
                tt(ta, xr, cs, ALU.mult)
                link(tt(tb, xr, sn, ALU.mult))
                tt(heads[:, :, 0:8], ta[:, :, 0:8], tb[:, :, 8:16], ALU.subtract)
                own(tt(heads[:, :, 8:16], ta[:, :, 8:16], tb[:, :, 0:8], ALU.add), "heads_ready", n + 1)

            def index_scores(m):
                i, h = units_c[m]
                nk = (i + 1) * P
                dve.wait_ge(sem("rel_ready"), m + 1)
                w = iw[:, 8 * i + h:8 * i + h + 1]
                if h == 0:
                    ins = ts(AM[i], REL[:, m % 2, 0:nk], w, None, ALU.mult)
                else:
                    ins = stt(AM[i], REL[:, m % 2, 0:nk], w, AM[i], ALU.mult, ALU.add)
                own(ins, "rel_used", m + 1)
                if h == 7:
                    link(dve.memset(AM[i][0:64, nk - 64:nk], NEG))

            def topk_round(i, r):
                link(dve.max(sm[:, 96:104], AM[i]))
                link(dve.match_replace(AM[i], sm[:, 96:104], AM[i], TAKEN))
                if r == 15:
                    link(ts(AM[i], AM[i], TAKEN, NEG, ALU.not_equal, ALU.mult))

            rounds = [(i, r) for i in range(1, NT) for r in range(16)]
            dve.wait_ge(sem("const_loaded"), 16)
            link(dve.memset(AM[0], 0.0))
            link(dve.memset(AM[0][0:64, 64:128], NEG))

            def head_work(n, ch, t):
                dve.wait_ge(sem("proj_evac"), n + 1)
                tmp = TMP[:, n % 3]
                if ch == IQc:
                    rope(tmp, t, 8, n)
                    return
                nh = 2 if ch == MISC else 8
                hv = tmp[:, 0:nh * HD].rearrange("p (h q) -> p h q", q=HD)
                sq = SQ[:, 0:nh * HD].rearrange("p (h q) -> p h q", q=HD)
                link(tt(sq, hv, hv, ALU.mult))
                if ch == MISC:
                    link(tt(SQ[:, 128:256], tmp[:, 256:384], tmp[:, 256:384], ALU.mult))
                    link(dve.memset(sm[:, 16:24], 64.0))
                    link(dve.tensor_reduce(sm[:, 16:18], sq, AX, ALU.add))
                    link(dve.tensor_reduce(sm[:, 18:19], SQ[:, 128:256], AX, ALU.add))
                    link(ts(sm[:, 18:19], sm[:, 18:19], 0.5, None, ALU.mult))
                    link(ts(iw[:, 8 * t:8 * t + 8], tmp[:, 384:392], 8 ** -0.5, 64 ** -0.5, ALU.mult, ALU.mult))
                else:
                    link(dve.tensor_reduce(sm[:, 16:24], sq, AX, ALU.add))
                ts(sm[:, 16:24], sm[:, 16:24], 1.0 / HD, EPS, ALU.mult, ALU.add).then_inc(sem("head_ms"), 1)
                dve.wait_ge(sem("head_sd"), nth_norm[n])
                link(dve.reciprocal(sm[:, 24:32], sm[:, 24:32]))
                link(tt(hv, hv, sm[:, 24:24 + nh].unsqueeze(2).to_broadcast([P, nh, HD]), ALU.mult))
                g = 3 if ch == MISC else GAIN[ch]
                link(tt(hv, hv, gains[:, HD * g:HD * g + HD].unsqueeze(1).to_broadcast([P, nh, HD]), ALU.mult))
                if ch == MISC:
                    link(stt(LAT[:, t, :], tmp[:, 256:384], sm[:, 26:27], gains[:, 256:384], ALU.mult, ALU.mult))
                rope(tmp[:, 0:256] if ch == MISC else tmp, t, 4 if ch == MISC else 8, n)

            for n, (ch, t) in enumerate(steps):
                if n < NTR:
                    head_work(n, ch, t)
                for m in C_STEP.get(n, ()):
                    index_scores(m)
                for _ in range(0 if n < 12 else 3 if n < NTR - 1 else 4):
                    if rounds:
                        topk_round(*rounds.pop(0))
                if n == NST - 1:
                    dve.wait_ge(sem("mod_done"), 6)
                    for k in range(KT):
                        ins = ts(DIAG[:, k, :], ident, mod[:, 16 + k:17 + k], None, ALU.mult)
                    ins.then_inc(sem("diag_ready"), 1)
                if t == 3 and 1 <= ch <= 4:
                    mod_evac(ch + 1)
            stt(amp[:, 8:16], mod[:, 32:40], 1.0, cols[:, 16:24], ALU.add, ALU.mult).then_inc(sem("amp2_ready"), 1)

            assert all(i == NT - 1 for i, _ in rounds) and len(rounds) < 12 * (NT - 1)
            for n in range(NSTEP):
                if d := unit(n, "diff"):
                    i, h, m = d
                    nk = (i + 1) * P
                    dve.wait_ge(sem("diff_qk"), m + 1)
                    pair = psum[:, 1024 * (1 + m % 2):1024 * (2 + m % 2)].rearrange("p (j n) -> p j n", j=2)
                    link(dve.memset(pair[0:64, :, nk - 64:nk], NEG))
                    link(dve.tensor_reduce(sm[:, 32:34], pair[:, :, 0:nk], AX, ALU.max))
                    own(ts(sm[:, 36 + 2 * (m % 2):38 + 2 * (m % 2)], sm[:, 32:34], -SCALE, None, ALU.mult),
                        "diff_max", m + 1)
                if e := unit(n, "sparse"):
                    i, h, m = e
                    nk = (i + 1) * P
                    dve.wait_ge(sem("sparse_qk"), m + 1)
                    if m >= 2:
                        dve.wait_ge(sem("sparse_exp"), m - 1)
                    link(dve.tensor_tensor_reduce(P2[:, m % 2, 0:nk], bank[2 + m % 4][:, 0:nk], AM[i], 1.0,
                                                  2 * NEG, ALU.add, ALU.max, sm[:, 54:55]))
                    own(ts(sm[:, 52 + m % 2:53 + m % 2], sm[:, 54:55], -SCALE, None, ALU.mult), "sparse_max", m + 1)
                if d := unit(n - 1, "diff"):
                    i, h, m = d
                    nk = (i + 1) * P
                    s0 = 40 + 2 * (m % 4)
                    dve.wait_ge(sem("diff_exp"), m + 1)
                    link(ts(sm[:, 35:36], sm[:, s0:s0 + 1], sm[:, 34:35], None, ALU.mult))
                    link(dve.reciprocal(sm[:, s0:s0 + 2], sm[:, s0:s0 + 2]))
                    link(tt(sm[:, 35:36], sm[:, 35:36], sm[:, s0 + 1:s0 + 2], ALU.mult))
                    own(stt(P1[:, m % 2, 0:nk], P2[:, m % 2, 0:nk], sm[:, 35:36], P1[:, m % 2, 0:nk], ALU.mult,
                            ALU.add), "diff_a", m + 1)
                if d := unit(n - 2, "diff"):
                    i, h, m = d
                    dve.wait_ge(sem("diff_pv"), m + 1)
                    if h == 0 and i >= 2:
                        dve.wait_ge(sem("mixT_done"), 2 * (i - 1))
                    s0 = 40 + 2 * (m % 4)
                    own(ts(MIX[:, i % 2, h * P:(h + 1) * P], bank[1 + 6 * (n % 2)][:, 0:P], sm[:, s0:s0 + 1],
                           None, ALU.mult), "diff_out", m + 1)
                if rounds and n >= 1:
                    topk_round(*rounds.pop(0))
                if n % 12 == 8 and n < NU:
                    i = n // 12
                    for h in range(4):
                        a = MIX[:, i % 2, h * P:(h + 1) * P]
                        link(dve.tensor_tensor_reduce(WTMP[:, 0:P], a, a, 1.0, 0.0, ALU.mult, ALU.add,
                                                      sm[:, 64 + h:65 + h]))
                    own(ts(sm[:, 64:68], sm[:, 64:68], 1.0 / P, EPS, ALU.mult, ALU.add), "sub_ms", i + 1)
                    dve.wait_ge(sem("sub_sd"), i + 1)
                    link(dve.reciprocal(sm[:, 80:84], sm[:, 80:84]))
                    for h in range(4):
                        a = MIX[:, i % 2, h * P:(h + 1) * P]
                        link(stt(a, a, sm[:, 80 + h:81 + h], gains[:, 384:512], ALU.mult, ALU.mult))
                if jb := job(n):
                    i, j = jb
                    if j in (5, 9):
                        hf = j // 9
                        if i == 0 and hf == 0:
                            dve.wait_ge(sem("x_again"), 16)
                            dve.wait_ge(sem("g1b_ready"), 2)
                        dve.wait_ge(sem("wout_done"), 2 * i + hf + 1)
                        cs = slice(hf * 512, hf * 512 + 512)
                        own(tt(WTMP, bank[0], G1B[:, cs], ALU.mult), "mix_added", 2 * i + hf + 1)
                        ins = tt(x2[:, i, cs], x2[:, i, cs], WTMP, ALU.add)
                        if hf == 0:
                            link(ins)
                        else:
                            own(ins, "x2_ready", i + 1)
                            dve.wait_ge(sem("n2_ssq"), i + 1)
                            ts(sm[:, 8 + i:9 + i], sm[:, 4 + i:5 + i], 1.0 / D, EPS, ALU.mult, ALU.add) \
                                .then_inc(sem("n2_ms"), 1)
                            dve.wait_ge(sem("n2_sd"), i + 1)
                            link(dve.reciprocal(sm[:, 12 + i:13 + i], sm[:, 12 + i:13 + i]))
                            ts(XH2[:, i, :], x2[:, i, :], sm[:, 12 + i:13 + i], None, ALU.mult) \
                                .then_inc(sem("xhat2_ready"), 1)
                    if j >= 10:
                        c0 = 4 * (j - 10)
                        q = [P, 4, P]
                        dst = h2T[:, c0:c0 + 4, i * P:(i + 1) * P]
                        dve.wait_ge(sem("xT2_done"), 2 * i + j - 9)
                        link(tt(dst, bank[0].rearrange("p (k t) -> p k t", k=4),
                                amp[:, 8 + c0:12 + c0].unsqueeze(2).to_broadcast(q), ALU.mult))
                        own(tt(dst, dst, mod[:, 24 + c0:28 + c0].unsqueeze(2).to_broadcast(q), ALU.add),
                            "h2T_ready", 2 * i + j - 9)
                if e := unit(n - 3, "sparse"):
                    i, h, m = e
                    link(dve.reciprocal(sm[:, 60 + m % 4:61 + m % 4], sm[:, 56 + m % 4:57 + m % 4]))
                    dve.wait_ge(sem("sparse_out_done"), m + 1)
                    own(ts(MIX[:, i % 2, 512 + h * HD:512 + (h + 1) * HD], bank[1 + 6 * ((n - 1) % 2)][:, P:P + HD],
                           sm[:, 60 + m % 4:61 + m % 4], None, ALU.mult), "sparse_out", m + 1)
                if e := unit(n - 1, "sparse"):
                    i, h, m = e
                    nk = (i + 1) * P
                    dve.wait_ge(sem("sparse_T"), m + 1)
                    if m >= 2:
                        dve.wait_ge(sem("sparse_oT"), m - 1)
                    if h < 2:
                        dve.wait_ge(sem("diff_pv"), 4 * i + 3 + h)
                    own(dve.tensor_copy(AT[:, m % 2, 0:nk], bank[6][:, 0:nk]), "sparse_Te", m + 1)
            lg = X[:, 0:128]
            top = X[:, 128:160]
            topi = X[:, 160:192].bitcast(U32)
            topf = X[:, 192:224]
            OH = [X[:, 256 + 128 * k:384 + 128 * k] for k in range(TOPK)]
            fl = X[:, 768:896]
            sl = X[:, 896:1024]
            rk = X[:, 1024:1152]
            pr_ = X[:, 1152:1280]
            sel = X[:, 1280:1312]
            nb = X[:, 1312:1344]
            cumf = X[:, 1344:1377]
            one32 = ones[:, 0:NE]
            mask = route[:, 0:128]
            gs = route[:, 512:528]
            ge = route[:, 528:544]
            gsum = route[:, 544:548]
            t3 = lambda a: a.rearrange("p (t e) -> p t e", t=NT)
            dve.wait_ge(sem("router_done"), 1)
            dve.tensor_copy(lgT, bank[4][:, 0:P]).then_inc(sem("logits_sb"), 1)
            dve.wait_ge(sem("logits_T"), 1)
            link(tt(t3(lg), t3(bank[0][:, 0:128]), rb[:, :].unsqueeze(1).to_broadcast([P, NT, NE]), ALU.add))
            for t in range(NT):
                link(dve.max(top[:, 8 * t:8 * t + 8], lg[:, NE * t:NE * t + NE]))
                link(dve.max_index(topi[:, 8 * t:8 * t + 8], top[:, 8 * t:8 * t + 8], lg[:, NE * t:NE * t + NE]))
            link(dve.tensor_copy(topf, topi))
            top3, topf3 = t3(top), t3(topf)
            for k in range(TOPK):
                link(tt(t3(OH[k]), iota[:, 0:NE].unsqueeze(1).to_broadcast([P, NT, NE]),
                        topf3[:, :, k:k + 1].to_broadcast([P, NT, NE]), ALU.is_equal))
            link(tt(mask, OH[0], OH[1], ALU.add))
            link(tt(mask, mask, OH[2], ALU.add))
            tt(mask, mask, OH[3], ALU.add).then_inc(sem("mask_ready"), 1)
            dve.wait_ge(sem("brow_T"), 1)
            for m in range(2):
                ins = dve.tensor_copy(biasT[:, m * 256:(m + 1) * 256], bank[5 + m][:, 0:256])
            ins.then_inc(sem("biasT_done"), 1)

            tt(t3(gs), top3[:, :, 0:TOPK], top3[:, :, 0:1].to_broadcast([P, NT, TOPK]), ALU.subtract) \
                .then_inc(sem("gate_sub"), 1)
            dve.wait_ge(sem("gate_exp"), 1)
            link(dve.tensor_reduce(gsum, t3(ge), AX, ALU.add))
            link(dve.reciprocal(gsum, gsum))
            link(tt(t3(ge), t3(ge), gsum.unsqueeze(2).to_broadcast([P, NT, TOPK]), ALU.mult))
            dve.wait_ge(sem("rank_done"), 1)
            link(dve.tensor_copy(rk, bank[0][:, 0:128]))
            link(ts(nb, bank[0][:, 128:160], float(BS), 1.0, ALU.is_gt, ALU.add))
            for j in range(2, T // BS):
                link(stt(nb, bank[0][:, 128:160], float(BS * j), nb, ALU.is_gt, ALU.add))
            link(dve.memset(cumf[:, 0:1], 0.0))
            link(dve.tensor_tensor_scan(cumf[:, 1:33], one32, nb, 0.0, ALU.mult, ALU.add))
            dve.tensor_copy(cum[:, :], cumf).then_inc(sem("cum_ready"), 1)
            link(ts(fl, rk, float(BS), None, ALU.is_ge))
            for j in range(2, T // BS):
                link(stt(fl, rk, float(BS * j), fl, ALU.is_ge, ALU.add))
            link(stt(sl, fl, -float(BS), rk, ALU.mult, ALU.add))
            link(tt(t3(fl), t3(fl), cumf[:, 0:NE].unsqueeze(1).to_broadcast([P, NT, NE]), ALU.add))
            for k in range(TOPK):
                for q, src in enumerate((fl, sl)):
                    link(tt(pr_, OH[k], src, ALU.mult))
                    link(dve.tensor_reduce(sel[:, 16 * q:16 * q + 16].rearrange("p (t k) -> p t k", k=TOPK)[:, :, k],
                                           t3(pr_), AX, ALU.add))
            g3 = lambda n: [P, 16, n]
            link(tt(LH, iota.unsqueeze(1).to_broadcast(g3(P)), sel[:, 16:32].unsqueeze(2).to_broadcast(g3(P)),
                    ALU.is_equal))
            link(tt(OB, iota[:, 0:64].unsqueeze(1).to_broadcast(g3(64)), sel[:, 0:16].unsqueeze(2).to_broadcast(g3(64)),
                    ALU.is_equal))
            link(tt(RH[:, :, 0:64], OB, ge.unsqueeze(2).to_broadcast(g3(64)), ALU.mult))
            link(ts(pr_[:, 0:NT], CT[:, C_TOK:C_TOK + NT], -float(T), None, ALU.add))
            link(dve.tensor_copy(sl[:, 0:16].rearrange("p (t k) -> p t k", k=TOPK),
                                 pr_[:, 0:NT].unsqueeze(2).to_broadcast([P, NT, TOPK])))
            own(tt(RH[:, :, 64:128], OB, sl[:, 0:16].unsqueeze(2).to_broadcast(g3(64)), ALU.mult), "onehot_ready", 1)
            for k in range(TOPK):
                w = t3(ge)[:, :, k:k + 1].to_broadcast([P, NT, NE])
                link(tt(t3(OH[k]), t3(OH[k]), w, ALU.mult))
            link(tt(gmat, OH[0], OH[1], ALU.add))
            link(tt(gmat, gmat, OH[2], ALU.add))
            own(tt(gmat, gmat, OH[3], ALU.add), "gate_mat", 1)
            dve.wait_ge(sem("tables_done"), 1)
            tk = bank[1][:, 64:128]
            emp = tab[:, 64:128]
            link(dve.tensor_copy(tab[:, 0:64], bank[1][:, 0:64]))
            link(ts(emp, tk, 0.0, None, ALU.is_equal))
            link(ts(tf, tk, 2.0, 2.0 * T, ALU.mult, ALU.add))
            link(ts(tf, tf, CT[:, C_HALF:C_HALF + 1], None, ALU.add))
            link(stt(tf2, emp, -2.0 * T, tf, ALU.mult, ALU.add))
            dve.tensor_copy(tabi[:, 0:64], tf2)
            dve.tensor_copy(tabi[:, MAXB:MAXB + AHEAD - 1], CT[:, C_HALF:C_HALF + 1].to_broadcast([P, AHEAD - 1]))
            link(ts(emp, emp, CT[:, C_HALF + 1:C_HALF + 2], -2.0 * T, ALU.mult, ALU.add))
            link(ts(emp, emp, 0.0, None, ALU.max))
            link(tt(tf, tf, emp, ALU.add))
            dve.tensor_copy(tabi[:, MAXB + AHEAD - 1:2 * MAXB + AHEAD - 1], tf).then_inc(sem("tabi_ready"), 1)

            for k in range(KT):
                ins = ts(DIAG2[:, k, :], ident, mod[:, 40 + k:41 + k], None, ALU.mult)
            ins.then_inc(sem("diag2_ready"), 1)
            dve.wait_ge(sem("gate_T"), 1)
            dve.tensor_copy(GT, bank[2][0:NE, :]).then_inc(sem("gate_Te"), 1)
            dve.wait_ge(sem("g2b_done"), 1)
            for j in range(2):
                link(dve.tensor_copy(G2B[:, j * 512:(j + 1) * 512], bank[3 + j][:, :]))

            def scale_shift(n):
                q = [P, KT, BS]
                ps = bank[7][:, :].rearrange("p (k s) -> p k s", k=KT)
                ins = tt(xT, ps, amp[:, 8:16].unsqueeze(2).to_broadcast(q), ALU.mult)
                ins.then_inc(sem("xT_scaled"), 1)
                dve.wait_ge(sem("xT_scaled"), n)
                tt(xT, xT, mod[:, 24:32].unsqueeze(2).to_broadcast(q), ALU.add).then_inc(sem("xTb_ready"), 1)

            for n in range(2 * NT):
                t, hf = n // 2, n % 2
                cs = slice(hf * 512, hf * 512 + 512)
                dve.wait_ge(sem("bias_done"), n + 1)
                own(tt(s4[:, 6656:7168], bank[5 + hf][:, :], G2B[:, cs], ALU.mult), "bias_added", n + 1)
                ins = tt(x2[:, t, cs], x2[:, t, cs], s4[:, 6656:7168], ALU.add)
                if hf:
                    own(ins, "start_ready", t + 1)
                else:
                    link(ins)
            dve.wait_ge(sem("xg_used"), 1)
            scale_shift(1)
            dve.wait_ge(sem("start_stored"), 16 * NT)
            dve.wait_ge(sem("scattered"), 16)
            dve.tensor_copy(G2H[0:64, :], G2B[0:64, 0:512])
            link(dve.tensor_copy(G2H[64:128, :], G2B[64:128, 512:1024]))
            dve.sem_inc(sem("g2_copied"), 1)
            dve.wait_ge(sem("cum_ready"), 1)

            def gate_act(e, b1):
                dve.wait_ge(sem("gate_done"), b1)
                dve.tensor_copy(gsb.rearrange("p h n -> p (h n)"), bank[0]).then_inc(sem("gsb_ready"), 1)
                dve.wait_ge(sem("up_done0"), b1)
                dve.tensor_copy(usb[:, 0, :], bank[2][:, 0:256]).then_inc(sem("usb_ready0"), 1)
                dve.wait_ge(sem("gate_turned"), b1)
                q = [P, KT, BS]
                tt(gc, bank[4].rearrange("p (m s) -> p m s", m=KT), bgT[:, :, bass.ds(e, 1)].to_broadcast(q), ALU.add) \
                    .then_inc(sem("gbias"), 1)
                dve.wait_ge(sem("gbias"), b1)
                ts(gc, gc, LIMIT, None, ALU.min).then_inc(sem("gclip"), 1)
                dve.wait_ge(sem("gclip"), b1)

            def up_act(hf, e, b1, h1):
                hs = slice(4 * hf, 4 * hf + 4)
                q = [P, 4, BS]
                up = bank[(5, 1)[hf]][:, 0:256].rearrange("p (m s) -> p m s", m=4)

                def after(ins, name):
                    ins.then_inc(sem(name), 1)
                    dve.wait_ge(sem(name), h1)

                if hf:
                    dve.wait_ge(sem("up_done1"), b1)
                    dve.tensor_copy(usb[:, 1, :], bank[3][:, 0:256]).then_inc(sem("usb_ready1"), 1)
                dve.wait_ge(sem(f"up_turned{hf}"), b1)
                after(tt(uc[:, hs, :], up, buT[:, hs, bass.ds(e, 1)].to_broadcast(q), ALU.add), "ubias")
                after(ts(uc[:, hs, :], uc[:, hs, :], -LIMIT, LIMIT, ALU.max, ALU.min), "uclip")
                after(stt(uc[:, hs, :], uc[:, hs, :], 1.0, gc[:, hs, :], ALU.add, ALU.mult), "ug")
                if hf == 0:
                    dve.wait_ge(sem("sig_ready"), b1)
                tt(aT[:, hs, :], uc[:, hs, :], sg[:, hs, :], ALU.mult).then_inc(sem(f"aT_ready{hf}"), 1)

            with dve.Fori(0, NE) as e:
                first = dve.value_load(cum[0:1, bass.ds(e, 1)], min_val=0, max_val=MAXB - 1)
                end = dve.value_load(cum[0:1, bass.ds(e + 1, 1)], min_val=1, max_val=MAXB - 1)
                with dve.Fori(first, end) as b:
                    b1 = dve.snap(b + 1)
                    gate_act(e, b1)
                    up_act(0, e, b1, dve.snap(b * 2 + 1))
                    up_act(1, e, b1, dve.snap(b * 2 + 2))
                    dve.wait_ge(sem("xg_used"), b1 + 1)
                    scale_shift(b1 + 1)
                    dve.wait_ge(sem("down_done"), b1)
                    dve.wait_ge(sem("ysb_ready"), b1)
                    stt(yv, bank[6][:, :], tab[:, bass.ds(b, 1)], G2H[:, :], ALU.mult, ALU.mult) \
                        .then_inc(sem("yv_ready"), 1)


_ARGS = ["x", "c", "norm1_g", "norm2_g", "w_ada", "b_ada", "w_in", "w_out", "a_q_norm_g", "a_k_norm_g", "a_lambda",
         "a_sub_g", "b_q_norm_g", "b_k_norm_g", "b_kv_norm_g", "b_w_uv", "router_w", "router_b", "w_gate", "b_gate",
         "w_up", "b_up", "w_down", "b_down"]
_SQUEEZE = {"x", "w_ada", "w_in", "w_out", "b_w_uv", "router_w", "w_gate", "b_gate", "w_up", "b_up", "w_down",
            "b_down"}


def kernel(**inputs):
    import concourse.bacc as bacc
    from concourse.bass_utils import run_bass_kernel_spmd

    nc = bacc.Bacc("TRN2", target_bir_lowering=False, num_devices=1)
    arrays, args = {}, []
    for name in ["consts"] + _ARGS:
        a = constants() if name == "consts" else np.ascontiguousarray(inputs[name])
        if name in _SQUEEZE:
            a = a.reshape(a.shape[1:])
        arrays[name] = a
        args.append(nc.dram_tensor(name, a.shape, mybir.dt.from_np(a.dtype), kind="ExternalInput").ap())
    out = nc.dram_tensor("out", (T, D), F32, kind="ExternalOutput").ap()
    build(nc, *args, out)
    r = run_bass_kernel_spmd(nc, [arrays], core_ids=[0])
    return np.asarray(r.results[0]["out"]).reshape(1, T, D)
```
